# Optimizing a Trainium2 kernel written in Bass

```python
import math
import jax, jax.numpy as jnp
from jax import lax
import numpy as np

D_MODEL = 2048
BATCH = 1
SEQ = 256
DEPTH = 2
DEC_BATCH = 8
DEC_SEQ = 1
PAST_LEN = 2048
PAGE_SIZE = 128

N_BRANCH = 4
BRANCH_WIDTH = D_MODEL // 4
RET_HEADS = 4
RET_DK = BRANCH_WIDTH // RET_HEADS
RET_DV = BRANCH_WIDTH // RET_HEADS
ROPE_BASE = 10000.0
GDN_HEADS = 4
GDN_DK = BRANCH_WIDTH // GDN_HEADS
GDN_DV = BRANCH_WIDTH // GDN_HEADS
GDN_CONV = 4
SCONV_W = 3
POOL_WINDOWS = (2, 4, 8, 16)
POOL_GROUPS = 4
POOL_GDIM = BRANCH_WIDTH // POOL_GROUPS
POOL_HIST = 15
CHUNK = 64
EPS = 1e-6
SPLIT_SIZES = (BRANCH_WIDTH, BRANCH_WIDTH, BRANCH_WIDTH, BRANCH_WIDTH,
               3 * BRANCH_WIDTH, BRANCH_WIDTH, GDN_HEADS, GDN_HEADS,
               BRANCH_WIDTH, BRANCH_WIDTH, BRANCH_WIDTH, BRANCH_WIDTH,
               BRANCH_WIDTH, BRANCH_WIDTH, N_BRANCH * D_MODEL)
IN_COLS = 14 * BRANCH_WIDTH + 2 * GDN_HEADS + N_BRANCH * D_MODEL

kernel_name = "hybrid_retention_gdn_conv_pool_step"

def _rms_norm(x, g):
    xf = x.astype(jnp.float32)
    y = xf * lax.rsqrt(jnp.mean(xf * xf, axis=-1, keepdims=True) + EPS)
    return (y * g.astype(jnp.float32)).astype(x.dtype)

def _head_rms(x):
    xf = x.astype(jnp.float32)
    return (xf * lax.rsqrt(jnp.mean(xf * xf, axis=-1, keepdims=True) + EPS)).astype(x.dtype)

def _l2norm(x):
    xf = x.astype(jnp.float32)
    return (xf * lax.rsqrt(jnp.sum(xf * xf, axis=-1, keepdims=True) + EPS)).astype(x.dtype)

def _rope(x, pos):
    half = x.shape[-1] // 2
    inv = ROPE_BASE ** (-jnp.arange(half, dtype=jnp.float32) / half)
    ang = pos.astype(jnp.float32)[:, None] * inv[None, :]
    cos = jnp.cos(ang)[None, :, None, :]
    sin = jnp.sin(ang)[None, :, None, :]
    xf = x.astype(jnp.float32)
    x1, x2 = xf[..., :half], xf[..., half:]
    return jnp.concatenate([x1 * cos - x2 * sin, x1 * sin + x2 * cos], axis=-1).astype(x.dtype)

def _causal_dwconv(u, hist, w):
    K = w.shape[0]
    T = u.shape[1]
    ext = jnp.concatenate([hist.astype(u.dtype), u], axis=1)
    out = ext[:, 0:T] * w[0]
    for k in range(1, K):
        out = out + ext[:, k:k + T] * w[k]
    return out, ext[:, ext.shape[1] - (K - 1):]

def _to_chunks(a, C, n):
    pad = n * C - a.shape[2]
    a = jnp.pad(a, [(0, 0), (0, 0), (0, pad)] + [(0, 0)] * (a.ndim - 3))
    return a.reshape(a.shape[:2] + (n, C) + a.shape[3:])

def _retention(q, k, v, g, s0):
    f32 = jnp.float32
    T = q.shape[2]
    C = min(CHUNK, T)
    n = -(-T // C)
    qc, kc, vc = (_to_chunks(a.astype(f32), C, n) for a in (q, k, v))
    b = jnp.cumsum(_to_chunks(g.astype(f32), C, n), axis=-1)
    causal = jnp.tril(jnp.ones((C, C), dtype=bool))
    dmask = jnp.exp(jnp.where(causal, b[..., :, None] - b[..., None, :], -jnp.inf))
    scores = jnp.einsum('bhnid,bhnjd->bhnij', qc, kc) * dmask
    o_intra = jnp.einsum('bhnij,bhnje->bhnie', scores, vc)
    b_last = b[..., -1]
    kv = jnp.einsum('bhnj,bhnjd,bhnje->bhnde', jnp.exp(b_last[..., None] - b), kc, vc)

    def step(s, inp):
        dec, kv_n = inp
        return s * dec[..., None, None] + kv_n, s

    s_fin, s_prev = lax.scan(step, s0.astype(f32),
                             (jnp.moveaxis(jnp.exp(b_last), 2, 0), jnp.moveaxis(kv, 2, 0)))
    s_prev = jnp.moveaxis(s_prev, 0, 2)
    o_inter = jnp.einsum('bhnid,bhnde->bhnie', qc * jnp.exp(b)[..., None], s_prev)
    o = (o_intra + o_inter).reshape(qc.shape[:2] + (n * C, vc.shape[-1]))[:, :, :T]
    return o, s_fin

def _gated_delta(q, k, v, g, beta, s0):
    f32 = jnp.float32
    T = q.shape[2]
    dv = v.shape[-1]
    C = min(CHUNK, T)
    n = -(-T // C)
    qc, kc, vc = (_to_chunks(a.astype(f32), C, n) for a in (q, k, v))
    bc = _to_chunks(beta.astype(f32), C, n)
    b = jnp.cumsum(_to_chunks(g.astype(f32), C, n), axis=-1)
    causal = jnp.tril(jnp.ones((C, C), dtype=bool))
    strict = jnp.tril(jnp.ones((C, C), dtype=bool), k=-1)
    decay = jnp.exp(jnp.where(causal, b[..., :, None] - b[..., None, :], -jnp.inf))
    kb = kc * bc[..., None]
    L = jnp.where(strict, jnp.einsum('bhnid,bhnjd->bhnij', kb, kc) * decay, 0.0)
    A = L + jnp.eye(C, dtype=f32)
    rhs = jnp.concatenate([vc * bc[..., None], kb * jnp.exp(b)[..., None]], axis=-1)
    sol = lax.linalg.triangular_solve(A, rhs, left_side=True, lower=True, unit_diagonal=True)
    u, w = sol[..., :dv], sol[..., dv:]
    attn = jnp.einsum('bhnid,bhnjd->bhnij', qc, kc) * decay
    q_dec = qc * jnp.exp(b)[..., None]
    b_last = b[..., -1]
    k_dec = kc * jnp.exp(b_last[..., None] - b)[..., None]

    def step(s, inp):
        u_n, w_n, attn_n, qd_n, kd_n, dl_n = inp
        v_new = u_n - jnp.einsum('bhcd,bhde->bhce', w_n, s)
        o = jnp.einsum('bhcd,bhde->bhce', qd_n, s) + jnp.einsum('bhij,bhje->bhie', attn_n, v_new)
        s = s * dl_n[..., None, None] + jnp.einsum('bhcd,bhce->bhde', kd_n, v_new)
        return s, o

    xs = tuple(jnp.moveaxis(a, 2, 0) for a in (u, w, attn, q_dec, k_dec, jnp.exp(b_last)))
    s_fin, o = lax.scan(step, s0.astype(f32), xs)
    o = jnp.moveaxis(o, 0, 2).reshape(qc.shape[:2] + (n * C, dv))[:, :, :T]
    return o, s_fin

def _layer(x, pos, s_ret, s_gdn, h_gdn, h_sc, h_pool,
           norm_g, w_in, gdn_conv_w, gdn_a_log, gdn_dt_bias, gdn_norm_g,
           sconv_w, pool_w, pool_scale, w_branch, w_out):
    Bn, T, _ = x.shape
    BW = BRANCH_WIDTH
    silu = jax.nn.silu
    h = _rms_norm(x, norm_g)
    z = h @ w_in
    idx, acc = [], 0
    for s in SPLIT_SIZES[:-1]:
        acc += s
        idx.append(acc)
    (ret_q, ret_k, ret_v, ret_gate, gdn_qkv, gdn_gate, gdn_a, gdn_b,
     sc_b, sc_c, sc_h, sc_gate, pool_u, pool_gate, merge_logits) = jnp.split(z, idx, axis=-1)

    q = _rope(ret_q.reshape(Bn, T, RET_HEADS, RET_DK), pos)
    k = _rope(ret_k.reshape(Bn, T, RET_HEADS, RET_DK), pos) * (RET_DK ** -0.5)
    v = ret_v.reshape(Bn, T, RET_HEADS, RET_DV)
    log_gamma = jnp.log(1.0 - 2.0 ** (-5.0 - jnp.arange(RET_HEADS, dtype=jnp.float32)))
    g_ret = jnp.broadcast_to(log_gamma[None, :, None], (Bn, RET_HEADS, T))
    o, s_ret_new = _retention(q.transpose(0, 2, 1, 3), k.transpose(0, 2, 1, 3),
                              v.transpose(0, 2, 1, 3), g_ret, s_ret)
    o = _head_rms(o.transpose(0, 2, 1, 3)).astype(x.dtype)
    y_ret = o.reshape(Bn, T, BW) * silu(ret_gate)

    qkv, h_gdn_new = _causal_dwconv(gdn_qkv, h_gdn, gdn_conv_w)
    qkv = silu(qkv)
    gq, gk, gv = jnp.split(qkv, 3, axis=-1)
    gq = _l2norm(gq.reshape(Bn, T, GDN_HEADS, GDN_DK)) * (GDN_DK ** -0.5)
    gk = _l2norm(gk.reshape(Bn, T, GDN_HEADS, GDN_DK))
    gv = gv.reshape(Bn, T, GDN_HEADS, GDN_DV)
    beta = jax.nn.sigmoid(gdn_b.astype(jnp.float32))
    g_gdn = -jnp.exp(gdn_a_log.astype(jnp.float32)) * jax.nn.softplus(
        gdn_a.astype(jnp.float32) + gdn_dt_bias.astype(jnp.float32))
    o, s_gdn_new = _gated_delta(gq.transpose(0, 2, 1, 3), gk.transpose(0, 2, 1, 3),
                                gv.transpose(0, 2, 1, 3), g_gdn.transpose(0, 2, 1),
                                beta.transpose(0, 2, 1), s_gdn)
    o = _rms_norm(o.transpose(0, 2, 1, 3).astype(x.dtype), gdn_norm_g)
    y_gdn = o.reshape(Bn, T, BW) * silu(gdn_gate)

    conv, h_sc_new = _causal_dwconv(sc_c * sc_h, h_sc, sconv_w)
    y_sc = sc_b * conv * silu(sc_gate)

    ext = jnp.concatenate([h_pool.astype(pool_u.dtype), pool_u], axis=1)
    cs = jnp.pad(jnp.cumsum(ext.astype(jnp.float32), axis=1), ((0, 0), (1, 0), (0, 0)))
    hi = cs[:, POOL_HIST + 1:]
    means = []
    for gi, wnd in enumerate(POOL_WINDOWS):
        c0, c1 = gi * POOL_GDIM, (gi + 1) * POOL_GDIM
        lo = cs[:, POOL_HIST + 1 - wnd:POOL_HIST + 1 - wnd + T, c0:c1]
        cnt = jnp.minimum(pos + 1, wnd).astype(jnp.float32)[None, :, None]
        means.append((hi[..., c0:c1] - lo) / cnt)
    pooled = jnp.concatenate(means, axis=-1).astype(pool_u.dtype) - pool_u
    mixed = jnp.einsum('btgc,gce->btge', pooled.reshape(Bn, T, POOL_GROUPS, POOL_GDIM), pool_w)
    y_pool = mixed.reshape(Bn, T, BW) * pool_scale * silu(pool_gate)
    h_pool_new = ext[:, ext.shape[1] - POOL_HIST:]

    ys = jnp.stack([y_ret, y_gdn, y_sc, y_pool], axis=2)
    proj = jnp.einsum('btnc,ncd->btnd', ys, w_branch)
    gates = jax.nn.sigmoid(merge_logits.reshape(Bn, T, N_BRANCH, D_MODEL))
    merged = jnp.sum(gates * proj, axis=2)
    out = x + merged @ w_out
    return out, (s_ret_new.astype(s_ret.dtype), s_gdn_new.astype(s_gdn.dtype),
                 h_gdn_new, h_sc_new, h_pool_new)

def setup_inputs(seed: int = 0) -> dict:
    key = jax.random.key(seed)
    ks = jax.random.split(key, 20)
    f32 = jnp.float32
    BW = BRANCH_WIDTH

    def nrm(k, shape, s):
        return jax.random.normal(k, shape, f32) * s

    dt = jnp.exp(jax.random.uniform(ks[11], (DEPTH, GDN_HEADS), f32, math.log(1e-3), math.log(1e-1)))
    return {
        "x_prompt": nrm(ks[0], (BATCH, SEQ, D_MODEL), 1.0),
        "x_sample": nrm(ks[1], (DEC_BATCH, DEC_SEQ, D_MODEL), 1.0),
        "state_ret": nrm(ks[2], (DEPTH, DEC_BATCH, RET_HEADS, RET_DK, RET_DV), 0.5),
        "state_gdn": nrm(ks[3], (DEPTH, DEC_BATCH, GDN_HEADS, GDN_DK, GDN_DV), 0.1),
        "state_gdn_conv": nrm(ks[4], (DEPTH, DEC_BATCH, GDN_CONV - 1, 3 * BW), 1.0),
        "state_sconv": nrm(ks[5], (DEPTH, DEC_BATCH, SCONV_W - 1, BW), 1.0),
        "state_pool": nrm(ks[6], (DEPTH, DEC_BATCH, POOL_HIST, BW), 1.0),
        "norm_g": 1.0 + nrm(ks[7], (DEPTH, D_MODEL), 0.02),
        "w_in": nrm(ks[8], (DEPTH, D_MODEL, IN_COLS), D_MODEL ** -0.5),
        "gdn_conv_w": nrm(ks[9], (DEPTH, GDN_CONV, 3 * BW), GDN_CONV ** -0.5),
        "gdn_a_log": jnp.log(jax.random.uniform(ks[10], (DEPTH, GDN_HEADS), f32, 1.0, 16.0)),
        "gdn_dt_bias": dt + jnp.log(-jnp.expm1(-dt)),
        "gdn_norm_g": 1.0 + nrm(ks[12], (DEPTH, GDN_DV), 0.02),
        "sconv_w": nrm(ks[13], (DEPTH, SCONV_W, BW), SCONV_W ** -0.5),
        "pool_w": nrm(ks[14], (DEPTH, POOL_GROUPS, POOL_GDIM, POOL_GDIM), POOL_GDIM ** -0.5),
        "pool_scale": 1.0 + nrm(ks[15], (DEPTH, BW), 0.1),
        "w_branch": nrm(ks[16], (DEPTH, N_BRANCH, BW, D_MODEL), BW ** -0.5),
        "w_out": nrm(ks[17], (DEPTH, D_MODEL, D_MODEL), D_MODEL ** -0.5),
        "final_norm_g": 1.0 + nrm(ks[18], (D_MODEL,), 0.02),
    }

def reference(x_prompt, x_sample, state_ret, state_gdn, state_gdn_conv, state_sconv, state_pool,
              norm_g, w_in, gdn_conv_w, gdn_a_log, gdn_dt_bias, gdn_norm_g,
              sconv_w, pool_w, pool_scale, w_branch, w_out, final_norm_g):
    BW = BRANCH_WIDTH
    Bp, Tp, _ = x_prompt.shape
    Ts = x_sample.shape[1]
    pos_p = jnp.arange(Tp, dtype=jnp.int32)
    pos_s = PAST_LEN + jnp.arange(Ts, dtype=jnp.int32)
    z_ret = jnp.zeros((Bp, RET_HEADS, RET_DK, RET_DV), state_ret.dtype)
    z_gdn = jnp.zeros((Bp, GDN_HEADS, GDN_DK, GDN_DV), state_gdn.dtype)
    z_gconv = jnp.zeros((Bp, GDN_CONV - 1, 3 * BW), x_prompt.dtype)
    z_sconv = jnp.zeros((Bp, SCONV_W - 1, BW), x_prompt.dtype)
    z_pool = jnp.zeros((Bp, POOL_HIST, BW), x_prompt.dtype)

    hp, hs = x_prompt, x_sample
    new_p = [[], [], [], [], []]
    new_s = [[], [], [], [], []]
    for l in range(DEPTH):
        wts = (norm_g[l], w_in[l], gdn_conv_w[l], gdn_a_log[l], gdn_dt_bias[l], gdn_norm_g[l],
               sconv_w[l], pool_w[l], pool_scale[l], w_branch[l], w_out[l])
        hp, st_p = _layer(hp, pos_p, z_ret, z_gdn, z_gconv, z_sconv, z_pool, *wts)
        hs, st_s = _layer(hs, pos_s, state_ret[l], state_gdn[l], state_gdn_conv[l],
                          state_sconv[l], state_pool[l], *wts)
        for i in range(5):
            new_p[i].append(st_p[i])
            new_s[i].append(st_s[i])
    p_ret, p_gdn, p_gconv, p_sconv, p_pool = (jnp.stack(a, axis=0) for a in new_p)
    s_ret, s_gdn, s_gconv, s_sconv, s_pool = (jnp.stack(a, axis=0) for a in new_s)
    y_prompt = _rms_norm(hp, final_norm_g)
    y_sample = _rms_norm(hs, final_norm_g)
    return (y_prompt, y_sample, p_ret, p_gdn, p_gconv, p_sconv, p_pool,
            s_ret, s_gdn, s_gconv, s_sconv, s_pool)


_drawn_inputs = setup_inputs


def setup_inputs(seed=0):
    import zlib

    import numpy as np

    out = dict(_drawn_inputs(seed))
    spreads = {}
    factors = {'gdn_norm_g': 7.257, 'final_norm_g': 7.993, 'pool_scale': 3.209}
    for name, (base, spread) in spreads.items():
        noise = np.random.default_rng([zlib.crc32(name.encode()), seed]).standard_normal(out[name].shape)
        drawn = base * np.exp(spread * noise) if base else spread * noise
        out[name] = __import__('jax').numpy.asarray(drawn.astype(out[name].dtype))
    for name, factor in factors.items():
        out[name] = (out[name] * factor).astype(out[name].dtype)
    return out
```

```python
from contextlib import ExitStack

import numpy as np

import concourse.bass as bass
from concourse import mybir

F32 = mybir.dt.float32
F32R = mybir.dt.float32r
ALU = mybir.AluOpType
ACT = mybir.ActivationFunctionType

P = 128
DEPTH = 2
D_MODEL = 2048
KT = D_MODEL // P
BW = D_MODEL // 4
BT = BW // P
T = 256
NS = 8
N = T + NS
CH = T // P
PAST = 2048
EPS = 1e-6
WINDOWS = (2, 4, 8, 16)
RET, GDN, SCV, POOL = range(4)
GW, SW, PH = 4, 3, 15

GE = GW - 1 + T + NS * GW
SE = SW - 1 + T + NS * SW
PE_ = PH + T + NS * (PH + 1)
GC = GE - (GW - 1)
SC = SE - (SW - 1)

UK = 4
UC = UK * P
RING = 4
UB = KT // UK
TURN = 4 * UB
PTURN = 2 * UB
MB = UB + 1
MTURN = 12 * MB
XTURN = 4 * MB
OFF_G = 0
OFF_R = OFF_G + 4 * TURN
OFF_S = OFF_R + 4 * TURN
OFF_P = OFF_S + 4 * TURN
OFF_M = OFF_P + 4 * PTURN
OFF_X = OFF_M + 4 * MTURN
OFF_O = OFF_X + 4 * XTURN
UNITS = OFF_O + 4 * TURN

BK_G, BK_R, BK_S, BK_P, BK_M, BK_X, BK_O = 0, 4, 8, 12, 14, 38, 46
BANK_USES = 50
BF = 4

PWIN_AT = (0, 2, 5, 9)
PWIN = 14

C_ID, C_ONE, C_TRI, C_NEG, C_STRICT, C_LEV = 0, P, 2 * P, 3 * P, 4 * P, 5 * P
LEVELS = 7
C_DM = C_LEV + LEVELS * P
C_COS = C_DM + BT * T
C_SIN = C_COS + N
C_CORR = C_SIN + N
C_GDEC = C_CORR + BT * 16
C_GAM = C_GDEC + BT * CH
C_END = C_GAM + BT

Q_NG = 0
Q_GCW = Q_NG + (DEPTH + 1) * KT
Q_SCW = Q_GCW + DEPTH * BT * 3 * GW
Q_GNG = Q_SCW + DEPTH * BT * SW
Q_PSC = Q_GNG + DEPTH
Q_DT = Q_PSC + DEPTH * BT
Q_AL = Q_DT + DEPTH * 3 * BT
Q_WAB = Q_AL + DEPTH * 3 * BT
Q_GH = Q_WAB + DEPTH * KT * 2 * BT
Q_SH = Q_GH + DEPTH * BT * 3 * NS * (GW - 1)
Q_PH = Q_SH + DEPTH * BT * NS * (SW - 1)
Q_END = Q_PH

H_G = 0
H_S = H_G + BT * 3 * (NS + 1) * (GW - 1)
H_P = H_S + BT * (NS + 1) * (SW - 1)
H_END = H_P + BT * (NS + 1) * PH

SHARED = 6514


def trunk(nc, w_stream, w_pool, pool_in, x_in, params, consts, ret_in, gdn_in, y_out, hist_out,
          p_ret, p_gdn, s_ret, s_gdn):
    with ExitStack() as ctx:
        def sb(name, shape, dt=F32):
            return ctx.enter_context(nc.sbuf_tensor(name, [P] + shape, dt))

        def psum(name):
            return ctx.enter_context(nc.psum_tensor(name, [P, 512], F32))

        primes = []

        def sem(name, primed=0):
            s = ctx.enter_context(nc.semaphore(name))
            if primed:
                primes.append((s, primed))
            return s

        raw = sb("raw", [RING, UC])
        whi = sb("whi", [RING, UC], F32R)
        wlo = sb("wlo", [RING, UC], F32R)
        x = sb("x", [KT, N])
        act_hi = sb("act_hi", [KT, N], F32R)
        act_lo = sb("act_lo", [KT, N], F32R)
        y_hi = sb("y_hi", [4 * BT, N], F32R)
        y_lo = sb("y_lo", [4 * BT, N], F32R)
        wide = sb("wide", [KT, N])
        rqkv = wide[:, 0:3 * BT, :].rearrange("p a n -> p (a n)")
        gqkv = sb("gqkv", [BT * 3 * N])
        gates = sb("gates", [BT, N])
        con = sb("con", [C_END])
        par = sb("par", [Q_END])
        hist = sb("hist", [H_END])
        phist = sb("phist", [BT * NS * PH])
        pieces = {}

        def shared(kind, shape):
            size = int(np.prod(shape))
            at = pieces.get(kind, 0)
            pieces[kind] = at + size
            assert at + size <= SHARED, (kind, at + size)
            view = share[:, at:at + size]
            if len(shape) == 2:
                view = view.rearrange("p (a b) -> p a b", b=shape[1])
            if len(shape) == 3:
                view = view.rearrange("p (a b c) -> p a b c", b=shape[1], c=shape[2])
            return view

        def early(shape):
            return shared("early", shape)

        def late(shape):
            return shared("late", shape)

        share = sb("share", [SHARED])
        ident, ones = con[:, C_ID:C_ID + P], con[:, C_ONE:C_ONE + P]
        tri, neg = con[:, C_TRI:C_TRI + P], con[:, C_NEG:C_NEG + P]
        strict = con[:, C_STRICT:C_STRICT + P]
        squares = early([2, N])
        ms = early([N])
        rms = early([N])
        ab = sb("ab", [3 * 2 * BT])
        A3 = 3 * BT
        ab_x, ab_abs, ab_e, ab_den, ab_rec, ab_s, ab_s2, ab_q, ab_relu, ab_sp, ab_ea, g_col, beta = \
            [sb(n, [A3]) for n in ("ab_x", "ab_abs", "ab_e", "ab_den", "ab_rec", "ab_s", "ab_s2", "ab_q",
                                   "ab_relu", "ab_sp", "ab_ea", "g_col", "beta")]
        b_col = sb("b_col", [CH * BT])
        gext = early([3, GE])
        gconv = early([3, GC])
        rope_a = early([2, N])
        rope_b = early([2, N])
        sc_c = early([N])
        sext = early([SE])
        sconv = early([SC])
        sgate = early([N])
        sprod = early([N])
        pext = early([PE_])
        psum_a = rope_a.rearrange("p a n -> p (a n)")[:, 0:PE_]
        psum_b = rope_b.rearrange("p a n -> p (a n)")[:, 0:PE_]
        pdiff = early([N])
        pgate = early([N])
        plw = sb("plw", [BT, P])
        y32 = sb("y32", [2, N])
        head = sb("head", [3, N])
        qd = late([P])
        state = sb("state", [NS, P])
        pstate = sb("pstate", [2, P])
        sq2 = late([2, N])
        rn2 = late([2, N])
        rq2 = late([2, N])
        osb = sb("osb", [N])
        osq = sb("osq", [N])
        oms = sb("oms", [N])
        orc = sb("orc", [N])
        scores = early([T + P])
        kd = sb("kd", [CH, P])
        vt = sb("vt", [CH, P])
        g_bc = late([3, P])
        beta_bc = late([P])
        BR = N + NS
        b_row = late([BR])
        eb_row = late([BR])
        hcol = sb("hcol", [8])
        nebc = sb("nebc", [CH])
        bet2 = sb("bet2", [CH])
        dec = late([CH, P])
        decs = late([CH, P])
        E_ = late([CH, P])
        Em = late([2, CH * P])
        attn = late([CH, P])
        TR = late([2, CH, P])
        Xs = late([CH, P])
        vn = late([CH, P])
        rhs1 = late([P])
        mk = sb("mk", [NS])
        kb = sb("kb", [NS])
        msig = late([2, N])
        mprod = late([2, N])

        acc = [psum(f"acc{i}") for i in range(4)]
        side = [psum(f"side{i}") for i in range(4)]

        raw_loaded = [sem(f"raw_loaded{i}") for i in range(RING)]
        hi_ready = sem("hi_ready")
        lo_ready = sem("lo_ready", RING)
        unit_used = sem("unit_used", RING)
        bank_free = [sem(f"bank_free{i}", BF) for i in range(4)]
        x_loaded, con_loaded, par_loaded = sem("x_loaded"), sem("con_loaded"), sem("par_loaded")
        plw_loaded, ph_loaded, state_loaded = sem("plw_loaded"), sem("ph_loaded"), sem("state_loaded")
        out_written, hist_written = sem("out_written"), sem("hist_written")
        state_written, pstate_written, pstate_free = sem("state_written"), sem("pstate_written"), sem("pstate_free", 1)
        zeros_set, passed = sem("zeros_set"), sem("passed")
        sq_ready, norm_mm, ms_ready, rms_ready, rstd_ready = [sem(n) for n in
            ("sq_ready", "norm_mm", "ms_ready", "rms_ready", "rstd_ready")]
        h_ready, act_hi_ready, act_lo_ready = sem("h_ready"), sem("act_hi_ready"), sem("act_lo_ready")
        ab_mm, ab_evac, ab_step, ab_act, bcol_mm, bcol_ready = [sem(n) for n in
            ("ab_mm", "ab_evac", "ab_step", "ab_act", "bcol_mm", "bcol_ready")]
        ghist_in, gconv_step, gqkv_ready, ghist_out = [sem(n, p) for n, p in
            (("ghist_in", 0), ("gconv_step", 3 * GW), ("gqkv_ready", 0), ("ghist_out", 3))]
        rope_step = sem("rope_step")
        head_copied, rsc_mm, rtr_mm, scores_ready, kdvt_ready, ro_mm, rst_mm, rst_ready, rvb_mm = [sem(n) for n in
            ("head_copied", "rsc_mm", "rtr_mm", "scores_ready", "kdvt_ready", "ro_mm", "rst_mm", "rst_ready", "rvb_mm")]
        rdecayed, rstate_new, ros_mm, ro_copied, rss_mm, ro_step, rors_ready = [sem(n) for n in
            ("rdecayed", "rstate_new", "ros_mm", "ro_copied", "rss_mm", "ro_step", "rors_ready")]
        sconv_step, shist_in, shist_out, sy_ready, syhi = [sem(n, p) for n, p in
            (("sconv_step", SW), ("shist_in", 0), ("shist_out", 1), ("sy_ready", 0), ("syhi", 0))]
        phist_in, psum_step, phist_out, pmix_mm, py_ready, pyhi, pwin = [sem(n, p) for n, p in
            (("phist_in", 0), ("psum_step", 1), ("phist_out", 1), ("pmix_mm", BT), ("py_ready", 1), ("pyhi", 0),
             ("pwin", 0))]
        y_ready = [sem(f"y_ready{n}") for n in range(4)]
        ryhi, gyhi = sem("ryhi"), sem("gyhi")
        gsq_ready, gbc_ready, gn_mm, grow_mm, gvt_mm, grow_ready, grn_step, grn_act, gqk_ready, gcol_step, gcol_act = \
            [sem(n) for n in ("gsq_ready", "gbc_ready", "gn_mm", "grow_mm", "gvt_mm", "grow_ready", "grn_step",
                              "grn_act", "gqk_ready", "gcol_step", "gcol_act")]
        gkq_mm, gkt_mm, gE_ready, gattn_ready, gkd_ready, gem_ready, gR_ready, gT_mm, gT_ready, gX_mm, gX_ready, \
            gD_mm, gTR_ready = [sem(n) for n in ("gkq_mm", "gkt_mm", "gE_ready", "gattn_ready", "gkd_ready",
            "gem_ready", "gR_ready", "gT_mm", "gT_ready", "gX_mm", "gX_ready", "gD_mm", "gTR_ready")]
        gsol_mm, gvn_ready, gst_mm, gst_ready, gks_mm, grhs_ready, gqd_ready, go_mm, go_copied, gss_mm, go_step, \
            gors_ready = [sem(n) for n in ("gsol_mm", "gvn_ready", "gst_mm", "gst_ready", "gks_mm", "grhs_ready",
            "gqd_ready", "go_mm", "go_copied", "gss_mm", "go_step", "gors_ready")]
        gmk_ready, gdl_mm, gdecayed, gstate_new, gos_mm, gos_copied = [sem(n) for n in
            ("gmk_ready", "gdl_mm", "gdecayed", "gstate_new", "gos_mm", "gos_copied")]
        merged_ready = sem("merged_ready")
        mhi_ready, mlo_ready = sem("mhi_ready"), sem("mlo_ready")

        def col(table, at):
            return table[:, bass.ds(at, 1)]

        def samples(tile, lead, taps, shift=0, width=1):
            body = tile[:, lead:lead + NS * taps].rearrange("p (b k) -> p b k", k=taps)
            return body[:, :, shift] if width == 1 else body[:, :, shift:shift + width]

        def settled(eng):
            eng.sem_inc(passed, 1)

        block = ctx.enter_context(nc.Block())

        @block.sync
        def _(sp):
            for s, n in primes:
                sp.sem_inc(s, n)
            sp.dma_start(x[:, :, :], x_in).then_inc(x_loaded, 16)
            sp.dma_start(con[:, :], consts).then_inc(con_loaded, 16)
            sp.dma_start(par[:, :], params).then_inc(par_loaded, 16)
            with sp.Fori(0, DEPTH) as l:
                with sp.Fori(0, UNITS // RING) as r:
                    u = sp.snap(l * UNITS + r * RING)
                    for s in range(RING):
                        sp.wait_ge(lo_ready, u + s + 1)
                        sp.dma_start(raw[:, s, :], w_stream[l, r * RING + s]).then_inc(raw_loaded[s], 16)

        @block.gpsimd
        def _(pool):
            gp = nc.gpsimd
            gp.memset(ab[:, :], 0.0).then_inc(zeros_set, 1)
            pool.wait_ge(par_loaded, 16)
            pool.wait_ge(con_loaded, 16)
            with pool.Fori(0, DEPTH) as l:
                gp.memset(gext[:, :, 0:GW - 1], 0.0)
                gp.memset(sext[:, 0:SW - 1], 0.0)
                gp.memset(pext[:, 0:PH], 0.0).then_inc(zeros_set, 1)
                pool.wait_ge(pmix_mm, l * BT + BT)
                settled(pool)
                pool.dma_start(plw[:, :, :], w_pool[l]).then_inc(plw_loaded, 16)
                pool.dma_start(phist[:, :], pool_in[l]).then_inc(ph_loaded, 16)
                with pool.Fori(0, BT) as h:
                    it = pool.snap(l * BT + h)
                    pool.wait_ge(ghist_out, it * 3 + 3)
                    settled(pool)
                    for j in range(3):
                        pool.wait_ge(gconv_step, it * (3 * GW) + GW * (j + 1))
                        settled(pool)
                        src = par[:, bass.ds(Q_GH + (it * 3 + j) * NS * (GW - 1), NS * (GW - 1))]
                        gp.tensor_copy(samples(gext[:, j, :], GW - 1 + T, GW, 0, GW - 1),
                                       src.rearrange("p (b k) -> p b k", k=GW - 1)).then_inc(ghist_in, 1)
                    for j in range(3):
                        pool.wait_ge(bank_free[j], l * BANK_USES + BK_G + h + 1 + BF)
                        pool.wait_ge(ghist_in, it * 3 + j + 1)
                        settled(pool)
                        at = H_G + (h * 3 + j) * (NS + 1) * (GW - 1)
                        gp.tensor_copy(hist[:, bass.ds(at, GW - 1)], gext[:, j, T:T + GW - 1])
                        gp.tensor_copy(hist[:, bass.ds(at + GW - 1, NS * (GW - 1))].rearrange("p (b k) -> p b k", k=GW - 1),
                                       samples(gext[:, j, :], GW - 1 + T, GW, 1, GW - 1)).then_inc(ghist_out, 1)
                with pool.Fori(0, BT) as h:
                    it = pool.snap(l * BT + h)
                    pool.dma_start(state[:, :, :], ret_in[l, :, h].rearrange("b d e -> d b e")).then_inc(state_loaded, 16)
                    pool.wait_ge(sconv_step, it * SW + SW)
                    pool.wait_ge(shist_out, it + 1)
                    settled(pool)
                    src = par[:, bass.ds(Q_SH + it * NS * (SW - 1), NS * (SW - 1))]
                    gp.tensor_copy(samples(sext[:, :], SW - 1 + T, SW, 0, SW - 1),
                                   src.rearrange("p (b k) -> p b k", k=SW - 1)).then_inc(shist_in, 1)
                    pool.wait_ge(bank_free[1], l * BANK_USES + BK_S + h + 1 + BF)
                    pool.wait_ge(shist_in, it + 1)
                    settled(pool)
                    at = H_S + h * (NS + 1) * (SW - 1)
                    gp.tensor_copy(hist[:, bass.ds(at, SW - 1)], sext[:, T:T + SW - 1])
                    gp.tensor_copy(hist[:, bass.ds(at + SW - 1, NS * (SW - 1))].rearrange("p (b k) -> p b k", k=SW - 1),
                                   samples(sext[:, :], SW - 1 + T, SW, 1, SW - 1)).then_inc(shist_out, 1)
                    pool.wait_ge(rst_ready, it + 1)
                    settled(pool)
                    pool.dma_start(p_ret[l, 0, h], pstate[:, 0, :]).then_inc(pstate_written, 16)
                    pool.wait_ge(pstate_written, (it + l * BT) * 16 + 16)
                    pool.sem_inc(pstate_free, 1)
                    pool.wait_ge(rstate_new, it * NS + NS)
                    settled(pool)
                    pool.dma_start(s_ret[l, :, h].rearrange("b d e -> d b e"), state[:, :, :]).then_inc(state_written, 16)
                    pool.wait_ge(ros_mm, it + 1)
                    pool.wait_ge(state_written, (it + l * BT) * 16 + 16)
                    settled(pool)
                pool.wait_ge(ph_loaded, l * 16 + 16)
                settled(pool)
                for g in range(BT):
                    it = pool.snap(l * BT + g)
                    pool.wait_ge(psum_step, it + 1)
                    pool.wait_ge(phist_out, it + 1)
                    settled(pool)
                    src = phist[:, g * NS * PH:(g + 1) * NS * PH]
                    gp.tensor_copy(samples(pext[:, :], PH + T, PH + 1, 0, PH),
                                   src.rearrange("p (b k) -> p b k", k=PH)).then_inc(phist_in, 1)
                    pool.wait_ge(bank_free[2 * (g % 2)], l * BANK_USES + BK_P + g // 2 + 1 + BF)
                    pool.wait_ge(phist_in, it + 1)
                    settled(pool)
                    at = H_P + g * (NS + 1) * PH
                    gp.tensor_copy(hist[:, at:at + PH], pext[:, T:T + PH])
                    gp.tensor_copy(hist[:, at + PH:at + PH + NS * PH].rearrange("p (b k) -> p b k", k=PH),
                                   samples(pext[:, :], PH + T, PH + 1, 1, PH)).then_inc(phist_out, 1)
                pool.wait_ge(phist_out, l * BT + BT + 1)
                settled(pool)
                pool.dma_start(hist_out[l], hist[:, :]).then_inc(hist_written, 16)
                pool.wait_ge(hist_written, l * 16 + 16)
                settled(pool)
                with pool.Fori(0, BT) as h:
                    it = pool.snap(l * BT + h)
                    pool.dma_start(state[:, :, :], gdn_in[l, :, h].rearrange("b d e -> d b e")).then_inc(state_loaded, 16)
                    pool.wait_ge(gE_ready, it + 1)
                    settled(pool)
                    for v in range(1, LEVELS):
                        if v > 2:
                            pool.wait_ge(gX_mm, it * 6 + v - 2)
                            settled(pool)
                        for c in range(CH):
                            last = gp.tensor_tensor(Em[:, v % 2, c * P:(c + 1) * P], E_[:, c, :],
                                                    con[:, C_LEV + v * P:C_LEV + (v + 1) * P], ALU.mult)
                        last.then_inc(gem_ready, 1)
                    pool.wait_ge(gstate_new, it * NS + NS)
                    settled(pool)
                    pool.dma_start(s_gdn[l, :, h].rearrange("b d e -> d b e"), state[:, :, :]).then_inc(state_written, 16)
                    pool.wait_ge(gos_mm, it + 1)
                    pool.wait_ge(state_written, (it + l * BT) * 16 + 16 * BT + 16)
                    pool.wait_ge(gst_ready, it * 2 + 2)
                    settled(pool)
                    pool.dma_start(p_gdn[l, 0, h], pstate[:, 1, :]).then_inc(pstate_written, 16)
                    pool.wait_ge(pstate_written, (it + l * BT) * 16 + 16 * BT + 16)
                    pool.sem_inc(pstate_free, 1)
            for q in range(4):
                pool.wait_ge(h_ready, DEPTH * 4 + q + 1)
                settled(pool)
                pool.dma_start(y_out[:, q * 4 * N:(q + 1) * 4 * N],
                               wide[:, 4 * q:4 * q + 4, :].rearrange("p a n -> p (a n)")).then_inc(out_written, 16)
            pool.wait_ge(out_written, 4 * 16)

        @block.scalar
        def _(act):
            sc = nc.scalar

            def splitter(l, off, i, per):
                ub = act.snap(l * UNITS + off + i * per)
                rb = act.snap((l * (UNITS // RING) + off // RING + i * (per // RING)) * 16)

                def split(a, b):
                    for j in range(a, b):
                        s = j % RING
                        act.wait_ge(raw_loaded[s], rb + 16 * (j // RING + 1))
                        act.wait_ge(unit_used, ub + j + 1)
                        sc.activation(whi[:, s, :], raw[:, s, :], ACT.Copy).then_inc(hi_ready, 1)
                return ub, split

            def norm_sums(n):
                for k in range(KT):
                    act.wait_ge(bank_free[k % 4], n * BANK_USES + k // 4 + 1)
                    if k >= 2:
                        act.wait_ge(norm_mm, n * KT + k - 1)
                    sc.activation(squares[:, k % 2, :], x[:, k, :], ACT.Square).then_inc(sq_ready, 1)
                act.wait_ge(rms_ready, n + 1)
                sc.activation(ms[:, :], rms[:, :], ACT.Sqrt).then_inc(rstd_ready, 1)

            act.wait_ge(x_loaded, 16)
            act.wait_ge(par_loaded, 16)
            act.wait_ge(con_loaded, 16)
            with act.Fori(0, DEPTH) as l:
                ub, split = splitter(l, 0, 0, 0)
                split(0, 3)
                norm_sums(l)
                for q in range(4):
                    act.wait_ge(h_ready, l * 4 + q + 1)
                    sc.activation(act_hi[:, 4 * q:4 * q + 4, :], wide[:, 4 * q:4 * q + 4, :], ACT.Copy).then_inc(act_hi_ready, 1)

                act.wait_ge(ab_step, l * 15 + 1)
                sc.activation(ab_abs[:, :], ab_x[:, :], ACT.Abs).then_inc(ab_act, 1)
                act.wait_ge(ab_act, l * 4 + 1)
                sc.activation(ab_e[:, :], ab_abs[:, :], ACT.Exp, scale=-1.0).then_inc(ab_act, 1)
                sc.activation(ab_ea[:, :], par[:, bass.ds(Q_AL + l * A3, A3)], ACT.Exp).then_inc(ab_act, 1)
                sc.activation(beta[:, :].rearrange("p (c h) -> p c h", h=BT),
                              ab[:, :].rearrange("p (c t h) -> p c t h", t=2, h=BT)[:, :, 1, :],
                              ACT.Sigmoid).then_inc(ab_act, 1)

                with act.Fori(0, BT) as h:
                    it = act.snap(l * BT + h)
                    ub, split = splitter(l, OFF_G, h, TURN)

                    def silu_out(j):
                        act.wait_ge(gconv_step, it * (3 * GW) + 3 * GW + GW * (j + 1))
                        at = (h * 3 + j) * N
                        sc.activation(gqkv[:, bass.ds(at, T)], gconv[:, j, 0:T], ACT.Silu)
                        sc.activation(gqkv[:, bass.ds(at + T, NS)], gconv[:, j, GW - 1 + T:GC:GW], ACT.Silu).then_inc(gqkv_ready, 1)

                    for j in range(3):
                        split(4 * j + 3, 4 * j + 7)
                        act.wait_ge(unit_used, ub + RING + UB * (j + 1))
                        act.wait_ge(ghist_out, it * 3 + j + 1)
                        if j:
                            silu_out(j - 1)
                        sc.activation(gext[:, j, GW - 1:GW - 1 + T], acc[j][:, 0:T], ACT.Copy)
                        sc.activation(samples(gext[:, j, :], GW - 1 + T, GW, GW - 1), acc[j][:, T:N], ACT.Copy).then_inc(bank_free[j], 1)
                    split(15, 19)
                    silu_out(2)
                    act.wait_ge(unit_used, ub + RING + UB * 4)
                    sc.activation(gates[:, bass.ds(h, 1), :], acc[3][:, 0:N], ACT.Silu).then_inc(bank_free[3], 1)

                with act.Fori(0, BT) as h:
                    ub, split = splitter(l, OFF_R, h, TURN)
                    split(3, 15)
                    act.wait_ge(unit_used, ub + RING + UB * 3)
                    sc.activation(rqkv[:, bass.ds((h * 3 + 2) * N, N)], acc[2][:, 0:N], ACT.Copy).then_inc(bank_free[2], 1)
                    split(15, 19)
                    act.wait_ge(unit_used, ub + RING + UB * 4)
                    sc.activation(wide[:, bass.ds(h + 3 * BT, 1), :], acc[3][:, 0:N], ACT.Silu).then_inc(bank_free[3], 1)

                with act.Fori(0, BT) as h:
                    it = act.snap(l * BT + h)
                    ub, split = splitter(l, OFF_S, h, TURN)
                    act.wait_ge(rope_step, it * 6 + 6)
                    act.wait_ge(bank_free[2], l * BANK_USES + BK_R + BT + BF)
                    sc.activation(head[:, :, :].rearrange("p a n -> p (a n)"), rqkv[:, bass.ds(h * 3 * N, 3 * N)],
                                  ACT.Copy).then_inc(head_copied, 1)
                    split(3, 7)
                    act.wait_ge(rtr_mm, it + 1)
                    for c in range(CH):
                        sc.activation(kd[:, c, :], side[1][:, c * P:(c + 1) * P], ACT.Copy, scale=col(con, C_GDEC + h * CH + c))
                    sc.activation(vt[:, :, :].rearrange("p c d -> p (c d)"), side[1][:, T:2 * T], ACT.Copy).then_inc(kdvt_ready, 1)
                    act.wait_ge(unit_used, ub + RING + UB)
                    sc.activation(sc_c[:, :], acc[0][:, 0:N], ACT.Copy).then_inc(bank_free[0], 1)
                    split(7, 9)
                    act.wait_ge(state_loaded, (it + l * BT) * 16 + 16)
                    sc.activation(state[:, :, :].rearrange("p b e -> p (b e)"), state[:, :, :].rearrange("p b e -> p (b e)"),
                                  ACT.Copy, scale=col(con, C_GAM + h)).then_inc(rdecayed, 1)
                    split(9, 15)
                    act.wait_ge(ros_mm, it + 1)
                    sc.activation(osb[:, :], side[2][:, 0:N], ACT.Copy)
                    sc.activation(osq[:, :], side[2][:, 0:N], ACT.Square).then_inc(ro_copied, 1)
                    split(15, 18)
                    act.wait_ge(ro_step, it * 4 + 2)
                    sc.activation(oms[:, :], orc[:, :], ACT.Sqrt).then_inc(rors_ready, 1)
                    split(18, 19)
                    act.wait_ge(unit_used, ub + RING + UB * 4)
                    sc.activation(sgate[:, :], acc[3][:, 0:N], ACT.Silu).then_inc(bank_free[3], 1)
                    act.wait_ge(ro_step, it * 4 + 4)
                    sc.activation(y_hi[:, bass.ds(RET * BT + h, 1), :], y32[:, 0, :], ACT.Copy).then_inc(ryhi, 1)
                    act.wait_ge(sy_ready, it + 1)
                    sc.activation(y_hi[:, bass.ds(SCV * BT + h, 1), :], y32[:, 1, :], ACT.Copy).then_inc(syhi, 1)

                for g in range(BT):
                    it = l * BT + g
                    ub, split = splitter(l, OFF_P, g, PTURN)
                    b0 = 2 * (g % 2)
                    split(3, 7)
                    act.wait_ge(unit_used, ub + RING + UB)
                    act.wait_ge(phist_out, it + 1)
                    act.wait_ge(psum_step, it + 1)
                    sc.activation(pext[:, PH:PH + T], acc[b0][:, 0:T], ACT.Copy)
                    sc.activation(samples(pext[:, :], PH + T, PH + 1, PH), acc[b0][:, T:N], ACT.Copy).then_inc(bank_free[b0], 1)
                    split(7, 11)
                    act.wait_ge(unit_used, ub + RING + UB * 2)
                    act.wait_ge(py_ready, it + 1)
                    sc.activation(pgate[:, :], acc[b0 + 1][:, 0:N], ACT.Silu).then_inc(bank_free[b0 + 1], 1)
                    act.wait_ge(py_ready, it + 2)
                    sc.activation(y_hi[:, POOL * BT + g, :], y32[:, 1, :], ACT.Copy).then_inc(pyhi, 1)

                act.wait_ge(phist_out, l * BT + BT + 1)
                settled(act)
                with act.Fori(0, BT) as h:
                    it = act.snap(l * BT + h)
                    ub, split = splitter(l, OFF_M, h, MTURN)
                    mb = act.snap(l * 4 * KT + h * 12)
                    fb = act.snap(l * BANK_USES + BK_M + h * 6)

                    def units(a, b):
                        for j in range(a, b):
                            split(j + 3, j + 4)
                            if j % MB == MB - 1:
                                i = j // MB
                                p = i % 2
                                act.wait_ge(unit_used, ub + RING + MB * i + UB)
                                act.wait_ge(bank_free[2 * p + 1], fb + i // 2 + BF)
                                sc.activation(msig[:, p, :], acc[2 * p][:, 0:N], ACT.Sigmoid).then_inc(bank_free[2 * p], 1)

                    act.wait_ge(gqkv_ready, l * 3 * BT + 3 * BT)
                    sc.activation(sq2[:, :, :].rearrange("p a n -> p (a n)"), gqkv[:, bass.ds(h * 3 * N, 2 * N)], ACT.Square).then_inc(gsq_ready, 1)
                    sc.activation(head[:, 2, :], gqkv[:, bass.ds((h * 3 + 2) * N, N)], ACT.Copy).then_inc(gsq_ready, 1)
                    units(0, 3)
                    act.wait_ge(grow_mm, it + 1)
                    sc.activation(b_row[:, :], side[2][:, 0:BR], ACT.Copy).then_inc(grow_ready, 1)
                    sc.activation(eb_row[:, 0:N], side[2][:, 0:N], ACT.Exp).then_inc(grow_ready, 1)
                    act.wait_ge(gvt_mm, it + 1)
                    sc.activation(vt[:, :, :].rearrange("p c d -> p (c d)"), side[3][:, 0:T], ACT.Copy).then_inc(kdvt_ready, 1)
                    act.wait_ge(gcol_step, it * 3 + 2)
                    sc.activation(hcol[:, 2:4], hcol[:, 0:2], ACT.Exp)
                    sc.activation(hcol[:, 6:8], hcol[:, 4:6], ACT.Exp).then_inc(gcol_act, 1)
                    sc.activation(dec[:, :, :].rearrange("p c d -> p (c d)"), dec[:, :, :].rearrange("p c d -> p (c d)"),
                                  ACT.Exp).then_inc(gcol_act, 1)
                    act.wait_ge(grn_step, it * 2 + 2)
                    sc.activation(rn2[:, :, :].rearrange("p a n -> p (a n)"), rq2[:, :, :].rearrange("p a n -> p (a n)"),
                                  ACT.Sqrt).then_inc(grn_act, 1)
                    units(3, 8)
                    act.wait_ge(gkt_mm, it + 1)
                    act.wait_ge(gcol_act, it * 2 + 1)
                    for c in range(CH):
                        last = sc.activation(kd[:, c, :], side[1][:, c * P:(c + 1) * P], ACT.Copy, scale=hcol[:, 6 + c:7 + c])
                    last.then_inc(gkd_ready, 1)
                    units(8, 11)
                    act.wait_ge(gT_mm, it + 1)
                    sc.activation(TR[:, 0, :, :].rearrange("p c d -> p (c d)"), side[0][:, 0:T], ACT.Copy).then_inc(gT_ready, 1)
                    at = 11
                    for v in range(1, LEVELS):
                        act.wait_ge(gX_mm, it * 6 + v)
                        sc.activation(Xs[:, :, :].rearrange("p c d -> p (c d)"), side[0][:, 0:T], ACT.Copy).then_inc(gX_ready, 1)
                        if v in (2, 4):
                            act.wait_ge(grow_ready, it * 2 + 2)
                            act.wait_ge(gdl_mm, it * 2 + v // 2)
                            for b in range(2 * v - 4, 2 * v):
                                last = sc.activation(state[:, b, :], state[:, b, :], ACT.Copy, scale=eb_row[:, T + b:T + b + 1])
                            last.then_inc(gdecayed, 1)
                        if v == 6:
                            act.wait_ge(gos_mm, it + 1)
                            sc.activation(osb[:, T:N], side[3][:, 0:NS], ACT.Copy).then_inc(gos_copied, 1)
                        units(at, at + 5)
                        at += 5
                    act.wait_ge(gsol_mm, it * 2 + 1)
                    sc.activation(vn[:, 0, :], side[2][:, 0:P], ACT.Copy, scale=bet2[:, 0:1]).then_inc(gvn_ready, 1)
                    units(at, 49)
                    act.wait_ge(gsol_mm, it * 2 + 2)
                    sc.activation(vn[:, 1, :], side[2][:, 0:P], ACT.Copy, scale=bet2[:, 1:2]).then_inc(gvn_ready, 1)
                    units(49, 52)
                    act.wait_ge(go_mm, it + 1)
                    sc.activation(osb[:, 0:T], side[0][:, 0:T], ACT.Copy).then_inc(go_copied, 1)
                    act.wait_ge(go_copied, it * 2 + 1)
                    sc.activation(osq[:, :], osb[:, :], ACT.Square).then_inc(go_copied, 1)
                    units(52, 57)
                    act.wait_ge(go_step, it * 4 + 2)
                    sc.activation(oms[:, :], orc[:, :], ACT.Sqrt).then_inc(gors_ready, 1)
                    units(57, 60)
                    act.wait_ge(go_step, it * 4 + 4)
                    sc.activation(y_hi[:, bass.ds(GDN * BT + h, 1), :], y32[:, 0, :], ACT.Copy).then_inc(gyhi, 1)

                with act.Fori(0, BT) as h:
                    ub, split = splitter(l, OFF_X, h, XTURN)
                    fb = act.snap(l * BANK_USES + BK_X + h * 2)
                    for i in range(4):
                        p = i % 2
                        split(MB * i + 3, MB * i + 8)
                        act.wait_ge(unit_used, ub + RING + MB * i + UB)
                        act.wait_ge(bank_free[2 * p + 1], fb + i // 2 + BF)
                        sc.activation(msig[:, p, :], acc[2 * p][:, 0:N], ACT.Sigmoid).then_inc(bank_free[2 * p], 1)

                act.wait_ge(unit_used, l * UNITS + RING + OFF_O)
                for q in range(4):
                    act.wait_ge(merged_ready, l * 3 * KT + 2 * KT + 4 * q + 4)
                    sc.activation(act_hi[:, 4 * q:4 * q + 4, :], wide[:, 4 * q:4 * q + 4, :], ACT.Copy).then_inc(mhi_ready, 1)
                with act.Fori(0, BT - 1) as h:
                    ub, split = splitter(l, OFF_O, h, TURN)
                    split(3, TURN + 3)
                ub, split = splitter(l, OFF_O, BT - 1, TURN)
                split(3, TURN)
            norm_sums(DEPTH)

        @block.vector
        def _(dve):
            ve = nc.vector

            def splitter(l, off, i, per):
                ub = dve.snap(l * UNITS + off + i * per)

                def split(a, b):
                    for j in range(a, b):
                        s = j % RING
                        dve.wait_ge(hi_ready, ub + j + 1)
                        ve.tensor_tensor(wlo[:, s, :], raw[:, s, :], whi[:, s, :].bitcast(F32), ALU.subtract).then_inc(lo_ready, 1)
                return ub, split

            def norm_apply(n, quarter_done):
                dve.wait_ge(norm_mm, n * KT + KT)
                ve.tensor_scalar(ms[:, :], side[0][:, 0:N], 1.0 / D_MODEL, EPS, ALU.mult, ALU.add).then_inc(ms_ready, 1)
                dve.wait_ge(ms_ready, n + 1)
                ve.reciprocal(rms[:, :], ms[:, :]).then_inc(rms_ready, 1)
                dve.wait_ge(rstd_ready, n + 1)
                for q in range(4):
                    for k in range(4 * q, 4 * q + 4):
                        last = ve.scalar_tensor_tensor(out=wide[:, k, :], in0=x[:, k, :], scalar=col(par, Q_NG + n * KT + k),
                                                       in1=ms[:, :], op0=ALU.mult, op1=ALU.mult)
                    last.then_inc(h_ready, 1)
                    quarter_done(q)

            dve.wait_ge(x_loaded, 16)
            dve.wait_ge(par_loaded, 16)
            dve.wait_ge(con_loaded, 16)
            with dve.Fori(0, DEPTH) as l:
                ub, split = splitter(l, 0, 0, 0)
                split(0, 3)

                def lo_of(q):
                    dve.wait_ge(act_hi_ready, l * 4 + q + 1)
                    ve.tensor_tensor(act_lo[:, 4 * q:4 * q + 4, :], wide[:, 4 * q:4 * q + 4, :],
                                     act_hi[:, 4 * q:4 * q + 4, :].bitcast(F32), ALU.subtract).then_inc(act_lo_ready, 1)

                norm_apply(l, lambda q: lo_of(q - 1) if q else None)
                lo_of(3)

                dve.wait_ge(ab_mm, l * 3 + 3)
                dve.wait_ge(zeros_set, 1)
                ve.tensor_copy(ab[:, 0:4 * BT], side[1][:, 0:4 * BT])
                ve.tensor_copy(ab[0:NS, 4 * BT:6 * BT], side[1][0:NS, 4 * BT:6 * BT]).then_inc(ab_evac, 1)
                dve.wait_ge(ab_evac, l + 1)
                nth = [0]

                def link(op):
                    nth[0] += 1
                    op.then_inc(ab_step, 1)
                    dve.wait_ge(ab_step, l * 15 + nth[0])

                link(ve.tensor_tensor(ab_x[:, :].rearrange("p (c h) -> p c h", h=BT),
                                      ab[:, :].rearrange("p (c t h) -> p c t h", t=2, h=BT)[:, :, 0, :],
                                      par[:, bass.ds(Q_DT + l * A3, A3)].rearrange("p (c h) -> p c h", h=BT), ALU.add))
                ve.tensor_scalar(ab_relu[:, :], ab_x[:, :], 0.0, None, ALU.max)
                dve.wait_ge(ab_act, l * 4 + 2)
                link(ve.tensor_scalar(ab_den[:, :], ab_e[:, :], 2.0, None, ALU.add))
                link(ve.reciprocal(ab_rec[:, :], ab_den[:, :]))
                link(ve.tensor_tensor(ab_s[:, :], ab_e[:, :], ab_rec[:, :], ALU.mult))
                link(ve.tensor_tensor(ab_s2[:, :], ab_s[:, :], ab_s[:, :], ALU.mult))
                link(ve.tensor_scalar(ab_q[:, :], ab_s2[:, :], 1.0 / 15, None, ALU.mult))
                for d in (13, 11, 9, 7, 5, 3):
                    link(ve.scalar_tensor_tensor(out=ab_q[:, :], in0=ab_q[:, :], scalar=1.0 / d, in1=ab_s2[:, :],
                                                 op0=ALU.add, op1=ALU.mult))
                link(ve.scalar_tensor_tensor(out=ab_q[:, :], in0=ab_q[:, :], scalar=1.0, in1=ab_s[:, :],
                                             op0=ALU.add, op1=ALU.mult))
                link(ve.scalar_tensor_tensor(out=ab_sp[:, :], in0=ab_q[:, :], scalar=2.0, in1=ab_relu[:, :],
                                             op0=ALU.mult, op1=ALU.add))
                dve.wait_ge(ab_act, l * 4 + 4)
                link(ve.scalar_tensor_tensor(out=g_col[:, :], in0=ab_sp[:, :], scalar=-1.0, in1=ab_ea[:, :],
                                             op0=ALU.mult, op1=ALU.mult))
                assert nth[0] == 15

                dve.wait_ge(zeros_set, l + 2)
                settled(dve)
                with dve.Fori(0, BT) as h:
                    it = dve.snap(l * BT + h)
                    ub, split = splitter(l, OFF_G, h, TURN)
                    split(3, 7)
                    for j in range(3):
                        dve.wait_ge(bank_free[j], l * BANK_USES + BK_G + h + 1 + BF)
                        dve.wait_ge(ghist_in, it * 3 + j + 1)
                        tap = Q_GCW + (it * 3 + j) * GW
                        ve.tensor_scalar(gconv[:, j, :], gext[:, j, 0:GC], col(par, tap), None, ALU.mult).then_inc(gconv_step, 1)
                        for k in range(1, GW):
                            dve.wait_ge(gconv_step, it * (3 * GW) + 3 * GW + GW * j + k)
                            ve.scalar_tensor_tensor(out=gconv[:, j, :], in0=gext[:, j, k:k + GC], scalar=col(par, tap + k),
                                                    in1=gconv[:, j, :], op0=ALU.mult, op1=ALU.add).then_inc(gconv_step, 1)
                            split(7 + 4 * j + k - 1, 7 + 4 * j + k)
                        split(10 + 4 * j, 11 + 4 * j)

                def rotate(out, a, table, scale):
                    return ve.scalar_tensor_tensor(out=out, in0=a, scalar=scale, in1=table, op0=ALU.mult, op1=ALU.mult)

                with dve.Fori(0, BT) as h:
                    it = dve.snap(l * BT + h)
                    ub, split = splitter(l, OFF_R, h, TURN)
                    split(3, 7)
                    for j, scale in enumerate((1.0, float(P) ** -0.5)):
                        dve.wait_ge(unit_used, ub + RING + UB * (j + 1))
                        rotate(rope_a[:, j, :], acc[j][:, 0:N], con[:, C_COS:C_COS + N], scale).then_inc(rope_step, 1)
                        rotate(rope_b[0:64, j, :], acc[j][64:P, 0:N], con[64:P, C_SIN:C_SIN + N], scale).then_inc(rope_step, 1)
                        rotate(rope_b[64:P, j, :], acc[j][0:64, 0:N], con[0:64, C_SIN:C_SIN + N], scale).then_inc(bank_free[j], 1)
                        dve.wait_ge(bank_free[j], l * BANK_USES + BK_R + h + 1 + BF)
                        ve.tensor_tensor(rqkv[:, bass.ds((h * 3 + j) * N, N)], rope_a[:, j, :], rope_b[:, j, :], ALU.add).then_inc(rope_step, 1)
                        split(7 + 4 * j, 11 + 4 * j)
                    split(15, 19)

                dve.wait_ge(bcol_mm, l + 1)
                ve.tensor_copy(b_col[:, :], side[1][:, 0:CH * BT]).then_inc(bcol_ready, 1)

                with dve.Fori(0, BT) as h:
                    it = dve.snap(l * BT + h)
                    ub, split = splitter(l, OFF_S, h, TURN)
                    split(3, 6)
                    dve.wait_ge(rsc_mm, it + 1)
                    ve.tensor_tensor(scores[:, 0:T], side[0][:, 0:T], con[:, bass.ds(C_DM + h * T, T)], ALU.mult)
                    ve.tensor_tensor(scores[:, T:T + P], side[0][:, T:T + P], con[:, bass.ds(C_DM + h * T, P)], ALU.mult).then_inc(scores_ready, 1)
                    split(6, 9)
                    dve.wait_ge(rst_mm, it + 1)
                    dve.wait_ge(pstate_free, it + l * BT + 1)
                    ve.tensor_copy(pstate[:, 0, :], side[3][:, 0:P]).then_inc(rst_ready, 1)
                    split(9, 11)
                    dve.wait_ge(unit_used, ub + RING + UB * 2)
                    dve.wait_ge(bank_free[0], l * BANK_USES + BK_S + h + 1 + BF)
                    dve.wait_ge(shist_out, it + 1)
                    ve.tensor_tensor(sext[:, SW - 1:SW - 1 + T], acc[1][:, 0:T], sc_c[:, 0:T], ALU.mult)
                    ve.tensor_tensor(samples(sext[:, :], SW - 1 + T, SW, SW - 1), acc[1][:, T:N], sc_c[:, T:N], ALU.mult).then_inc(bank_free[1], 1)
                    dve.wait_ge(rvb_mm, it + 1)
                    dve.wait_ge(rdecayed, it + 1)
                    for b in range(NS):
                        ve.scalar_tensor_tensor(out=state[:, b, :], in0=side[b // 4][:, (b % 4) * P:(b % 4 + 1) * P],
                                                scalar=head[:, 1, T + b:T + b + 1], in1=state[:, b, :],
                                                op0=ALU.mult, op1=ALU.add).then_inc(rstate_new, 1)
                    split(11, 13)
                    dve.wait_ge(bank_free[1], l * BANK_USES + BK_S + h + 1 + BF)
                    dve.wait_ge(shist_in, it + 1)
                    tap = Q_SCW + it * SW
                    ve.tensor_scalar(sconv[:, :], sext[:, 0:SC], col(par, tap), None, ALU.mult).then_inc(sconv_step, 1)
                    for k in range(1, SW):
                        dve.wait_ge(sconv_step, it * SW + SW + k)
                        ve.scalar_tensor_tensor(out=sconv[:, :], in0=sext[:, k:k + SC], scalar=col(par, tap + k),
                                                in1=sconv[:, :], op0=ALU.mult, op1=ALU.add).then_inc(sconv_step, 1)
                    split(13, 17)
                    dve.wait_ge(rss_mm, it + 1)
                    ve.tensor_scalar(oms[:, :], side[3][:, 0:N], 1.0 / P, EPS, ALU.mult, ALU.add).then_inc(ro_step, 1)
                    dve.wait_ge(ro_step, it * 4 + 1)
                    ve.reciprocal(orc[:, :], oms[:, :]).then_inc(ro_step, 1)
                    dve.wait_ge(sconv_step, it * SW + 2 * SW)
                    dve.wait_ge(unit_used, ub + RING + UB * 3)
                    ve.tensor_tensor(sprod[:, 0:T], acc[2][:, 0:T], sconv[:, 0:T], ALU.mult)
                    ve.tensor_tensor(sprod[:, T:N], acc[2][:, T:N], sconv[:, SW - 1 + T:SC:SW], ALU.mult).then_inc(bank_free[2], 1)
                    split(17, 19)
                    dve.wait_ge(rors_ready, it + 1)
                    ve.tensor_tensor(orc[:, :], osb[:, :], oms[:, :], ALU.mult).then_inc(ro_step, 1)
                    dve.wait_ge(ro_step, it * 4 + 3)
                    ve.tensor_tensor(y32[:, 0, :], orc[:, :], wide[:, bass.ds(h + 3 * BT, 1), :].rearrange("p a n -> p (a n)"),
                                     ALU.mult).then_inc(ro_step, 1)
                    dve.wait_ge(bank_free[3], l * BANK_USES + BK_S + h + 1 + BF)
                    dve.wait_ge(bank_free[2], l * BANK_USES + BK_S + h + 1 + BF)
                    ve.tensor_tensor(y32[:, 1, :], sprod[:, :], sgate[:, :], ALU.mult).then_inc(sy_ready, 1)
                    dve.wait_ge(ryhi, it + 1)
                    ve.tensor_tensor(y_lo[:, bass.ds(RET * BT + h, 1), :], y32[:, 0, :],
                                     y_hi[:, bass.ds(RET * BT + h, 1), :].bitcast(F32), ALU.subtract).then_inc(y_ready[RET], 1)
                    dve.wait_ge(syhi, it + 1)
                    ve.tensor_tensor(y_lo[:, bass.ds(SCV * BT + h, 1), :], y32[:, 1, :],
                                     y_hi[:, bass.ds(SCV * BT + h, 1), :].bitcast(F32), ALU.subtract).then_inc(y_ready[SCV], 1)

                for g in range(BT):
                    it = l * BT + g
                    ub, split = splitter(l, OFF_P, g, PTURN)
                    split(3, 7)
                    dve.wait_ge(bank_free[2 * (g % 2)], l * BANK_USES + BK_P + g // 2 + 1 + BF)
                    dve.wait_ge(phist_in, it + 1)
                    src, w, steps = pext, 1, 0
                    for v in range(g + 1):
                        dst = (psum_a, psum_b)[v % 2]
                        lo = 2 * w - 1
                        ve.tensor_tensor(dst[:, lo:PE_], src[:, lo:PE_], src[:, lo - w:PE_ - w], ALU.add).then_inc(pwin, 1)
                        steps += 1
                        dve.wait_ge(pwin, l * PWIN + PWIN_AT[g] + steps)
                        src, w = dst, 2 * w
                    ve.tensor_tensor(src[:, PH:PH + 16], src[:, PH:PH + 16], con[:, C_CORR + 16 * g:C_CORR + 16 * g + 16],
                                     ALU.mult).then_inc(pwin, 1)
                    dve.wait_ge(pwin, l * PWIN + PWIN_AT[g] + steps + 1)
                    ve.scalar_tensor_tensor(out=pdiff[:, 0:T], in0=src[:, PH:PH + T], scalar=1.0 / w, in1=pext[:, PH:PH + T],
                                            op0=ALU.mult, op1=ALU.subtract)
                    ve.scalar_tensor_tensor(out=pdiff[:, T:N], in0=samples(src[:, :], PH + T, PH + 1, PH), scalar=1.0 / w,
                                            in1=samples(pext[:, :], PH + T, PH + 1, PH),
                                            op0=ALU.mult, op1=ALU.subtract).then_inc(psum_step, 1)
                    split(7, 11)
                    dve.wait_ge(pmix_mm, it + 1 + BT)
                    dve.wait_ge(bank_free[2 * (g % 2) + 1], l * BANK_USES + BK_P + g // 2 + 1 + BF)
                    ve.scalar_tensor_tensor(out=y32[:, 1, :], in0=side[0][:, 0:N], scalar=col(par, Q_PSC + it), in1=pgate[:, :],
                                            op0=ALU.mult, op1=ALU.mult).then_inc(py_ready, 1)
                    dve.wait_ge(pyhi, it + 1)
                    ve.tensor_tensor(y_lo[:, POOL * BT + g, :], y32[:, 1, :], y_hi[:, POOL * BT + g, :].bitcast(F32),
                                     ALU.subtract).then_inc(y_ready[POOL], 1)

                def merge_block(ub, i, p, first, m):
                    dve.wait_ge(unit_used, ub + RING + MB * (i + 1))
                    dve.wait_ge(bank_free[2 * p], bank_now[0] + i // 2 + 1 + BF)
                    dst = wide[:, bass.ds(m, 1), :]
                    if first:
                        ve.tensor_tensor(dst, msig[:, p, :], acc[2 * p + 1][:, 0:N], ALU.mult).then_inc(bank_free[2 * p + 1], 1)
                    else:
                        ve.tensor_tensor(mprod[:, p, :], msig[:, p, :], acc[2 * p + 1][:, 0:N], ALU.mult).then_inc(bank_free[2 * p + 1], 1)
                        dve.wait_ge(bank_free[2 * p + 1], bank_now[0] + i // 2 + 1 + BF)
                        ve.tensor_tensor(dst, dst, mprod[:, p, :], ALU.add).then_inc(merged_ready, 1)

                bank_now = [None]

                dve.wait_ge(phist_out, l * BT + BT + 1)
                settled(dve)
                with dve.Fori(0, BT) as h:
                    it = dve.snap(l * BT + h)
                    ub, split = splitter(l, OFF_M, h, MTURN)
                    bank_now[0] = dve.snap(l * BANK_USES + BK_M + h * 6)

                    def units(a, b):
                        for j in range(a, b):
                            split(j + 3, j + 4)
                            if j % MB == MB - 1:
                                i = j // MB
                                merge_block(ub, i, i % 2, i % 3 == 0, h * 4 + i // 3)

                    for c in range(3):
                        ve.tensor_copy(g_bc[:, c, :], col(g_col, h + c * BT).to_broadcast([P, P]))
                    ve.tensor_copy(beta_bc[:, :], col(beta, h + 2 * BT).to_broadcast([P, P]))
                    for c in range(CH):
                        ve.tensor_copy(hcol[:, c:c + 1], col(b_col, h + c * BT))
                        last = ve.tensor_copy(bet2[:, c:c + 1], col(beta, h + c * BT))
                    last.then_inc(gbc_ready, 1)
                    units(0, 3)
                    dve.wait_ge(gn_mm, it + 1)
                    for a in range(2):
                        last = ve.tensor_scalar(rn2[:, a, :], side[a][:, 0:N], EPS, None, ALU.add)
                    last.then_inc(grn_step, 1)
                    dve.wait_ge(grow_ready, it * 2 + 1)
                    dve.wait_ge(gbc_ready, it + 1)
                    for c in range(CH):
                        ve.scalar_tensor_tensor(out=dec[:, c, :], in0=b_row[:, c * P:(c + 1) * P], scalar=hcol[:, c:c + 1], in1=neg,
                                                op0=ALU.subtract, op1=ALU.add)
                    for c in range(CH):
                        ve.tensor_tensor(hcol[:, 4 + c:5 + c], b_row[:, c * P + P - 1:c * P + P], hcol[:, c:c + 1],
                                         ALU.subtract).then_inc(gcol_step, 1)
                    dve.wait_ge(grn_step, it * 2 + 1)
                    ve.reciprocal(rq2[:, :, :], rn2[:, :, :]).then_inc(grn_step, 1)
                    units(3, 4)
                    dve.wait_ge(grn_act, it + 1)
                    ve.scalar_tensor_tensor(out=head[:, 0, :], in0=gqkv[:, bass.ds(h * 3 * N, N)], scalar=float(P) ** -0.5,
                                            in1=rn2[:, 0, :], op0=ALU.mult, op1=ALU.mult)
                    ve.tensor_tensor(head[:, 1, :], gqkv[:, bass.ds(h * 3 * N + N, N)], rn2[:, 1, :], ALU.mult).then_inc(gqk_ready, 1)
                    dve.wait_ge(gcol_act, it * 2 + 1)
                    ve.tensor_scalar(nebc[:, :], hcol[:, 2:4], -1.0, None, ALU.mult)
                    dve.wait_ge(gcol_act, it * 2 + 2)
                    ve.tensor_tensor(decs[:, 0, :], dec[:, 0, :], strict, ALU.mult)
                    ve.tensor_tensor(decs[:, 1, :], dec[:, 1, :], strict, ALU.mult).then_inc(gcol_step, 1)
                    dve.wait_ge(gqk_ready, it + 1)
                    dve.wait_ge(grow_ready, it * 2 + 2)
                    ve.scalar_tensor_tensor(out=mk[:, :], in0=head[:, 1, T:N], scalar=-1.0, in1=eb_row[:, T:N],
                                            op0=ALU.mult, op1=ALU.mult)
                    ve.tensor_tensor(kb[:, :], b_row[:, N:BR], head[:, 1, T:N], ALU.mult)
                    ve.tensor_tensor(qd[:, :], head[:, 0, P:T], eb_row[:, P:T], ALU.mult).then_inc(gqd_ready, 1)
                    units(4, 8)
                    dve.wait_ge(gkq_mm, it + 1)
                    dve.wait_ge(gcol_step, it * 3 + 3)
                    for c in range(CH):
                        last = ve.scalar_tensor_tensor(out=E_[:, c, :], in0=side[0][:, c * P:(c + 1) * P], scalar=bet2[:, c:c + 1],
                                                       in1=decs[:, c, :], op0=ALU.mult, op1=ALU.mult)
                    last.then_inc(gE_ready, 1)
                    ve.tensor_tensor(attn[:, :, :].rearrange("p c d -> p (c d)"), side[0][:, T:2 * T],
                                     dec[:, :, :].rearrange("p c d -> p (c d)"), ALU.mult).then_inc(gattn_ready, 1)
                    dve.wait_ge(gE_ready, it + 1)
                    for c in range(CH):
                        last = ve.tensor_tensor(Xs[:, c, :], E_[:, c, :], con[:, C_LEV:C_LEV + P], ALU.mult)
                    last.then_inc(gR_ready, 1)
                    dve.wait_ge(gR_ready, it * 2 + 1)
                    for c in range(CH):
                        last = ve.tensor_tensor(TR[:, 1, c, :], ident, Xs[:, c, :], ALU.subtract)
                    last.then_inc(gR_ready, 1)
                    units(8, 11)
                    at = 11
                    for v in range(1, LEVELS):
                        if v in (3, 5):
                            dve.wait_ge(gdecayed, it * 2 + v // 2)
                            for b in range(2 * v - 6, 2 * v - 2):
                                ve.scalar_tensor_tensor(out=state[:, b, :], in0=side[3][:, (b % 4) * P:(b % 4 + 1) * P],
                                                        scalar=kb[:, b:b + 1], in1=state[:, b, :],
                                                        op0=ALU.mult, op1=ALU.add).then_inc(gstate_new, 1)
                        units(at, at + 2)
                        dve.wait_ge(gD_mm, it * 6 + v)
                        flat = TR[:, :, :, :].rearrange("p t c d -> p (t c d)")
                        if v < LEVELS - 1:
                            ve.tensor_tensor(flat, flat, side[1][:, :], ALU.subtract).then_inc(gTR_ready, 1)
                        else:
                            ve.tensor_tensor(flat[:, T:2 * T], flat[:, T:2 * T], side[1][:, T:2 * T], ALU.subtract).then_inc(gTR_ready, 1)
                        units(at + 2, at + 5)
                        at += 5
                    units(at, 45)
                    dve.wait_ge(gst_mm, it * 2 + 1)
                    dve.wait_ge(pstate_free, it + l * BT + BT + 1)
                    ve.tensor_copy(pstate[:, 1, :], side[3][:, 0:P]).then_inc(gst_ready, 1)
                    units(45, 47)
                    dve.wait_ge(gks_mm, it + 1)
                    ve.scalar_tensor_tensor(out=rhs1[:, :], in0=side[1][:, 0:P], scalar=nebc[:, 1:2], in1=vt[:, 1, :],
                                            op0=ALU.mult, op1=ALU.add).then_inc(grhs_ready, 1)
                    units(47, 52)
                    dve.wait_ge(gst_mm, it * 2 + 2)
                    ve.scalar_tensor_tensor(out=pstate[:, 1, :], in0=pstate[:, 1, :], scalar=eb_row[:, T - 1:T], in1=side[3][:, 0:P],
                                            op0=ALU.mult, op1=ALU.add).then_inc(gst_ready, 1)
                    units(52, 55)
                    dve.wait_ge(gss_mm, it + 1)
                    ve.tensor_scalar(oms[:, :], side[2][:, 0:N], 1.0 / P, EPS, ALU.mult, ALU.add).then_inc(go_step, 1)
                    dve.wait_ge(go_step, it * 4 + 1)
                    ve.reciprocal(orc[:, :], oms[:, :]).then_inc(go_step, 1)
                    units(55, 58)
                    dve.wait_ge(gors_ready, it + 1)
                    ve.scalar_tensor_tensor(out=orc[:, :], in0=osb[:, :], scalar=col(par, Q_GNG + l), in1=oms[:, :],
                                            op0=ALU.mult, op1=ALU.mult).then_inc(go_step, 1)
                    dve.wait_ge(go_step, it * 4 + 3)
                    ve.tensor_tensor(y32[:, 0, :], orc[:, :], gates[:, bass.ds(h, 1), :].rearrange("p a n -> p (a n)"),
                                     ALU.mult).then_inc(go_step, 1)
                    units(58, 60)
                    dve.wait_ge(gyhi, it + 1)
                    ve.tensor_tensor(y_lo[:, bass.ds(GDN * BT + h, 1), :], y32[:, 0, :],
                                     y_hi[:, bass.ds(GDN * BT + h, 1), :].bitcast(F32), ALU.subtract).then_inc(y_ready[GDN], 1)

                with dve.Fori(0, BT) as h:
                    ub, split = splitter(l, OFF_X, h, XTURN)
                    bank_now[0] = dve.snap(l * BANK_USES + BK_X + h * 2)
                    for i in range(4):
                        split(MB * i + 3, MB * i + 8)
                        merge_block(ub, i, i % 2, False, h * 4 + i)

                for q in range(4):
                    dve.wait_ge(mhi_ready, l * 4 + q + 1)
                    ve.tensor_tensor(act_lo[:, 4 * q:4 * q + 4, :], wide[:, 4 * q:4 * q + 4, :],
                                     act_hi[:, 4 * q:4 * q + 4, :].bitcast(F32), ALU.subtract).then_inc(mlo_ready, 1)

                def out_turn(h, ahead):
                    ub, split = splitter(l, OFF_O, h, TURN)
                    for i in range(4):
                        split(4 * i + 3, 4 * i + 7 if i < 3 else TURN + ahead)
                        dve.wait_ge(unit_used, ub + RING + UB * (i + 1))
                        dst = x[:, bass.ds(h * 4 + i, 1), :]
                        ve.tensor_tensor(dst, dst, acc[i][:, 0:N], ALU.add).then_inc(bank_free[i], 1)

                with dve.Fori(0, BT - 1) as h:
                    out_turn(h, 3)
                out_turn(BT - 1, 0)
            norm_apply(DEPTH, lambda q: None)

        @block.tensor
        def _(pe):
            mm = nc.tensor.matmul

            def product(bank, slot, hi, lo, k0, first, last):
                for k in range(UK):
                    w_h, w_l = whi[:, slot, k * P:(k + 1) * P], wlo[:, slot, k * P:(k + 1) * P]
                    mm(acc[bank][:, 0:N], w_h, hi[:, k0 + k, :], start=first and k == 0, stop=False)
                    mm(acc[bank][:, 0:N], w_h, lo[:, k0 + k, :], start=False, stop=False)
                    op = mm(acc[bank][:, 0:N], w_l, hi[:, k0 + k, :], start=False, stop=last and k == UK - 1)
                op.then_inc(unit_used, 1)

            def streamer(l, off, i, per):
                ub = pe.snap(l * UNITS + off + i * per)

                def unit(j, bank, hi, lo, k0, first, last):
                    pe.wait_ge(lo_ready, ub + j + 1 + RING)
                    product(bank, j % RING, hi, lo, k0, first, last)
                return unit

            def norm_sums(n):
                for k in range(KT):
                    pe.wait_ge(sq_ready, n * KT + k + 1)
                    mm(side[0][:, 0:N], ones, squares[:, k % 2, :], start=k == 0, stop=k == KT - 1).then_inc(norm_mm, 1)

            pe.wait_ge(con_loaded, 16)
            pe.wait_ge(par_loaded, 16)
            with pe.Fori(0, DEPTH) as l:
                norm_sums(l)

                def blocks(unit, a, b, free):
                    for j in range(a, b):
                        i = j // UB
                        if j % UB == 0:
                            pe.wait_ge(bank_free[i % 4], free + BF)
                        unit(j, i % 4, act_hi, act_lo, UK * (j % UB), j % UB == 0, j % UB == UB - 1)

                pe.wait_ge(h_ready, l * 4 + 4)
                for c in range(3):
                    lo, n = c * P, (P, P, NS)[c]
                    for k in range(KT):
                        op = mm(side[1][0:n, 2 * BT * c:2 * BT * (c + 1)], wide[:, k, lo:lo + n],
                                par[:, bass.ds(Q_WAB + (l * KT + k) * 2 * BT, 2 * BT)], start=k == 0, stop=k == KT - 1)
                    op.then_inc(ab_mm, 1)

                pe.wait_ge(act_lo_ready, l * 4 + 4)
                settled(pe)
                with pe.Fori(0, BT) as h:
                    unit = streamer(l, OFF_G, h, TURN)
                    blocks(unit, 0, TURN, pe.snap(l * BANK_USES + BK_G + h))
                with pe.Fori(0, BT) as h:
                    unit = streamer(l, OFF_R, h, TURN)
                    blocks(unit, 0, TURN, pe.snap(l * BANK_USES + BK_R + h))

                pe.wait_ge(ab_step, l * 15 + 15)
                mm(side[1][:, 0:CH * BT], tri, g_col[:, 0:CH * BT], start=True, stop=True).then_inc(bcol_mm, 1)

                with pe.Fori(0, BT) as h:
                    it = pe.snap(l * BT + h)
                    unit = streamer(l, OFF_S, h, TURN)
                    free = pe.snap(l * BANK_USES + BK_S + h)
                    blocks(unit, 0, 2, free)
                    pe.wait_ge(head_copied, it + 1)
                    pe.wait_ge(bcol_ready, l + 1)
                    mm(side[0][:, 0:T], head[:, 1, 0:P], head[:, 0, 0:T], start=True, stop=True)
                    mm(side[0][:, T:T + P], head[:, 1, P:T], head[:, 0, P:T], start=True, stop=True).then_inc(rsc_mm, 1)
                    for a in range(2):
                        for c in range(CH):
                            op = nc.tensor.transpose(side[1][:, (2 * a + c) * P:(2 * a + c + 1) * P],
                                                     head[:, 1 + a, c * P:(c + 1) * P], ident)
                    op.then_inc(rtr_mm, 1)
                    blocks(unit, 2, 5, free)
                    pe.wait_ge(scores_ready, it + 1)
                    pe.wait_ge(kdvt_ready, it + l * BT + 1)
                    mm(side[2][:, 0:T], vt[:, 0, :], scores[:, 0:T], start=True, stop=False)
                    mm(side[2][:, P:T], vt[:, 1, :], scores[:, T:T + P], start=False, stop=True).then_inc(ro_mm, 1)
                    for c in range(CH):
                        op = mm(side[3][:, 0:P], kd[:, c, :], vt[:, c, :], start=c == 0, stop=c == CH - 1)
                    op.then_inc(rst_mm, 1)
                    blocks(unit, 5, 7, free)
                    for b in range(NS):
                        op = mm(side[b // 4][:, (b % 4) * P:(b % 4 + 1) * P], head[:, 2, T + b:T + b + 1].to_broadcast([P, P]),
                                ident, start=True, stop=True)
                    op.then_inc(rvb_mm, 1)
                    blocks(unit, 7, 11, free)
                    pe.wait_ge(rstate_new, it * NS + NS)
                    for b in range(NS):
                        op = mm(side[2][:, T + b:T + b + 1], state[:, b, :], head[:, 0, T + b:T + b + 1], start=True, stop=True)
                    op.then_inc(ros_mm, 1)
                    blocks(unit, 11, 14, free)
                    pe.wait_ge(ro_copied, it + 1)
                    mm(side[3][:, 0:N], ones, osq[:, :], start=True, stop=True).then_inc(rss_mm, 1)
                    blocks(unit, 14, TURN, free)

                pe.wait_ge(plw_loaded, l * 16 + 16)
                for g in range(BT):
                    unit = streamer(l, OFF_P, g, PTURN)
                    for j in range(PTURN):
                        bank = 2 * (g % 2) + j // UB
                        if j % UB == 0:
                            pe.wait_ge(bank_free[bank], l * BANK_USES + BK_P + g // 2 + BF)
                        unit(j, bank, act_hi, act_lo, UK * (j % UB), j % UB == 0, j % UB == UB - 1)
                    pe.wait_ge(psum_step, l * BT + g + 2)
                    mm(side[0][:, 0:N], plw[:, g, :], pdiff[:, :], start=True, stop=True).then_inc(pmix_mm, 1)

                def merge_units(unit, a, b, branches, free):
                    for j in range(a, b):
                        i, u = j // MB, j % MB
                        p = i % 2
                        if u == 0:
                            pe.wait_ge(bank_free[2 * p], free + i // 2 + BF)
                        if u < UB:
                            unit(j, 2 * p, act_hi, act_lo, UK * u, u == 0, u == UB - 1)
                        else:
                            pe.wait_ge(bank_free[2 * p + 1], free + i // 2 + BF)
                            unit(j, 2 * p + 1, y_hi, y_lo, BT * branches[i % len(branches)], True, True)

                for n in (SCV, POOL, RET):
                    pe.wait_ge(y_ready[n], l * BT + BT)
                settled(pe)
                with pe.Fori(0, BT) as h:
                    it = pe.snap(l * BT + h)
                    unit = streamer(l, OFF_M, h, MTURN)
                    free = pe.snap(l * BANK_USES + BK_M + h * 6)

                    def units(a, b):
                        merge_units(unit, a, b, (SCV, POOL, RET), free)

                    units(0, 1)
                    pe.wait_ge(gbc_ready, it + 1)
                    pe.wait_ge(gsq_ready, it * 2 + 2)
                    for a in range(2):
                        op = mm(side[a][:, 0:N], ones, sq2[:, a, :], start=True, stop=True)
                    op.then_inc(gn_mm, 1)
                    for c in range(CH):
                        mm(side[2][:, c * P:(c + 1) * P], g_bc[:, c, :], tri, start=True, stop=True)
                    mm(side[2][:, T:N], g_bc[0:NS, 2, :], con[0:NS, C_ID:C_ID + NS], start=True, stop=True)
                    mm(side[2][:, N:BR], beta_bc[0:NS, :], con[0:NS, C_ID:C_ID + NS], start=True, stop=True).then_inc(grow_mm, 1)
                    for c in range(CH):
                        op = nc.tensor.transpose(side[3][:, c * P:(c + 1) * P], head[:, 2, c * P:(c + 1) * P], ident)
                    op.then_inc(gvt_mm, 1)
                    units(1, 6)
                    pe.wait_ge(gqk_ready, it + 1)
                    for a in range(2):
                        for c in range(CH):
                            op = mm(side[0][:, (2 * a + c) * P:(2 * a + c + 1) * P], head[:, 1, c * P:(c + 1) * P],
                                    head[:, 1 - a, c * P:(c + 1) * P], start=True, stop=True)
                    op.then_inc(gkq_mm, 1)
                    for c in range(CH):
                        op = nc.tensor.transpose(side[1][:, c * P:(c + 1) * P], head[:, 1, c * P:(c + 1) * P], ident)
                    op.then_inc(gkt_mm, 1)
                    units(6, 9)
                    pe.wait_ge(gR_ready, it * 2 + 2)
                    for c in range(CH):
                        op = nc.tensor.transpose(side[0][:, c * P:(c + 1) * P], TR[:, 1, c, :], ident)
                    op.then_inc(gT_mm, 1)
                    units(9, 11)
                    at = 11
                    for v in range(1, LEVELS):
                        if v == 1:
                            pe.wait_ge(gT_ready, it + 1)
                        else:
                            pe.wait_ge(gTR_ready, it * 6 + v - 1)
                        pe.wait_ge(gem_ready, it * 6 + v)
                        for c in range(CH):
                            op = mm(side[0][:, c * P:(c + 1) * P], Em[:, v % 2, c * P:(c + 1) * P], TR[:, 0, c, :], start=True, stop=True)
                        op.then_inc(gX_mm, 1)
                        if v in (2, 4):
                            if v == 2:
                                pe.wait_ge(state_loaded, (it + l * BT) * 16 + 16 * BT + 16)
                                pe.wait_ge(gqd_ready, it + 1)
                                pe.wait_ge(kdvt_ready, it + (l + 1) * BT + 1)
                            else:
                                pe.wait_ge(gstate_new, it * NS + 4)
                            for b in range(2 * v - 4, 2 * v):
                                dst = side[3][:, (b % 4) * P:(b % 4 + 1) * P]
                                mm(dst, head[:, 2, T + b:T + b + 1].to_broadcast([P, P]), ident, start=True, stop=False)
                                op = mm(dst, mk[:, b:b + 1].to_broadcast([P, P]), state[:, b, :], start=False, stop=True)
                            op.then_inc(gdl_mm, 1)
                        if v == 6:
                            pe.wait_ge(gstate_new, it * NS + NS)
                            for b in range(NS):
                                op = mm(side[3][:, b:b + 1], state[:, b, :], head[:, 0, T + b:T + b + 1], start=True, stop=True)
                            op.then_inc(gos_mm, 1)
                        units(at, at + 2)
                        pe.wait_ge(gX_ready, it * 6 + v)
                        if v < LEVELS - 1:
                            for c in range(CH):
                                mm(side[1][:, c * P:(c + 1) * P], TR[:, 1, c, :], Xs[:, c, :], start=True, stop=True)
                        for c in range(CH):
                            op = mm(side[1][:, T + c * P:T + (c + 1) * P], Xs[:, c, :], TR[:, 1, c, :], start=True, stop=True)
                        op.then_inc(gD_mm, 1)
                        units(at + 2, at + 5)
                        at += 5
                    pe.wait_ge(gTR_ready, it * 6 + 6)
                    mm(side[2][:, 0:P], TR[:, 1, 0, :], vt[:, 0, :], start=True, stop=True).then_inc(gsol_mm, 1)
                    units(at, 43)
                    pe.wait_ge(gvn_ready, it * 2 + 1)
                    pe.wait_ge(gkd_ready, it + 1)
                    pe.wait_ge(gos_copied, it + 1)
                    mm(side[3][:, 0:P], kd[:, 0, :], vn[:, 0, :], start=True, stop=True).then_inc(gst_mm, 1)
                    units(43, 46)
                    pe.wait_ge(gst_ready, it * 2 + 1)
                    mm(side[1][:, 0:P], head[:, 1, P:T], pstate[:, 1, :], start=True, stop=True).then_inc(gks_mm, 1)
                    pe.wait_ge(gattn_ready, it + 1)
                    mm(side[0][:, 0:P], vn[:, 0, :], attn[:, 0, :], start=True, stop=True)
                    units(46, 48)
                    pe.wait_ge(grhs_ready, it + 1)
                    mm(side[2][:, 0:P], TR[:, 1, 1, :], rhs1[:, :], start=True, stop=True).then_inc(gsol_mm, 1)
                    units(48, 51)
                    mm(side[0][:, P:T], pstate[:, 1, :], qd[:, :], start=True, stop=False)
                    pe.wait_ge(gvn_ready, it * 2 + 2)
                    mm(side[0][:, P:T], vn[:, 1, :], attn[:, 1, :], start=False, stop=True).then_inc(go_mm, 1)
                    mm(side[3][:, 0:P], kd[:, 1, :], vn[:, 1, :], start=True, stop=True).then_inc(gst_mm, 1)
                    units(51, 54)
                    pe.wait_ge(go_copied, it * 2 + 2)
                    mm(side[2][:, 0:N], ones, osq[:, :], start=True, stop=True).then_inc(gss_mm, 1)
                    units(54, 60)

                with pe.Fori(0, BT) as h:
                    unit = streamer(l, OFF_X, h, XTURN)
                    free = pe.snap(l * BANK_USES + BK_X + h * 2)
                    merge_units(unit, 0, 4, (GDN,), free)
                    pe.wait_ge(y_ready[GDN], l * BT + BT)
                    merge_units(unit, 4, XTURN, (GDN,), free)

                pe.wait_ge(mlo_ready, l * 4 + 4)
                settled(pe)
                with pe.Fori(0, BT) as h:
                    unit = streamer(l, OFF_O, h, TURN)
                    blocks(unit, 0, TURN, pe.snap(l * BANK_USES + BK_O + h))
            norm_sums(DEPTH)


def shape_constants():
    f = np.float32
    con = np.zeros((P, C_END), f)
    i = np.arange(P)
    con[:, C_ID:C_ID + P] = np.eye(P)
    con[:, C_ONE:C_ONE + P] = 1.0
    upper = i[None, :] >= i[:, None]
    con[:, C_TRI:C_TRI + P] = upper
    con[:, C_NEG:C_NEG + P] = np.where(upper, 0.0, -1e30)
    con[:, C_STRICT:C_STRICT + P] = i[None, :] > i[:, None]
    for v in range(LEVELS):
        blk = i >> v
        con[:, C_LEV + v * P:C_LEV + (v + 1) * P] = (blk[:, None] % 2 == 0) & (blk[None, :] == blk[:, None] + 1)
    lg = np.log(1.0 - 2.0 ** (-5.0 - np.arange(BT)))
    t = np.arange(T)
    lag = t[None, :] - i[:, None]
    for h in range(BT):
        con[:, C_DM + h * T:C_DM + (h + 1) * T] = np.where(lag >= 0, np.exp(lg[h] * np.maximum(lag, 0)), 0.0)
        for c in range(CH):
            con[:, C_GDEC + h * CH + c] = np.exp(lg[h] * (T - 1 - (c * P + i)))
        con[:, C_GAM + h] = np.exp(lg[h])
    half = P // 2
    inv = (f(10000.0) ** (-np.arange(half, dtype=f) / f(half))).astype(f)
    pos = np.concatenate([np.arange(T), np.full(NS, PAST)]).astype(f)
    ang = (pos[None, :] * inv[:, None]).astype(f).astype(np.float64)
    cos, sin = np.cos(ang), np.sin(ang)
    con[:, C_COS:C_COS + N] = np.concatenate([cos, cos])
    con[:, C_SIN:C_SIN + N] = np.concatenate([sin, -sin])
    for g, w in enumerate(WINDOWS):
        con[:, C_CORR + 16 * g:C_CORR + 16 * (g + 1)] = w / np.minimum(np.arange(16) + 1, w)
    return con


def kernel(x_prompt, x_sample, state_ret, state_gdn, state_gdn_conv, state_sconv, state_pool,
           norm_g, w_in, gdn_conv_w, gdn_a_log, gdn_dt_bias, gdn_norm_g,
           sconv_w, pool_w, pool_scale, w_branch, w_out, final_norm_g):
    import concourse.bacc as bacc
    from concourse.bass_utils import run_bass_kernel_spmd

    A = np.asarray
    w_in, w_branch, w_out = A(w_in), A(w_branch), A(w_out)

    SPLIT = [BW] * 4 + [3 * BW, BW, BT, BT] + [BW] * 6 + [4 * D_MODEL]
    start = np.concatenate([[0], np.cumsum(SPLIT)])
    (RQ, RK, RV, RG, GQKV, GG, GA, GB, SB, SCC, SH, SG, PU, PG, ML) = start[:-1]

    def units(w, c0):
        k = w.shape[1] // P
        b = w[:, :, c0:c0 + P].reshape(DEPTH, k // UK, UK, P, P)
        return b.transpose(0, 1, 3, 2, 4).reshape(DEPTH, k // UK, P, UC)

    parts = []
    for h in range(BT):
        parts += [units(w_in, c + h * P) for c in (GQKV, GQKV + BW, GQKV + 2 * BW, GG)]
    for h in range(BT):
        parts += [units(w_in, c + h * P) for c in (RQ, RK, RV, RG)]
    for h in range(BT):
        parts += [units(w_in, c + h * P) for c in (SCC, SH, SB, SG)]
    for h in range(BT):
        parts += [units(w_in, c + h * P) for c in (PU, PG)]
    for m in range(KT):
        for n in (SCV, POOL, RET):
            parts += [units(w_in, ML + n * D_MODEL + m * P), units(w_branch[:, n], m * P)]
    for m in range(KT):
        parts += [units(w_in, ML + GDN * D_MODEL + m * P), units(w_branch[:, GDN], m * P)]
    for m in range(KT):
        parts += [units(w_out, m * P)]
    w_stream = np.concatenate(parts, axis=1)
    assert w_stream.shape[1] == UNITS

    xt = np.concatenate([A(x_prompt)[0], A(x_sample)[:, 0]], axis=0)
    x_in = np.ascontiguousarray(xt.T.reshape(KT, P, N).transpose(1, 0, 2))

    def chan(a, tiles):
        a = A(a)
        a = a.reshape(a.shape[:-1] + (tiles, P))
        return np.moveaxis(a, -1, 0)

    def flat(a):
        return np.ascontiguousarray(a).reshape(P, -1)

    def rows(a):
        return flat(np.broadcast_to(A(a)[None, :, None, :], (P, DEPTH, 3, BT)))

    wab = w_in[:, :, GA:GA + 2 * BT].reshape(DEPTH, KT, P, 2 * BT).transpose(2, 0, 1, 3)
    gh = chan(state_gdn_conv, 3 * BT).reshape(P, DEPTH, NS, GW - 1, 3, BT).transpose(0, 1, 5, 4, 2, 3)
    sh = chan(state_sconv, BT).transpose(0, 1, 4, 2, 3)
    pool_in = np.ascontiguousarray(chan(state_pool, BT).transpose(1, 0, 4, 2, 3)).reshape(DEPTH, P, BT * NS * PH)
    params = np.concatenate([
        flat(chan(norm_g, KT)), flat(chan(final_norm_g, KT)),
        flat(chan(gdn_conv_w, 3 * BT).reshape(P, DEPTH, GW, 3, BT).transpose(0, 1, 4, 3, 2)),
        flat(chan(sconv_w, BT).transpose(0, 1, 3, 2)),
        flat(A(gdn_norm_g).T), flat(chan(pool_scale, BT)),
        rows(gdn_dt_bias), rows(gdn_a_log), flat(wab), flat(gh), flat(sh)], axis=1)
    assert params.shape[1] == Q_END
    w_pool = np.ascontiguousarray(A(pool_w).transpose(0, 2, 1, 3))

    arrays = {"w_stream": w_stream, "w_pool": w_pool, "pool_in": pool_in, "x_in": x_in, "params": params, "consts": shape_constants(),
              "ret_in": A(state_ret), "gdn_in": A(state_gdn)}
    st = (DEPTH, NS, BT, P, P)
    outs = {"y_out": (P, KT * N), "hist_out": (DEPTH, P, H_END), "p_ret": (DEPTH, 1, BT, P, P), "p_gdn": (DEPTH, 1, BT, P, P),
            "s_ret": st, "s_gdn": st}
    nc = bacc.Bacc("TRN2", target_bir_lowering=False, num_devices=1)
    args = [nc.dram_tensor(k, a.shape, F32, kind="ExternalInput").ap() for k, a in arrays.items()]
    args += [nc.dram_tensor(k, s, F32, kind="ExternalOutput").ap() for k, s in outs.items()]
    trunk(nc, *args)
    r = run_bass_kernel_spmd(nc, [arrays], core_ids=[0]).results[0]

    y = r["y_out"].reshape(P, KT, N).transpose(2, 1, 0).reshape(N, D_MODEL)
    y_prompt, y_sample = y[None, :T], y[T:, None]
    ho = r["hist_out"]

    def hists(lo, hi, shape, perm, k, ch):
        a = ho[:, :, lo:hi].reshape((DEPTH, P) + shape).transpose(perm)
        a = a.reshape(DEPTH, NS + 1, k, ch)
        return np.ascontiguousarray(a[:, :1]), np.ascontiguousarray(a[:, 1:])

    pgc, sgc = hists(H_G, H_S, (BT, 3, NS + 1, GW - 1), (0, 4, 5, 3, 2, 1), GW - 1, 3 * BW)
    psc, ssc = hists(H_S, H_P, (BT, NS + 1, SW - 1), (0, 3, 4, 2, 1), SW - 1, BW)
    ppl, spl = hists(H_P, H_END, (BT, NS + 1, PH), (0, 3, 4, 2, 1), PH, BW)
    return (np.ascontiguousarray(y_prompt), np.ascontiguousarray(y_sample), r["p_ret"], r["p_gdn"], pgc, psc, ppl,
            r["s_ret"], r["s_gdn"], sgc, ssc, spl)
```

```python
from contextlib import ExitStack

import numpy as np

import concourse.bass as bass
from concourse import mybir

F32 = mybir.dt.float32
F32R = mybir.dt.float32r
ALU = mybir.AluOpType
ACT = mybir.ActivationFunctionType

P = 128
DEPTH = 2
D_MODEL = 2048
KT = D_MODEL // P
BW = D_MODEL // 4
BT = BW // P
T = 256
NS = 8
N = T + NS
CH = T // P
PAST = 2048
EPS = 1e-6
WINDOWS = (2, 4, 8, 16)
RET, GDN, SCV, POOL = range(4)
YT = {SCV: 0, POOL: BT, RET: 2 * BT, GDN: 3 * BT}
GW, SW, PH = 4, 3, 15

GE = GW - 1 + T + NS * GW
SE = SW - 1 + T + NS * SW
PE_ = PH + T + NS * (PH + 1)
GC = GE - (GW - 1)
SC = SE - (SW - 1)

UK = 4
UC = UK * P
RING = 4
UB = KT // UK
TURN = 4 * UB
PTURN = 2 * UB
MB = UB + 1
MTURN = 12 * MB
LEV0, LEVU = 16, 4
XTURN = 4 * MB
OFF_G = 0
OFF_R = OFF_G + 4 * TURN
OFF_S = OFF_R + 4 * TURN
OFF_P = OFF_S + 4 * TURN
OFF_M = OFF_P + 4 * PTURN
OFF_X = OFF_M + 4 * MTURN
OFF_O = OFF_X + 4 * XTURN
UNITS = OFF_O + 4 * TURN

BK_G, BK_R, BK_S, BK_P, BK_M, BK_X, BK_O = 0, 4, 8, 12, 14, 38, 46
BANK_USES = 50
BF = 4

PWIN_AT = (0, 2, 5, 9)
PWIN = 14

C_ID, C_ONE, C_TRI, C_NEG, C_STRICT, C_LEV = 0, P, 2 * P, 3 * P, 4 * P, 5 * P
LEVELS = 7
C_DM = C_LEV + LEVELS * P
C_COS = C_DM + BT * T
C_SIN = C_COS + N
C_CORR = C_SIN + N
C_GDEC = C_CORR + BT * 16
C_GAM = C_GDEC + BT * CH
C_END = C_GAM + BT

Q_NG = 0
Q_GCW = Q_NG + (DEPTH + 1) * KT
Q_SCW = Q_GCW + DEPTH * BT * 3 * GW
Q_GNG = Q_SCW + DEPTH * BT * SW
Q_PSC = Q_GNG + DEPTH
Q_DT = Q_PSC + DEPTH * BT
Q_AL = Q_DT + DEPTH * 3 * BT
Q_WAB = Q_AL + DEPTH * 3 * BT
Q_GH = Q_WAB + DEPTH * KT * 2 * BT
Q_SH = Q_GH + DEPTH * BT * 3 * NS * (GW - 1)
Q_PH = Q_SH + DEPTH * BT * NS * (SW - 1)
Q_END = Q_PH

H_G = 0
H_S = H_G + BT * 3 * (NS + 1) * (GW - 1)
H_P = H_S + BT * (NS + 1) * (SW - 1)
H_END = H_P + BT * (NS + 1) * PH

SHARED = 6514


def trunk(nc, w_stream, w_pool, pool_in, x_in, params, consts, ret_in, gdn_in, y_out, hist_out,
          p_ret, p_gdn, s_ret, s_gdn):
    with ExitStack() as ctx:
        def sb(name, shape, dt=F32):
            return ctx.enter_context(nc.sbuf_tensor(name, [P] + shape, dt))

        def psum(name):
            return ctx.enter_context(nc.psum_tensor(name, [P, 512], F32))

        primes = []

        def sem(name, primed=0):
            s = ctx.enter_context(nc.semaphore(name))
            if primed:
                primes.append((s, primed))
            return s

        raw = sb("raw", [RING, UC])
        whi = sb("whi", [RING, UC], F32R)
        wlo = sb("wlo", [RING, UC], F32R)
        x = sb("x", [KT, N])
        act_hi = sb("act_hi", [KT, N], F32R)
        act_lo = sb("act_lo", [KT, N], F32R)
        y_hi = sb("y_hi", [KT, N], F32R)
        y_lo = sb("y_lo", [KT, N], F32R)
        wide = sb("wide", [KT, N])
        rqkv = wide[:, 0:3 * BT, :].rearrange("p a n -> p (a n)")
        gqkv = sb("gqkv", [BT * 3 * N])
        gates = sb("gates", [BT, N])
        con = sb("con", [C_END])
        par = sb("par", [Q_END])
        hist = sb("hist", [H_END])
        phist = sb("phist", [BT * NS * PH])
        pieces = {}

        def shared(kind, shape):
            size = int(np.prod(shape))
            at = pieces.get(kind, 0)
            pieces[kind] = at + size
            assert at + size <= SHARED, (kind, at + size)
            view = share[:, at:at + size]
            if len(shape) == 2:
                view = view.rearrange("p (a b) -> p a b", b=shape[1])
            if len(shape) == 3:
                view = view.rearrange("p (a b c) -> p a b c", b=shape[1], c=shape[2])
            return view

        def early(shape):
            return shared("early", shape)

        def late(shape):
            return shared("late", shape)

        share = sb("share", [SHARED])
        ident, ones = con[:, C_ID:C_ID + P], con[:, C_ONE:C_ONE + P]
        tri, neg = con[:, C_TRI:C_TRI + P], con[:, C_NEG:C_NEG + P]
        strict = con[:, C_STRICT:C_STRICT + P]
        squares = early([2, N])
        ms = early([N])
        rms = early([N])
        rstd = ms
        ab = sb("ab", [3 * 2 * BT])
        A3 = 3 * BT
        ab_x, ab_abs, ab_e, ab_den, ab_rec, ab_s, ab_s2, ab_q, ab_relu, ab_sp, ab_ea, g_col, beta = \
            [sb(n, [A3]) for n in ("ab_x", "ab_abs", "ab_e", "ab_den", "ab_rec", "ab_s", "ab_s2", "ab_q",
                                   "ab_relu", "ab_sp", "ab_ea", "g_col", "beta")]
        b_col = sb("b_col", [CH * BT])
        gext = early([3, GE])
        gconv = early([3, GC])
        rope_a = early([2, N])
        rope_b = early([2, N])
        sc_c = early([N])
        sext = early([SE])
        sconv = early([SC])
        sgate = early([N])
        sprod = early([N])
        pext = early([PE_])
        psum_a = rope_a.rearrange("p a n -> p (a n)")[:, 0:PE_]
        psum_b = rope_b.rearrange("p a n -> p (a n)")[:, 0:PE_]
        pdiff = early([N])
        pgate = early([N])
        plw = sb("plw", [BT, P])
        y32 = sb("y32", [2, N])
        head = sb("head", [3, N])
        qd = late([P])
        state = sb("state", [NS, P])
        pstate = sb("pstate", [2, P])
        sq2 = late([2, N])
        rn2 = late([2, N])
        rq2 = late([2, N])
        osb = sb("osb", [N])
        osq = sb("osq", [N])
        sq_sum = osq
        oms = sb("oms", [N])
        orc = sb("orc", [N])
        scores = early([T + P])
        kd = sb("kd", [CH, P])
        vt = sb("vt", [CH, P])
        g_bc = late([3, P])
        beta_bc = late([P])
        BR = N + NS
        b_row = late([BR])
        eb_row = late([BR])
        hcol = sb("hcol", [8])
        nebc = sb("nebc", [CH])
        bet2 = sb("bet2", [CH])
        dec = late([CH, P])
        decs = late([CH, P])
        E_ = late([CH, P])
        Em = late([2, CH * P])
        attn = late([CH, P])
        TR = late([2, CH, P])
        Xs = late([CH, P])
        vn = late([CH, P])
        rhs1 = late([P])
        mk = sb("mk", [NS])
        kb = sb("kb", [NS])
        msig = late([2, N])
        mprod = late([2, N])

        acc = [psum(f"acc{i}") for i in range(4)]
        side = [psum(f"side{i}") for i in range(4)]

        raw_loaded = [sem(f"raw_loaded{i}") for i in range(RING)]
        hi_ready = sem("hi_ready")
        lo_ready = sem("lo_ready", RING)
        unit_used = sem("unit_used", RING)
        bank_free = [sem(f"bank_free{i}", BF) for i in range(4)]
        x_loaded = [sem(f"x_loaded{q}") for q in range(4)]
        con_loaded, par_loaded = sem("con_loaded"), sem("par_loaded")
        plw_loaded, ph_loaded, state_loaded = sem("plw_loaded"), sem("ph_loaded"), sem("state_loaded")
        out_written, hist_written = sem("out_written"), sem("hist_written")
        state_written, pstate_written, pstate_free = sem("state_written"), sem("pstate_written"), sem("pstate_free", 1)
        zeros_set, passed = sem("zeros_set"), sem("passed")
        sum_cleared = sem("sum_cleared")
        sq_ready, norm_mm, ms_ready, rms_ready, rstd_ready = [sem(n) for n in
            ("sq_ready", "norm_mm", "ms_ready", "rms_ready", "rstd_ready")]
        sq_added, xhi_ready, xlo_ready = sem("sq_added", 1), sem("xhi_ready"), sem("xlo_ready")
        x_updated = sem("x_updated")
        h_ready, hhi_ready, hlo_ready = sem("h_ready"), sem("hhi_ready"), sem("hlo_ready")
        ahi_copied, alo_copied = sem("ahi_copied"), sem("alo_copied")
        ab_mm, ab_evac, ab_step, ab_act, bcol_mm, bcol_ready = [sem(n) for n in
            ("ab_mm", "ab_evac", "ab_step", "ab_act", "bcol_mm", "bcol_ready")]
        ghist_in, gconv_step, gqkv_ready, ghist_out = [sem(n, p) for n, p in
            (("ghist_in", 0), ("gconv_step", 3 * GW), ("gqkv_ready", 0), ("ghist_out", 3))]
        rope_step = sem("rope_step")
        head_copied, rsc_mm, rtr_mm, scores_ready, kdvt_ready, ro_mm, rst_mm, rst_ready, rvb_mm = [sem(n) for n in
            ("head_copied", "rsc_mm", "rtr_mm", "scores_ready", "kdvt_ready", "ro_mm", "rst_mm", "rst_ready", "rvb_mm")]
        rdecayed, rstate_new, ros_mm, ro_copied, rss_mm, ro_step, rors_ready = [sem(n) for n in
            ("rdecayed", "rstate_new", "ros_mm", "ro_copied", "rss_mm", "ro_step", "rors_ready")]
        sconv_step, shist_in, shist_out, sy_ready, syhi = [sem(n, p) for n, p in
            (("sconv_step", SW), ("shist_in", 0), ("shist_out", 1), ("sy_ready", 0), ("syhi", 0))]
        phist_in, psum_step, phist_out, pmix_mm, py_ready, pyhi, pwin = [sem(n, p) for n, p in
            (("phist_in", 0), ("psum_step", 1), ("phist_out", 1), ("pmix_mm", BT), ("py_ready", 1), ("pyhi", 0),
             ("pwin", 0))]
        y_ready = [sem(f"y_ready{n}") for n in range(4)]
        ryhi, gyhi = sem("ryhi"), sem("gyhi")
        gsq_ready, gbc_ready, gn_mm, grow_mm, gvt_mm, grow_ready, grn_step, grn_act, gqk_ready, gcol_step, gcol_act = \
            [sem(n) for n in ("gsq_ready", "gbc_ready", "gn_mm", "grow_mm", "gvt_mm", "grow_ready", "grn_step",
                              "grn_act", "gqk_ready", "gcol_step", "gcol_act")]
        gkq_mm, gkt_mm, gE_ready, gattn_ready, gkd_ready, gem_ready, gR_ready, gT_mm, gT_ready, gX_mm, gX_ready, \
            gD_mm, gTR_ready = [sem(n) for n in ("gkq_mm", "gkt_mm", "gE_ready", "gattn_ready", "gkd_ready",
            "gem_ready", "gR_ready", "gT_mm", "gT_ready", "gX_mm", "gX_ready", "gD_mm", "gTR_ready")]
        gsol_mm, gvn_ready, gst_mm, gst_ready, gks_mm, grhs_ready, gqd_ready, go_mm, go_copied, gss_mm, go_step, \
            gors_ready = [sem(n) for n in ("gsol_mm", "gvn_ready", "gst_mm", "gst_ready", "gks_mm", "grhs_ready",
            "gqd_ready", "go_mm", "go_copied", "gss_mm", "go_step", "gors_ready")]
        gmk_ready, gdl_mm, gdecayed, gstate_new, gos_mm, gos_copied = [sem(n) for n in
            ("gmk_ready", "gdl_mm", "gdecayed", "gstate_new", "gos_mm", "gos_copied")]
        merged_ready = sem("merged_ready")
        mhi_ready, mlo_ready = sem("mhi_ready"), sem("mlo_ready")

        def col(table, at):
            return table[:, bass.ds(at, 1)]

        def tile_of(tiles, k):
            return tiles[:, k, :] if isinstance(k, int) else tiles[:, bass.ds(k, 1), :].rearrange("p a n -> p (a n)")

        def samples(tile, lead, taps, shift=0, width=1):
            body = tile[:, lead:lead + NS * taps].rearrange("p (b k) -> p b k", k=taps)
            return body[:, :, shift] if width == 1 else body[:, :, shift:shift + width]

        def settled(eng):
            eng.sem_inc(passed, 1)

        block = ctx.enter_context(nc.Block())

        @block.sync
        def _(sp):
            for s, n in primes:
                sp.sem_inc(s, n)
            sp.dma_start(par[:, :], params).then_inc(par_loaded, 16)
            for q in range(4):
                sp.dma_start(x[:, 4 * q:4 * q + 4, :], x_in[:, 4 * q:4 * q + 4, :]).then_inc(x_loaded[q], 16)
                if q == 0:
                    for s in range(RING):
                        sp.dma_start(raw[:, s, :], w_stream[s]).then_inc(raw_loaded[s], 16)
            sp.dma_start(con[:, :], consts).then_inc(con_loaded, 16)
            with sp.Fori(0, DEPTH * UNITS // RING) as r:
                u = sp.snap(r * RING)
                for s in range(RING):
                    sp.wait_ge(lo_ready, u + s + 1 + RING)
                    sp.dma_start(raw[:, s, :], w_stream[u + RING + s]).then_inc(raw_loaded[s], 16)
            for s in range(RING):
                sp.wait_ge(raw_loaded[s], (DEPTH * UNITS // RING + 1) * 16)

        @block.gpsimd
        def _(pool):
            gp = nc.gpsimd
            gp.memset(ab[:, :], 0.0).then_inc(zeros_set, 1)
            pool.wait_ge(par_loaded, 16)
            pool.wait_ge(con_loaded, 16)
            with pool.Fori(0, DEPTH) as l:
                gp.memset(gext[:, :, 0:GW - 1], 0.0)
                gp.memset(sext[:, 0:SW - 1], 0.0)
                gp.memset(pext[:, 0:PH], 0.0).then_inc(zeros_set, 1)
                pool.wait_ge(pmix_mm, l * BT + BT)
                settled(pool)
                pool.dma_start(plw[:, :, :], w_pool[l]).then_inc(plw_loaded, 16)
                pool.dma_start(phist[:, :], pool_in[l]).then_inc(ph_loaded, 16)
                with pool.Fori(0, BT) as h:
                    it = pool.snap(l * BT + h)
                    pool.wait_ge(ghist_out, it * 3 + 3)
                    settled(pool)
                    for j in range(3):
                        pool.wait_ge(gconv_step, it * (3 * GW) + GW * (j + 1))
                        settled(pool)
                        src = par[:, bass.ds(Q_GH + (it * 3 + j) * NS * (GW - 1), NS * (GW - 1))]
                        gp.tensor_copy(samples(gext[:, j, :], GW - 1 + T, GW, 0, GW - 1),
                                       src.rearrange("p (b k) -> p b k", k=GW - 1)).then_inc(ghist_in, 1)
                    for j in range(3):
                        pool.wait_ge(bank_free[j], l * BANK_USES + BK_G + h + 1 + BF)
                        pool.wait_ge(ghist_in, it * 3 + j + 1)
                        settled(pool)
                        at = H_G + (h * 3 + j) * (NS + 1) * (GW - 1)
                        gp.tensor_copy(hist[:, bass.ds(at, GW - 1)], gext[:, j, T:T + GW - 1])
                        gp.tensor_copy(hist[:, bass.ds(at + GW - 1, NS * (GW - 1))].rearrange("p (b k) -> p b k", k=GW - 1),
                                       samples(gext[:, j, :], GW - 1 + T, GW, 1, GW - 1)).then_inc(ghist_out, 1)
                with pool.Fori(0, BT) as h:
                    pool.wait_ge(unit_used, l * UNITS + RING + OFF_R)
                    pool.wait_ge(hlo_ready, l * 2 * BT + 2 * BT)
                    settled(pool)
                    gp.tensor_copy(act_lo[:, bass.ds(h * 4, 4), :], y_lo[:, bass.ds(h * 4, 4), :]).then_inc(alo_copied, 1)
                with pool.Fori(0, BT) as h:
                    it = pool.snap(l * BT + h)
                    pool.dma_start(state[:, :, :], ret_in[l, :, h].rearrange("b d e -> d b e")).then_inc(state_loaded, 16)
                    pool.wait_ge(sconv_step, it * SW + SW)
                    pool.wait_ge(shist_out, it + 1)
                    settled(pool)
                    src = par[:, bass.ds(Q_SH + it * NS * (SW - 1), NS * (SW - 1))]
                    gp.tensor_copy(samples(sext[:, :], SW - 1 + T, SW, 0, SW - 1),
                                   src.rearrange("p (b k) -> p b k", k=SW - 1)).then_inc(shist_in, 1)
                    pool.wait_ge(bank_free[1], l * BANK_USES + BK_S + h + 1 + BF)
                    pool.wait_ge(shist_in, it + 1)
                    settled(pool)
                    at = H_S + h * (NS + 1) * (SW - 1)
                    gp.tensor_copy(hist[:, bass.ds(at, SW - 1)], sext[:, T:T + SW - 1])
                    gp.tensor_copy(hist[:, bass.ds(at + SW - 1, NS * (SW - 1))].rearrange("p (b k) -> p b k", k=SW - 1),
                                   samples(sext[:, :], SW - 1 + T, SW, 1, SW - 1)).then_inc(shist_out, 1)
                    pool.wait_ge(rst_ready, it + 1)
                    settled(pool)
                    pool.dma_start(p_ret[l, 0, h], pstate[:, 0, :]).then_inc(pstate_written, 16)
                    pool.wait_ge(pstate_written, (it + l * BT) * 16 + 16)
                    pool.sem_inc(pstate_free, 1)
                    pool.wait_ge(rstate_new, it * NS + NS)
                    settled(pool)
                    pool.dma_start(s_ret[l, :, h].rearrange("b d e -> d b e"), state[:, :, :]).then_inc(state_written, 16)
                    pool.wait_ge(ros_mm, it + 1)
                    pool.wait_ge(state_written, (it + l * BT) * 16 + 16)
                    settled(pool)
                pool.wait_ge(ph_loaded, l * 16 + 16)
                settled(pool)
                for g in range(BT):
                    it = pool.snap(l * BT + g)
                    pool.wait_ge(psum_step, it + 1)
                    pool.wait_ge(phist_out, it + 1)
                    settled(pool)
                    src = phist[:, g * NS * PH:(g + 1) * NS * PH]
                    gp.tensor_copy(samples(pext[:, :], PH + T, PH + 1, 0, PH),
                                   src.rearrange("p (b k) -> p b k", k=PH)).then_inc(phist_in, 1)
                    pool.wait_ge(bank_free[2 * (g % 2)], l * BANK_USES + BK_P + g // 2 + 1 + BF)
                    pool.wait_ge(phist_in, it + 1)
                    settled(pool)
                    at = H_P + g * (NS + 1) * PH
                    gp.tensor_copy(hist[:, at:at + PH], pext[:, T:T + PH])
                    gp.tensor_copy(hist[:, at + PH:at + PH + NS * PH].rearrange("p (b k) -> p b k", k=PH),
                                   samples(pext[:, :], PH + T, PH + 1, 1, PH)).then_inc(phist_out, 1)
                pool.wait_ge(phist_out, l * BT + BT + 1)
                settled(pool)
                pool.dma_start(hist_out[l], hist[:, :]).then_inc(hist_written, 16)
                pool.wait_ge(hist_written, l * 16 + 16)
                settled(pool)
                with pool.Fori(0, BT) as h:
                    it = pool.snap(l * BT + h)
                    pool.dma_start(state[:, :, :], gdn_in[l, :, h].rearrange("b d e -> d b e")).then_inc(state_loaded, 16)
                    pool.wait_ge(gE_ready, it + 1)
                    settled(pool)
                    for v in range(1, LEVELS):
                        if v > 2:
                            pool.wait_ge(gX_mm, it * 6 + v - 2)
                            settled(pool)
                        for c in range(CH):
                            last = gp.tensor_tensor(Em[:, v % 2, c * P:(c + 1) * P], E_[:, c, :],
                                                    con[:, C_LEV + v * P:C_LEV + (v + 1) * P], ALU.mult)
                        last.then_inc(gem_ready, 1)
                    pool.wait_ge(gstate_new, it * NS + NS)
                    settled(pool)
                    pool.dma_start(s_gdn[l, :, h].rearrange("b d e -> d b e"), state[:, :, :]).then_inc(state_written, 16)
                    pool.wait_ge(gos_mm, it + 1)
                    pool.wait_ge(state_written, (it + l * BT) * 16 + 16 * BT + 16)
                    pool.wait_ge(gst_ready, it * 2 + 2)
                    settled(pool)
                    pool.dma_start(p_gdn[l, 0, h], pstate[:, 1, :]).then_inc(pstate_written, 16)
                    pool.wait_ge(pstate_written, (it + l * BT) * 16 + 16 * BT + 16)
                    pool.sem_inc(pstate_free, 1)
            for q in range(4):
                pool.wait_ge(h_ready, DEPTH * 2 * BT + q + 1)
                settled(pool)
                pool.dma_start(y_out[:, q * 4 * N:(q + 1) * 4 * N],
                               wide[:, 4 * q:4 * q + 4, :].rearrange("p a n -> p (a n)")).then_inc(out_written, 16)
            pool.wait_ge(out_written, 4 * 16)

        @block.scalar
        def _(act):
            sc = nc.scalar

            def splitter(l, off, i, per):
                ub = act.snap(l * UNITS + off + i * per)
                rb = act.snap((l * (UNITS // RING) + off // RING + i * (per // RING)) * 16)

                def split(a, b):
                    for j in range(a, b):
                        s = j % RING
                        act.wait_ge(raw_loaded[s], rb + 16 * (j // RING + 1))
                        act.wait_ge(unit_used, ub + j + 1)
                        sc.activation(whi[:, s, :], raw[:, s, :], ACT.Copy).then_inc(hi_ready, 1)
                return ub, split

            def x_tile(n, k, done):
                act.wait_ge(sq_added, done + 1 if isinstance(done, int) else act.snap(done + 1))
                sc.activation(squares[:, 0, :], tile_of(x, k), ACT.Square).then_inc(sq_ready, 1)
                sc.activation(tile_of(act_hi, k), tile_of(x, k), ACT.Copy, scale=col(par, Q_NG + n * KT + k)).then_inc(xhi_ready, 1)

            def inverse_rms(n):
                act.wait_ge(rms_ready, n + 1)
                sc.activation(rstd[:, :], rms[:, :], ACT.Sqrt).then_inc(rstd_ready, 1)

            act.wait_ge(par_loaded, 16)
            ub, split = splitter(0, 0, 0, 0)
            for k in range(KT):
                if k % 4 == 0:
                    act.wait_ge(x_loaded[k // 4], 16)
                x_tile(0, k, k)
                if k < 3:
                    split(k, k + 1)
            act.wait_ge(con_loaded, 16)
            with act.Fori(0, DEPTH) as l:
                def gdn_turn(h, first):
                    it = act.snap(l * BT + h)
                    ub, split = splitter(l, OFF_G, h, TURN)

                    def silu_out(j):
                        act.wait_ge(gconv_step, it * (3 * GW) + 3 * GW + GW * (j + 1))
                        at = (h * 3 + j) * N
                        sc.activation(gqkv[:, bass.ds(at, T)], gconv[:, j, 0:T], ACT.Silu)
                        sc.activation(gqkv[:, bass.ds(at + T, NS)], gconv[:, j, GW - 1 + T:GC:GW], ACT.Silu).then_inc(gqkv_ready, 1)

                    if first:
                        split(3, 6)
                        inverse_rms(l)
                        split(6, 7)
                    else:
                        split(3, 7)
                    for j in (1, 2):
                        split(4 * j + 3, 4 * j + 7)
                        silu_out(j - 1)
                    for a in range(2):
                        act.wait_ge(h_ready, it * 2 + a + 1)
                        sc.activation(y_hi[:, bass.ds(h * 4 + 2 * a, 2), :], wide[:, bass.ds(h * 4 + 2 * a, 2), :],
                                      ACT.Copy).then_inc(hhi_ready, 1)
                    split(15, 19)
                    silu_out(2)
                    act.wait_ge(bank_free[3], l * BANK_USES + BK_G + h + 1 + BF)
                    sc.activation(gates[:, bass.ds(h, 1), :], gates[:, bass.ds(h, 1), :], ACT.Silu).then_inc(gqkv_ready, 1)

                gdn_turn(0, True)
                with act.Fori(0, BT - 1) as r:
                    gdn_turn(act.snap(r + 1), False)

                with act.Fori(0, BT) as h:
                    ub, split = splitter(l, OFF_R, h, TURN)
                    split(3, 7)
                    act.wait_ge(unit_used, ub + RING)
                    sc.activation(act_hi[:, bass.ds(h * 4, 4), :], y_hi[:, bass.ds(h * 4, 4), :].bitcast(F32), ACT.Copy).then_inc(ahi_copied, 1)
                    split(7, 15)
                    act.wait_ge(unit_used, ub + RING + UB * 3)
                    sc.activation(rqkv[:, bass.ds((h * 3 + 2) * N, N)], acc[2][:, 0:N], ACT.Copy).then_inc(bank_free[2], 1)
                    split(15, 19)
                    act.wait_ge(unit_used, ub + RING + UB * 4)
                    sc.activation(wide[:, bass.ds(h + 3 * BT, 1), :], acc[3][:, 0:N], ACT.Silu).then_inc(bank_free[3], 1)

                with act.Fori(0, BT) as h:
                    it = act.snap(l * BT + h)
                    ub, split = splitter(l, OFF_S, h, TURN)
                    act.wait_ge(rope_step, it * 6 + 6)
                    act.wait_ge(bank_free[2], l * BANK_USES + BK_R + BT + BF)
                    sc.activation(head[:, :, :].rearrange("p a n -> p (a n)"), rqkv[:, bass.ds(h * 3 * N, 3 * N)],
                                  ACT.Copy).then_inc(head_copied, 1)
                    split(3, 7)
                    act.wait_ge(rtr_mm, it + 1)
                    for c in range(CH):
                        sc.activation(kd[:, c, :], side[1][:, c * P:(c + 1) * P], ACT.Copy, scale=col(con, C_GDEC + h * CH + c))
                    sc.activation(vt[:, :, :].rearrange("p c d -> p (c d)"), side[1][:, T:2 * T], ACT.Copy).then_inc(kdvt_ready, 1)
                    act.wait_ge(unit_used, ub + RING + UB)
                    sc.activation(sc_c[:, :], acc[0][:, 0:N], ACT.Copy).then_inc(bank_free[0], 1)
                    split(7, 9)
                    act.wait_ge(state_loaded, (it + l * BT) * 16 + 16)
                    sc.activation(state[:, :, :].rearrange("p b e -> p (b e)"), state[:, :, :].rearrange("p b e -> p (b e)"),
                                  ACT.Copy, scale=col(con, C_GAM + h)).then_inc(rdecayed, 1)
                    split(9, 15)
                    act.wait_ge(ros_mm, it + 1)
                    sc.activation(osb[:, :], side[2][:, 0:N], ACT.Copy)
                    sc.activation(osq[:, :], side[2][:, 0:N], ACT.Square).then_inc(ro_copied, 1)
                    split(15, 18)
                    act.wait_ge(ro_step, it * 4 + 2)
                    sc.activation(oms[:, :], orc[:, :], ACT.Sqrt).then_inc(rors_ready, 1)
                    split(18, 19)
                    act.wait_ge(unit_used, ub + RING + UB * 4)
                    sc.activation(sgate[:, :], acc[3][:, 0:N], ACT.Silu).then_inc(bank_free[3], 1)
                    act.wait_ge(ro_step, it * 4 + 4)
                    sc.activation(y_hi[:, bass.ds(h + YT[RET], 1), :], y32[:, 0, :], ACT.Copy).then_inc(ryhi, 1)
                    act.wait_ge(sy_ready, it + 1)
                    sc.activation(y_hi[:, bass.ds(h + YT[SCV], 1), :], y32[:, 1, :], ACT.Copy).then_inc(syhi, 1)

                act.wait_ge(ab_step, l * 15 + 1)
                sc.activation(ab_abs[:, :], ab_x[:, :], ACT.Abs).then_inc(ab_act, 1)
                act.wait_ge(ab_act, l * 4 + 1)
                sc.activation(ab_e[:, :], ab_abs[:, :], ACT.Exp, scale=-1.0).then_inc(ab_act, 1)
                sc.activation(ab_ea[:, :], par[:, bass.ds(Q_AL + l * A3, A3)], ACT.Exp).then_inc(ab_act, 1)
                sc.activation(beta[:, :].rearrange("p (c h) -> p c h", h=BT),
                              ab[:, :].rearrange("p (c t h) -> p c t h", t=2, h=BT)[:, :, 1, :],
                              ACT.Sigmoid).then_inc(ab_act, 1)

                for g in range(BT):
                    it = l * BT + g
                    ub, split = splitter(l, OFF_P, g, PTURN)
                    b0 = 2 * (g % 2)
                    split(3, 7)
                    act.wait_ge(unit_used, ub + RING + UB)
                    act.wait_ge(phist_out, it + 1)
                    act.wait_ge(psum_step, it + 1)
                    sc.activation(pext[:, PH:PH + T], acc[b0][:, 0:T], ACT.Copy)
                    sc.activation(samples(pext[:, :], PH + T, PH + 1, PH), acc[b0][:, T:N], ACT.Copy).then_inc(bank_free[b0], 1)
                    split(7, 11)
                    act.wait_ge(unit_used, ub + RING + UB * 2)
                    act.wait_ge(py_ready, it + 1)
                    sc.activation(pgate[:, :], acc[b0 + 1][:, 0:N], ACT.Silu).then_inc(bank_free[b0 + 1], 1)
                    act.wait_ge(py_ready, it + 2)
                    sc.activation(y_hi[:, YT[POOL] + g, :], y32[:, 1, :], ACT.Copy).then_inc(pyhi, 1)

                act.wait_ge(phist_out, l * BT + BT + 1)
                settled(act)
                with act.Fori(0, BT) as h:
                    it = act.snap(l * BT + h)
                    ub, split = splitter(l, OFF_M, h, MTURN)
                    mb = act.snap(l * 4 * KT + h * 12)
                    fb = act.snap(l * BANK_USES + BK_M + h * 6)

                    def units(a, b):
                        for j in range(a, b):
                            split(j + 3, j + 4)
                            if j % MB == MB - 1:
                                i = j // MB
                                p = i % 2
                                act.wait_ge(unit_used, ub + RING + MB * i + UB)
                                act.wait_ge(bank_free[2 * p + 1], fb + i // 2 + BF)
                                sc.activation(msig[:, p, :], acc[2 * p][:, 0:N], ACT.Sigmoid).then_inc(bank_free[2 * p], 1)

                    act.wait_ge(gqkv_ready, l * 4 * BT + 4 * BT)
                    sc.activation(sq2[:, :, :].rearrange("p a n -> p (a n)"), gqkv[:, bass.ds(h * 3 * N, 2 * N)], ACT.Square).then_inc(gsq_ready, 1)
                    sc.activation(head[:, 2, :], gqkv[:, bass.ds((h * 3 + 2) * N, N)], ACT.Copy).then_inc(gsq_ready, 1)
                    units(0, 3)
                    act.wait_ge(grow_mm, it + 1)
                    sc.activation(b_row[:, :], side[2][:, 0:BR], ACT.Copy).then_inc(grow_ready, 1)
                    sc.activation(eb_row[:, 0:N], side[2][:, 0:N], ACT.Exp).then_inc(grow_ready, 1)
                    act.wait_ge(gvt_mm, it + 1)
                    sc.activation(vt[:, :, :].rearrange("p c d -> p (c d)"), side[3][:, 0:T], ACT.Copy).then_inc(kdvt_ready, 1)
                    act.wait_ge(gcol_step, it * 3 + 2)
                    sc.activation(hcol[:, 2:4], hcol[:, 0:2], ACT.Exp)
                    sc.activation(hcol[:, 6:8], hcol[:, 4:6], ACT.Exp).then_inc(gcol_act, 1)
                    sc.activation(dec[:, :, :].rearrange("p c d -> p (c d)"), dec[:, :, :].rearrange("p c d -> p (c d)"),
                                  ACT.Exp).then_inc(gcol_act, 1)
                    act.wait_ge(grn_step, it * 2 + 2)
                    sc.activation(rn2[:, :, :].rearrange("p a n -> p (a n)"), rq2[:, :, :].rearrange("p a n -> p (a n)"),
                                  ACT.Sqrt).then_inc(grn_act, 1)
                    units(3, 11)
                    act.wait_ge(gkt_mm, it + 1)
                    act.wait_ge(gcol_act, it * 2 + 1)
                    for c in range(CH):
                        last = sc.activation(kd[:, c, :], side[1][:, c * P:(c + 1) * P], ACT.Copy, scale=hcol[:, 6 + c:7 + c])
                    last.then_inc(gkd_ready, 1)
                    units(11, 14)
                    act.wait_ge(gT_mm, it + 1)
                    sc.activation(TR[:, 0, :, :].rearrange("p c d -> p (c d)"), side[0][:, 0:T], ACT.Copy).then_inc(gT_ready, 1)
                    units(14, LEV0)
                    at = LEV0
                    for v in range(1, LEVELS):
                        act.wait_ge(gX_mm, it * 6 + v)
                        sc.activation(Xs[:, :, :].rearrange("p c d -> p (c d)"), side[0][:, 0:T], ACT.Copy).then_inc(gX_ready, 1)
                        if v in (2, 4):
                            act.wait_ge(grow_ready, it * 2 + 2)
                            act.wait_ge(gdl_mm, it * 2 + v // 2)
                            for b in range(2 * v - 4, 2 * v):
                                last = sc.activation(state[:, b, :], state[:, b, :], ACT.Copy, scale=eb_row[:, T + b:T + b + 1])
                            last.then_inc(gdecayed, 1)
                        if v == 6:
                            act.wait_ge(gos_mm, it + 1)
                            sc.activation(osb[:, T:N], side[3][:, 0:NS], ACT.Copy).then_inc(gos_copied, 1)
                        units(at, at + LEVU)
                        at += LEVU
                    act.wait_ge(gsol_mm, it * 2 + 1)
                    sc.activation(vn[:, 0, :], side[2][:, 0:P], ACT.Copy, scale=bet2[:, 0:1]).then_inc(gvn_ready, 1)
                    units(at, 49)
                    act.wait_ge(gsol_mm, it * 2 + 2)
                    sc.activation(vn[:, 1, :], side[2][:, 0:P], ACT.Copy, scale=bet2[:, 1:2]).then_inc(gvn_ready, 1)
                    units(49, 52)
                    act.wait_ge(go_mm, it + 1)
                    sc.activation(osb[:, 0:T], side[0][:, 0:T], ACT.Copy).then_inc(go_copied, 1)
                    act.wait_ge(go_copied, it * 2 + 1)
                    sc.activation(osq[:, :], osb[:, :], ACT.Square).then_inc(go_copied, 1)
                    units(52, 57)
                    act.wait_ge(go_step, it * 4 + 2)
                    sc.activation(oms[:, :], orc[:, :], ACT.Sqrt).then_inc(gors_ready, 1)
                    units(57, 60)
                    act.wait_ge(go_step, it * 4 + 4)
                    sc.activation(y_hi[:, bass.ds(h + YT[GDN], 1), :], y32[:, 0, :], ACT.Copy).then_inc(gyhi, 1)

                def merged_hi(k):
                    act.wait_ge(merged_ready, l * 3 * KT + 2 * KT + k + 1)
                    sc.activation(tile_of(y_hi, k), tile_of(wide, k), ACT.Copy).then_inc(mhi_ready, 1)

                def gdn_merge_turn(h, last):
                    ub, split = splitter(l, OFF_X, h, XTURN)
                    fb = act.snap(l * BANK_USES + BK_X + h * 2)
                    for i in range(4):
                        p = i % 2
                        split(MB * i + 3, MB * i + 8)
                        act.wait_ge(unit_used, ub + RING + MB * i + UB)
                        act.wait_ge(bank_free[2 * p + 1], fb + i // 2 + BF)
                        sc.activation(msig[:, p, :], acc[2 * p][:, 0:N], ACT.Sigmoid).then_inc(bank_free[2 * p], 1)
                        if not last:
                            merged_hi(act.snap(h * 4 + i))

                with act.Fori(0, BT - 1) as h:
                    gdn_merge_turn(h, False)
                gdn_merge_turn(BT - 1, True)
                act.wait_ge(unit_used, l * UNITS + RING + OFF_O)
                for k in range(KT - 4, KT):
                    merged_hi(k)

                with act.Fori(0, BT) as h:
                    ub, split = splitter(l, OFF_O, h, TURN)
                    for i in range(4):
                        split(4 * i + 3, 4 * i + 7)
                        k = act.snap(h * 4 + i)
                        act.wait_ge(x_updated, l * KT + h * 4 + i + 1)
                        x_tile(l + 1, k, (l + 1) * KT + h * 4 + i)
            inverse_rms(DEPTH)

        @block.vector
        def _(dve):
            ve = nc.vector

            def splitter(l, off, i, per):
                ub = dve.snap(l * UNITS + off + i * per)

                def split(a, b):
                    for j in range(a, b):
                        s = j % RING
                        dve.wait_ge(hi_ready, ub + j + 1)
                        ve.tensor_tensor(wlo[:, s, :], raw[:, s, :], whi[:, s, :].bitcast(F32), ALU.subtract).then_inc(lo_ready, 1)
                return ub, split

            def x_added(done):
                dve.wait_ge(sq_ready, done + 1)
                dve.wait_ge(sq_added, done + 1)
                return ve.tensor_tensor(sq_sum[:, :], sq_sum[:, :], squares[:, 0, :], ALU.add).then_inc(sq_added, 1)

            def x_lo(n, k, done):
                dve.wait_ge(xhi_ready, done + 1)
                ve.scalar_tensor_tensor(out=tile_of(act_lo, k), in0=tile_of(x, k), scalar=col(par, Q_NG + n * KT + k),
                                        in1=tile_of(act_hi, k).bitcast(F32), op0=ALU.mult, op1=ALU.subtract).then_inc(xlo_ready, 1)

            def mean_square(n):
                dve.wait_ge(norm_mm, n + 1)
                ve.tensor_scalar(ms[:, :], side[0][:, 0:N], 1.0 / D_MODEL, EPS, ALU.mult, ALU.add).then_inc(ms_ready, 1)
                dve.wait_ge(ms_ready, n + 1)
                ve.reciprocal(rms[:, :], ms[:, :]).then_inc(rms_ready, 1)

            def normed(n, k):
                return ve.scalar_tensor_tensor(out=tile_of(wide, k), in0=tile_of(x, k), scalar=col(par, Q_NG + n * KT + k),
                                               in1=rstd[:, :], op0=ALU.mult, op1=ALU.mult)

            ve.memset(sq_sum[:, :], 0.0).then_inc(sum_cleared, 1)
            dve.wait_ge(sum_cleared, 1)
            dve.wait_ge(par_loaded, 16)
            ub, split = splitter(0, 0, 0, 0)
            for k in range(KT):
                if k % 4 == 0:
                    dve.wait_ge(x_loaded[k // 4], 16)
                x_added(k)
                x_lo(0, k, k)
                if k < 3:
                    split(k, k + 1)
            dve.wait_ge(con_loaded, 16)
            with dve.Fori(0, DEPTH) as l:
                def gdn_turn(h, first):
                    it = dve.snap(l * BT + h)
                    ub, split = splitter(l, OFF_G, h, TURN)
                    split(3, 5)
                    if first:
                        mean_square(l)
                    split(5, 7)
                    if first:
                        dve.wait_ge(zeros_set, l + 2)
                        dve.wait_ge(rstd_ready, l + 1)
                    for j in range(3):
                        dve.wait_ge(unit_used, ub + RING + UB * (j + 1))
                        dve.wait_ge(ghist_out, it * 3 + j + 1)
                        ve.tensor_tensor(gext[:, j, GW - 1:GW - 1 + T], acc[j][:, 0:T], rstd[:, 0:T], ALU.mult)
                        ve.tensor_tensor(samples(gext[:, j, :], GW - 1 + T, GW, GW - 1), acc[j][:, T:N], rstd[:, T:N],
                                         ALU.mult).then_inc(bank_free[j], 1)
                        split(7 + 4 * j, 8 + 4 * j)
                        dve.wait_ge(bank_free[j], l * BANK_USES + BK_G + h + 1 + BF)
                        dve.wait_ge(ghist_in, it * 3 + j + 1)
                        tap = Q_GCW + (it * 3 + j) * GW
                        ve.tensor_scalar(gconv[:, j, :], gext[:, j, 0:GC], col(par, tap), None, ALU.mult).then_inc(gconv_step, 1)
                        for k in range(1, GW):
                            dve.wait_ge(gconv_step, it * (3 * GW) + 3 * GW + GW * j + k)
                            ve.scalar_tensor_tensor(out=gconv[:, j, :], in0=gext[:, j, k:k + GC], scalar=col(par, tap + k),
                                                    in1=gconv[:, j, :], op0=ALU.mult, op1=ALU.add).then_inc(gconv_step, 1)
                            split(7 + 4 * j + k, 8 + 4 * j + k)
                        if j < 2:
                            normed(l, dve.snap(h * 4 + 2 * j))
                            normed(l, dve.snap(h * 4 + 2 * j + 1)).then_inc(h_ready, 1)
                    for a in range(2):
                        dve.wait_ge(hhi_ready, it * 2 + a + 1)
                        ve.tensor_tensor(y_lo[:, bass.ds(h * 4 + 2 * a, 2), :], wide[:, bass.ds(h * 4 + 2 * a, 2), :],
                                         y_hi[:, bass.ds(h * 4 + 2 * a, 2), :].bitcast(F32), ALU.subtract).then_inc(hlo_ready, 1)
                    dve.wait_ge(unit_used, ub + RING + UB * 4)
                    ve.tensor_tensor(tile_of(gates, h), acc[3][:, 0:N], rstd[:, :], ALU.mult).then_inc(bank_free[3], 1)

                gdn_turn(0, True)
                with dve.Fori(0, BT - 1) as r:
                    gdn_turn(dve.snap(r + 1), False)

                def rotate(out, a, table, scale):
                    return ve.scalar_tensor_tensor(out=out, in0=a, scalar=scale, in1=table, op0=ALU.mult, op1=ALU.mult)

                dve.wait_ge(ab_mm, l * 3 + 3)
                dve.wait_ge(zeros_set, 1)
                settled(dve)
                ve.tensor_copy(ab[:, 0:4 * BT], side[1][:, 0:4 * BT])
                ve.tensor_copy(ab[0:NS, 4 * BT:6 * BT], side[1][0:NS, 4 * BT:6 * BT]).then_inc(ab_evac, 1)

                with dve.Fori(0, BT) as h:
                    it = dve.snap(l * BT + h)
                    ub, split = splitter(l, OFF_R, h, TURN)
                    split(3, 7)
                    for j, scale in enumerate((1.0, float(P) ** -0.5)):
                        dve.wait_ge(unit_used, ub + RING + UB * (j + 1))
                        rotate(rope_a[:, j, :], acc[j][:, 0:N], con[:, C_COS:C_COS + N], scale).then_inc(rope_step, 1)
                        rotate(rope_b[0:64, j, :], acc[j][64:P, 0:N], con[64:P, C_SIN:C_SIN + N], scale).then_inc(rope_step, 1)
                        rotate(rope_b[64:P, j, :], acc[j][0:64, 0:N], con[0:64, C_SIN:C_SIN + N], scale).then_inc(bank_free[j], 1)
                        dve.wait_ge(bank_free[j], l * BANK_USES + BK_R + h + 1 + BF)
                        ve.tensor_tensor(rqkv[:, bass.ds((h * 3 + j) * N, N)], rope_a[:, j, :], rope_b[:, j, :], ALU.add).then_inc(rope_step, 1)
                        split(7 + 4 * j, 11 + 4 * j)
                    split(15, 19)

                with dve.Fori(0, BT) as h:
                    it = dve.snap(l * BT + h)
                    ub, split = splitter(l, OFF_S, h, TURN)
                    split(3, 6)
                    dve.wait_ge(rsc_mm, it + 1)
                    ve.tensor_tensor(scores[:, 0:T], side[0][:, 0:T], con[:, bass.ds(C_DM + h * T, T)], ALU.mult)
                    ve.tensor_tensor(scores[:, T:T + P], side[0][:, T:T + P], con[:, bass.ds(C_DM + h * T, P)], ALU.mult).then_inc(scores_ready, 1)
                    split(6, 9)
                    dve.wait_ge(rst_mm, it + 1)
                    dve.wait_ge(pstate_free, it + l * BT + 1)
                    ve.tensor_copy(pstate[:, 0, :], side[3][:, 0:P]).then_inc(rst_ready, 1)
                    split(9, 11)
                    dve.wait_ge(unit_used, ub + RING + UB * 2)
                    dve.wait_ge(bank_free[0], l * BANK_USES + BK_S + h + 1 + BF)
                    dve.wait_ge(shist_out, it + 1)
                    ve.tensor_tensor(sext[:, SW - 1:SW - 1 + T], acc[1][:, 0:T], sc_c[:, 0:T], ALU.mult)
                    ve.tensor_tensor(samples(sext[:, :], SW - 1 + T, SW, SW - 1), acc[1][:, T:N], sc_c[:, T:N], ALU.mult).then_inc(bank_free[1], 1)
                    dve.wait_ge(rvb_mm, it + 1)
                    dve.wait_ge(rdecayed, it + 1)
                    for b in range(NS):
                        ve.scalar_tensor_tensor(out=state[:, b, :], in0=side[b // 4][:, (b % 4) * P:(b % 4 + 1) * P],
                                                scalar=head[:, 1, T + b:T + b + 1], in1=state[:, b, :],
                                                op0=ALU.mult, op1=ALU.add).then_inc(rstate_new, 1)
                    split(11, 13)
                    dve.wait_ge(bank_free[1], l * BANK_USES + BK_S + h + 1 + BF)
                    dve.wait_ge(shist_in, it + 1)
                    tap = Q_SCW + it * SW
                    ve.tensor_scalar(sconv[:, :], sext[:, 0:SC], col(par, tap), None, ALU.mult).then_inc(sconv_step, 1)
                    for k in range(1, SW):
                        dve.wait_ge(sconv_step, it * SW + SW + k)
                        ve.scalar_tensor_tensor(out=sconv[:, :], in0=sext[:, k:k + SC], scalar=col(par, tap + k),
                                                in1=sconv[:, :], op0=ALU.mult, op1=ALU.add).then_inc(sconv_step, 1)
                    split(13, 17)
                    dve.wait_ge(rss_mm, it + 1)
                    ve.tensor_scalar(oms[:, :], side[3][:, 0:N], 1.0 / P, EPS, ALU.mult, ALU.add).then_inc(ro_step, 1)
                    dve.wait_ge(ro_step, it * 4 + 1)
                    ve.reciprocal(orc[:, :], oms[:, :]).then_inc(ro_step, 1)
                    dve.wait_ge(sconv_step, it * SW + 2 * SW)
                    dve.wait_ge(unit_used, ub + RING + UB * 3)
                    ve.tensor_tensor(sprod[:, 0:T], acc[2][:, 0:T], sconv[:, 0:T], ALU.mult)
                    ve.tensor_tensor(sprod[:, T:N], acc[2][:, T:N], sconv[:, SW - 1 + T:SC:SW], ALU.mult).then_inc(bank_free[2], 1)
                    split(17, 19)
                    dve.wait_ge(rors_ready, it + 1)
                    ve.tensor_tensor(orc[:, :], osb[:, :], oms[:, :], ALU.mult).then_inc(ro_step, 1)
                    dve.wait_ge(ro_step, it * 4 + 3)
                    ve.tensor_tensor(y32[:, 0, :], orc[:, :], wide[:, bass.ds(h + 3 * BT, 1), :].rearrange("p a n -> p (a n)"),
                                     ALU.mult).then_inc(ro_step, 1)
                    dve.wait_ge(bank_free[3], l * BANK_USES + BK_S + h + 1 + BF)
                    dve.wait_ge(bank_free[2], l * BANK_USES + BK_S + h + 1 + BF)
                    ve.tensor_tensor(y32[:, 1, :], sprod[:, :], sgate[:, :], ALU.mult).then_inc(sy_ready, 1)
                    dve.wait_ge(ryhi, it + 1)
                    ve.tensor_tensor(y_lo[:, bass.ds(h + YT[RET], 1), :], y32[:, 0, :],
                                     y_hi[:, bass.ds(h + YT[RET], 1), :].bitcast(F32), ALU.subtract).then_inc(y_ready[RET], 1)
                    dve.wait_ge(syhi, it + 1)
                    ve.tensor_tensor(y_lo[:, bass.ds(h + YT[SCV], 1), :], y32[:, 1, :],
                                     y_hi[:, bass.ds(h + YT[SCV], 1), :].bitcast(F32), ALU.subtract).then_inc(y_ready[SCV], 1)

                nth = [0]

                def link(op):
                    nth[0] += 1
                    op.then_inc(ab_step, 1)
                    dve.wait_ge(ab_step, l * 15 + nth[0])

                link(ve.tensor_tensor(ab_x[:, :].rearrange("p (c h) -> p c h", h=BT),
                                      ab[:, :].rearrange("p (c t h) -> p c t h", t=2, h=BT)[:, :, 0, :],
                                      par[:, bass.ds(Q_DT + l * A3, A3)].rearrange("p (c h) -> p c h", h=BT), ALU.add))
                ve.tensor_scalar(ab_relu[:, :], ab_x[:, :], 0.0, None, ALU.max)
                dve.wait_ge(ab_act, l * 4 + 2)
                link(ve.tensor_scalar(ab_den[:, :], ab_e[:, :], 2.0, None, ALU.add))
                link(ve.reciprocal(ab_rec[:, :], ab_den[:, :]))
                link(ve.tensor_tensor(ab_s[:, :], ab_e[:, :], ab_rec[:, :], ALU.mult))
                link(ve.tensor_tensor(ab_s2[:, :], ab_s[:, :], ab_s[:, :], ALU.mult))
                link(ve.tensor_scalar(ab_q[:, :], ab_s2[:, :], 1.0 / 15, None, ALU.mult))
                for d in (13, 11, 9, 7, 5, 3):
                    link(ve.scalar_tensor_tensor(out=ab_q[:, :], in0=ab_q[:, :], scalar=1.0 / d, in1=ab_s2[:, :],
                                                 op0=ALU.add, op1=ALU.mult))
                link(ve.scalar_tensor_tensor(out=ab_q[:, :], in0=ab_q[:, :], scalar=1.0, in1=ab_s[:, :],
                                             op0=ALU.add, op1=ALU.mult))
                link(ve.scalar_tensor_tensor(out=ab_sp[:, :], in0=ab_q[:, :], scalar=2.0, in1=ab_relu[:, :],
                                             op0=ALU.mult, op1=ALU.add))
                dve.wait_ge(ab_act, l * 4 + 4)
                link(ve.scalar_tensor_tensor(out=g_col[:, :], in0=ab_sp[:, :], scalar=-1.0, in1=ab_ea[:, :],
                                             op0=ALU.mult, op1=ALU.mult))
                assert nth[0] == 15

                for g in range(BT):
                    it = l * BT + g
                    ub, split = splitter(l, OFF_P, g, PTURN)
                    split(3, 7)
                    dve.wait_ge(bank_free[2 * (g % 2)], l * BANK_USES + BK_P + g // 2 + 1 + BF)
                    dve.wait_ge(phist_in, it + 1)
                    src, w, steps = pext, 1, 0
                    for v in range(g + 1):
                        dst = (psum_a, psum_b)[v % 2]
                        lo = 2 * w - 1
                        ve.tensor_tensor(dst[:, lo:PE_], src[:, lo:PE_], src[:, lo - w:PE_ - w], ALU.add).then_inc(pwin, 1)
                        steps += 1
                        dve.wait_ge(pwin, l * PWIN + PWIN_AT[g] + steps)
                        src, w = dst, 2 * w
                    ve.tensor_tensor(src[:, PH:PH + 16], src[:, PH:PH + 16], con[:, C_CORR + 16 * g:C_CORR + 16 * g + 16],
                                     ALU.mult).then_inc(pwin, 1)
                    dve.wait_ge(pwin, l * PWIN + PWIN_AT[g] + steps + 1)
                    ve.scalar_tensor_tensor(out=pdiff[:, 0:T], in0=src[:, PH:PH + T], scalar=1.0 / w, in1=pext[:, PH:PH + T],
                                            op0=ALU.mult, op1=ALU.subtract)
                    ve.scalar_tensor_tensor(out=pdiff[:, T:N], in0=samples(src[:, :], PH + T, PH + 1, PH), scalar=1.0 / w,
                                            in1=samples(pext[:, :], PH + T, PH + 1, PH),
                                            op0=ALU.mult, op1=ALU.subtract).then_inc(psum_step, 1)
                    split(7, 11)
                    dve.wait_ge(pmix_mm, it + 1 + BT)
                    dve.wait_ge(bank_free[2 * (g % 2) + 1], l * BANK_USES + BK_P + g // 2 + 1 + BF)
                    ve.scalar_tensor_tensor(out=y32[:, 1, :], in0=side[0][:, 0:N], scalar=col(par, Q_PSC + it), in1=pgate[:, :],
                                            op0=ALU.mult, op1=ALU.mult).then_inc(py_ready, 1)
                    dve.wait_ge(pyhi, it + 1)
                    ve.tensor_tensor(y_lo[:, YT[POOL] + g, :], y32[:, 1, :], y_hi[:, YT[POOL] + g, :].bitcast(F32),
                                     ALU.subtract).then_inc(y_ready[POOL], 1)

                dve.wait_ge(bcol_mm, l + 1)
                ve.tensor_copy(b_col[:, :], side[1][:, 0:CH * BT]).then_inc(bcol_ready, 1)
                dve.wait_ge(bcol_ready, l + 1)

                def merge_block(ub, i, p, first, m):
                    dve.wait_ge(unit_used, ub + RING + MB * (i + 1))
                    dve.wait_ge(bank_free[2 * p], bank_now[0] + i // 2 + 1 + BF)
                    dst = wide[:, bass.ds(m, 1), :]
                    if first:
                        ve.tensor_tensor(dst, msig[:, p, :], acc[2 * p + 1][:, 0:N], ALU.mult).then_inc(bank_free[2 * p + 1], 1)
                    else:
                        ve.tensor_tensor(mprod[:, p, :], msig[:, p, :], acc[2 * p + 1][:, 0:N], ALU.mult).then_inc(bank_free[2 * p + 1], 1)
                        dve.wait_ge(bank_free[2 * p + 1], bank_now[0] + i // 2 + 1 + BF)
                        ve.tensor_tensor(dst, dst, mprod[:, p, :], ALU.add).then_inc(merged_ready, 1)

                bank_now = [None]

                dve.wait_ge(phist_out, l * BT + BT + 1)
                settled(dve)
                with dve.Fori(0, BT) as h:
                    it = dve.snap(l * BT + h)
                    ub, split = splitter(l, OFF_M, h, MTURN)
                    bank_now[0] = dve.snap(l * BANK_USES + BK_M + h * 6)

                    def units(a, b):
                        for j in range(a, b):
                            split(j + 3, j + 4)
                            if j % MB == MB - 1:
                                i = j // MB
                                merge_block(ub, i, i % 2, i % 3 == 0, h * 4 + i // 3)

                    for c in range(3):
                        ve.tensor_copy(g_bc[:, c, :], col(g_col, h + c * BT).to_broadcast([P, P]))
                    ve.tensor_copy(beta_bc[:, :], col(beta, h + 2 * BT).to_broadcast([P, P]))
                    for c in range(CH):
                        ve.tensor_copy(hcol[:, c:c + 1], col(b_col, h + c * BT))
                        last = ve.tensor_copy(bet2[:, c:c + 1], col(beta, h + c * BT))
                    last.then_inc(gbc_ready, 1)
                    units(0, 3)
                    dve.wait_ge(gn_mm, it + 1)
                    for a in range(2):
                        last = ve.tensor_scalar(rn2[:, a, :], side[a][:, 0:N], EPS, None, ALU.add)
                    last.then_inc(grn_step, 1)
                    dve.wait_ge(grow_ready, it * 2 + 1)
                    dve.wait_ge(gbc_ready, it + 1)
                    for c in range(CH):
                        ve.scalar_tensor_tensor(out=dec[:, c, :], in0=b_row[:, c * P:(c + 1) * P], scalar=hcol[:, c:c + 1], in1=neg,
                                                op0=ALU.subtract, op1=ALU.add)
                    for c in range(CH):
                        ve.tensor_tensor(hcol[:, 4 + c:5 + c], b_row[:, c * P + P - 1:c * P + P], hcol[:, c:c + 1],
                                         ALU.subtract).then_inc(gcol_step, 1)
                    dve.wait_ge(grn_step, it * 2 + 1)
                    ve.reciprocal(rq2[:, :, :], rn2[:, :, :]).then_inc(grn_step, 1)
                    units(3, 6)
                    dve.wait_ge(grn_act, it + 1)
                    ve.scalar_tensor_tensor(out=head[:, 0, :], in0=gqkv[:, bass.ds(h * 3 * N, N)], scalar=float(P) ** -0.5,
                                            in1=rn2[:, 0, :], op0=ALU.mult, op1=ALU.mult)
                    ve.tensor_tensor(head[:, 1, :], gqkv[:, bass.ds(h * 3 * N + N, N)], rn2[:, 1, :], ALU.mult).then_inc(gqk_ready, 1)
                    dve.wait_ge(gcol_act, it * 2 + 1)
                    ve.tensor_scalar(nebc[:, :], hcol[:, 2:4], -1.0, None, ALU.mult)
                    dve.wait_ge(gcol_act, it * 2 + 2)
                    ve.tensor_tensor(decs[:, 0, :], dec[:, 0, :], strict, ALU.mult)
                    ve.tensor_tensor(decs[:, 1, :], dec[:, 1, :], strict, ALU.mult).then_inc(gcol_step, 1)
                    dve.wait_ge(gqk_ready, it + 1)
                    dve.wait_ge(grow_ready, it * 2 + 2)
                    ve.scalar_tensor_tensor(out=mk[:, :], in0=head[:, 1, T:N], scalar=-1.0, in1=eb_row[:, T:N],
                                            op0=ALU.mult, op1=ALU.mult)
                    ve.tensor_tensor(kb[:, :], b_row[:, N:BR], head[:, 1, T:N], ALU.mult)
                    ve.tensor_tensor(qd[:, :], head[:, 0, P:T], eb_row[:, P:T], ALU.mult).then_inc(gqd_ready, 1)
                    units(6, 11)
                    dve.wait_ge(gkq_mm, it + 1)
                    dve.wait_ge(gcol_step, it * 3 + 3)
                    for c in range(CH):
                        last = ve.scalar_tensor_tensor(out=E_[:, c, :], in0=side[0][:, c * P:(c + 1) * P], scalar=bet2[:, c:c + 1],
                                                       in1=decs[:, c, :], op0=ALU.mult, op1=ALU.mult)
                    last.then_inc(gE_ready, 1)
                    ve.tensor_tensor(attn[:, :, :].rearrange("p c d -> p (c d)"), side[0][:, T:2 * T],
                                     dec[:, :, :].rearrange("p c d -> p (c d)"), ALU.mult).then_inc(gattn_ready, 1)
                    dve.wait_ge(gE_ready, it + 1)
                    for c in range(CH):
                        last = ve.tensor_tensor(Xs[:, c, :], E_[:, c, :], con[:, C_LEV:C_LEV + P], ALU.mult)
                    last.then_inc(gR_ready, 1)
                    dve.wait_ge(gR_ready, it * 2 + 1)
                    for c in range(CH):
                        last = ve.tensor_tensor(TR[:, 1, c, :], ident, Xs[:, c, :], ALU.subtract)
                    last.then_inc(gR_ready, 1)
                    units(11, LEV0)
                    at = LEV0
                    for v in range(1, LEVELS):
                        if v in (3, 5):
                            dve.wait_ge(gdecayed, it * 2 + v // 2)
                            for b in range(2 * v - 6, 2 * v - 2):
                                ve.scalar_tensor_tensor(out=state[:, b, :], in0=side[3][:, (b % 4) * P:(b % 4 + 1) * P],
                                                        scalar=kb[:, b:b + 1], in1=state[:, b, :],
                                                        op0=ALU.mult, op1=ALU.add).then_inc(gstate_new, 1)
                        units(at, at + 2)
                        dve.wait_ge(gD_mm, it * 6 + v)
                        flat = TR[:, :, :, :].rearrange("p t c d -> p (t c d)")
                        if v < LEVELS - 1:
                            ve.tensor_tensor(flat, flat, side[1][:, :], ALU.subtract).then_inc(gTR_ready, 1)
                        else:
                            ve.tensor_tensor(flat[:, T:2 * T], flat[:, T:2 * T], side[1][:, T:2 * T], ALU.subtract).then_inc(gTR_ready, 1)
                        units(at + 2, at + LEVU)
                        at += LEVU
                    units(at, 45)
                    dve.wait_ge(gst_mm, it * 2 + 1)
                    dve.wait_ge(pstate_free, it + l * BT + BT + 1)
                    ve.tensor_copy(pstate[:, 1, :], side[3][:, 0:P]).then_inc(gst_ready, 1)
                    units(45, 47)
                    dve.wait_ge(gks_mm, it + 1)
                    ve.scalar_tensor_tensor(out=rhs1[:, :], in0=side[1][:, 0:P], scalar=nebc[:, 1:2], in1=vt[:, 1, :],
                                            op0=ALU.mult, op1=ALU.add).then_inc(grhs_ready, 1)
                    units(47, 52)
                    dve.wait_ge(gst_mm, it * 2 + 2)
                    ve.scalar_tensor_tensor(out=pstate[:, 1, :], in0=pstate[:, 1, :], scalar=eb_row[:, T - 1:T], in1=side[3][:, 0:P],
                                            op0=ALU.mult, op1=ALU.add).then_inc(gst_ready, 1)
                    units(52, 55)
                    dve.wait_ge(gss_mm, it + 1)
                    ve.tensor_scalar(oms[:, :], side[2][:, 0:N], 1.0 / P, EPS, ALU.mult, ALU.add).then_inc(go_step, 1)
                    dve.wait_ge(go_step, it * 4 + 1)
                    ve.reciprocal(orc[:, :], oms[:, :]).then_inc(go_step, 1)
                    units(55, 58)
                    dve.wait_ge(gors_ready, it + 1)
                    ve.scalar_tensor_tensor(out=orc[:, :], in0=osb[:, :], scalar=col(par, Q_GNG + l), in1=oms[:, :],
                                            op0=ALU.mult, op1=ALU.mult).then_inc(go_step, 1)
                    dve.wait_ge(go_step, it * 4 + 3)
                    ve.tensor_tensor(y32[:, 0, :], orc[:, :], gates[:, bass.ds(h, 1), :].rearrange("p a n -> p (a n)"),
                                     ALU.mult).then_inc(go_step, 1)
                    units(58, 60)
                    dve.wait_ge(gyhi, it + 1)
                    ve.tensor_tensor(y_lo[:, bass.ds(h + YT[GDN], 1), :], y32[:, 0, :],
                                     y_hi[:, bass.ds(h + YT[GDN], 1), :].bitcast(F32), ALU.subtract).then_inc(y_ready[GDN], 1)

                def merged_lo(k):
                    dve.wait_ge(mhi_ready, l * KT + k + 1)
                    ve.tensor_tensor(tile_of(y_lo, k), tile_of(wide, k), tile_of(y_hi, k).bitcast(F32),
                                     ALU.subtract).then_inc(mlo_ready, 1)

                def gdn_merge_turn(h, last):
                    ub, split = splitter(l, OFF_X, h, XTURN)
                    bank_now[0] = dve.snap(l * BANK_USES + BK_X + h * 2)
                    for i in range(4):
                        split(MB * i + 3, MB * i + 8)
                        merge_block(ub, i, i % 2, False, h * 4 + i)
                        if not last:
                            merged_lo(dve.snap(h * 4 + i))

                with dve.Fori(0, BT - 1) as h:
                    gdn_merge_turn(h, False)
                gdn_merge_turn(BT - 1, True)
                for k in range(KT - 4, KT):
                    merged_lo(k)

                ve.memset(sq_sum[:, :], 0.0).then_inc(sum_cleared, 1)
                dve.wait_ge(sum_cleared, l + 2)
                settled(dve)
                with dve.Fori(0, BT) as h:
                    ub, split = splitter(l, OFF_O, h, TURN)
                    for i in range(4):
                        split(4 * i + 3, 4 * i + 7)
                        k = dve.snap(h * 4 + i)
                        dve.wait_ge(unit_used, ub + RING + UB * (i + 1))
                        ve.tensor_tensor(tile_of(x, k), tile_of(x, k), acc[i][:, 0:N], ALU.add).then_inc(bank_free[i], 1)
                        dve.wait_ge(bank_free[i], l * BANK_USES + BK_O + h + 1 + BF)
                        dve.sem_inc(x_updated, 1)
                        x_added((l + 1) * KT + h * 4 + i)
                        x_lo(l + 1, k, (l + 1) * KT + h * 4 + i)
            mean_square(DEPTH)
            dve.wait_ge(rstd_ready, DEPTH + 1)
            for k in range(KT):
                last = normed(DEPTH, k)
                if k % 4 == 3:
                    last.then_inc(h_ready, 1)

        @block.tensor
        def _(pe):
            mm = nc.tensor.matmul

            def product(bank, slot, hi, lo, k0, first, last):
                for k in range(UK):
                    w_h, w_l = whi[:, slot, k * P:(k + 1) * P], wlo[:, slot, k * P:(k + 1) * P]
                    mm(acc[bank][:, 0:N], w_h, hi[:, k0 + k, :], start=first and k == 0, stop=False)
                    mm(acc[bank][:, 0:N], w_h, lo[:, k0 + k, :], start=False, stop=False)
                    op = mm(acc[bank][:, 0:N], w_l, hi[:, k0 + k, :], start=False, stop=last and k == UK - 1)
                op.then_inc(unit_used, 1)

            def streamer(l, off, i, per):
                ub = pe.snap(l * UNITS + off + i * per)

                def unit(j, bank, hi, lo, k0, first, last):
                    pe.wait_ge(lo_ready, ub + j + 1 + RING)
                    product(bank, j % RING, hi, lo, k0, first, last)
                return unit

            def norm_sum(n):
                pe.wait_ge(sq_added, n * KT + KT + 1)
                mm(side[0][:, 0:N], ones, sq_sum[:, :], start=True, stop=True).then_inc(norm_mm, 1)

            pe.wait_ge(con_loaded, 16)
            pe.wait_ge(par_loaded, 16)
            with pe.Fori(0, DEPTH) as l:
                def blocks(unit, a, b, free, hi=act_hi, lo=act_lo, ready=None):
                    for j in range(a, b):
                        i = j // UB
                        if j % UB == 0:
                            pe.wait_ge(bank_free[i % 4], free + BF)
                        if ready and j < UB:
                            pe.wait_ge(ready, l * KT + UK * (j + 1))
                        unit(j, i % 4, hi, lo, UK * (j % UB), j % UB == 0, j % UB == UB - 1)

                unit = streamer(l, OFF_G, 0, TURN)
                free = pe.snap(l * BANK_USES + BK_G)
                blocks(unit, 0, UB, free, ready=xlo_ready)
                norm_sum(l)
                blocks(unit, UB, TURN, free)
                with pe.Fori(0, BT - 1) as r:
                    h = pe.snap(r + 1)
                    unit = streamer(l, OFF_G, h, TURN)
                    blocks(unit, 0, TURN, pe.snap(l * BANK_USES + BK_G + h))

                pe.wait_ge(h_ready, l * 2 * BT + 2 * BT)
                for c in range(3):
                    lo, n = c * P, (P, P, NS)[c]
                    for k in range(KT):
                        op = mm(side[1][0:n, 2 * BT * c:2 * BT * (c + 1)], wide[:, k, lo:lo + n],
                                par[:, bass.ds(Q_WAB + (l * KT + k) * 2 * BT, 2 * BT)], start=k == 0, stop=k == KT - 1)
                    op.then_inc(ab_mm, 1)

                pe.wait_ge(hlo_ready, l * 2 * BT + 2 * BT)
                settled(pe)
                with pe.Fori(0, BT) as h:
                    unit = streamer(l, OFF_R, h, TURN)
                    blocks(unit, 0, TURN, pe.snap(l * BANK_USES + BK_R + h), y_hi, y_lo)

                pe.wait_ge(ahi_copied, l * BT + BT)
                pe.wait_ge(alo_copied, l * BT + BT)
                settled(pe)
                with pe.Fori(0, BT) as h:
                    it = pe.snap(l * BT + h)
                    unit = streamer(l, OFF_S, h, TURN)
                    free = pe.snap(l * BANK_USES + BK_S + h)
                    blocks(unit, 0, 3, free)
                    pe.wait_ge(head_copied, it + 1)
                    pe.wait_ge(ab_evac, l + 1)
                    mm(side[0][:, 0:T], head[:, 1, 0:P], head[:, 0, 0:T], start=True, stop=True)
                    mm(side[0][:, T:T + P], head[:, 1, P:T], head[:, 0, P:T], start=True, stop=True).then_inc(rsc_mm, 1)
                    for a in range(2):
                        for c in range(CH):
                            op = nc.tensor.transpose(side[1][:, (2 * a + c) * P:(2 * a + c + 1) * P],
                                                     head[:, 1 + a, c * P:(c + 1) * P], ident)
                    op.then_inc(rtr_mm, 1)
                    blocks(unit, 3, 5, free)
                    pe.wait_ge(scores_ready, it + 1)
                    pe.wait_ge(kdvt_ready, it + l * BT + 1)
                    mm(side[2][:, 0:T], vt[:, 0, :], scores[:, 0:T], start=True, stop=False)
                    mm(side[2][:, P:T], vt[:, 1, :], scores[:, T:T + P], start=False, stop=True).then_inc(ro_mm, 1)
                    for c in range(CH):
                        op = mm(side[3][:, 0:P], kd[:, c, :], vt[:, c, :], start=c == 0, stop=c == CH - 1)
                    op.then_inc(rst_mm, 1)
                    blocks(unit, 5, 7, free)
                    for b in range(NS):
                        op = mm(side[b // 4][:, (b % 4) * P:(b % 4 + 1) * P], head[:, 2, T + b:T + b + 1].to_broadcast([P, P]),
                                ident, start=True, stop=True)
                    op.then_inc(rvb_mm, 1)
                    blocks(unit, 7, 11, free)
                    pe.wait_ge(rstate_new, it * NS + NS)
                    for b in range(NS):
                        op = mm(side[2][:, T + b:T + b + 1], state[:, b, :], head[:, 0, T + b:T + b + 1], start=True, stop=True)
                    op.then_inc(ros_mm, 1)
                    blocks(unit, 11, 14, free)
                    pe.wait_ge(ro_copied, it + 1)
                    mm(side[3][:, 0:N], ones, osq[:, :], start=True, stop=True).then_inc(rss_mm, 1)
                    blocks(unit, 14, TURN, free)

                pe.wait_ge(plw_loaded, l * 16 + 16)
                for g in range(BT):
                    unit = streamer(l, OFF_P, g, PTURN)
                    for j in range(PTURN):
                        bank = 2 * (g % 2) + j // UB
                        if j % UB == 0:
                            pe.wait_ge(bank_free[bank], l * BANK_USES + BK_P + g // 2 + BF)
                        unit(j, bank, act_hi, act_lo, UK * (j % UB), j % UB == 0, j % UB == UB - 1)
                    pe.wait_ge(psum_step, l * BT + g + 2)
                    mm(side[0][:, 0:N], plw[:, g, :], pdiff[:, :], start=True, stop=True).then_inc(pmix_mm, 1)
                    if g == 1:
                        pe.wait_ge(ab_step, l * 15 + 15)
                        mm(side[1][:, 0:CH * BT], tri, g_col[:, 0:CH * BT], start=True, stop=True).then_inc(bcol_mm, 1)

                def merge_units(unit, a, b, branches, free):
                    for j in range(a, b):
                        i, u = j // MB, j % MB
                        p = i % 2
                        if u == 0:
                            pe.wait_ge(bank_free[2 * p], free + i // 2 + BF)
                        if u < UB:
                            unit(j, 2 * p, act_hi, act_lo, UK * u, u == 0, u == UB - 1)
                        else:
                            pe.wait_ge(bank_free[2 * p + 1], free + i // 2 + BF)
                            unit(j, 2 * p + 1, y_hi, y_lo, YT[branches[i % len(branches)]], True, True)

                for n in (SCV, POOL, RET):
                    pe.wait_ge(y_ready[n], l * BT + BT)
                settled(pe)
                with pe.Fori(0, BT) as h:
                    it = pe.snap(l * BT + h)
                    unit = streamer(l, OFF_M, h, MTURN)
                    free = pe.snap(l * BANK_USES + BK_M + h * 6)

                    def units(a, b):
                        merge_units(unit, a, b, (SCV, POOL, RET), free)

                    units(0, 3)
                    pe.wait_ge(gbc_ready, it + 1)
                    pe.wait_ge(gsq_ready, it * 2 + 2)
                    for a in range(2):
                        op = mm(side[a][:, 0:N], ones, sq2[:, a, :], start=True, stop=True)
                    op.then_inc(gn_mm, 1)
                    for c in range(CH):
                        mm(side[2][:, c * P:(c + 1) * P], g_bc[:, c, :], tri, start=True, stop=True)
                    mm(side[2][:, T:N], g_bc[0:NS, 2, :], con[0:NS, C_ID:C_ID + NS], start=True, stop=True)
                    mm(side[2][:, N:BR], beta_bc[0:NS, :], con[0:NS, C_ID:C_ID + NS], start=True, stop=True).then_inc(grow_mm, 1)
                    for c in range(CH):
                        op = nc.tensor.transpose(side[3][:, c * P:(c + 1) * P], head[:, 2, c * P:(c + 1) * P], ident)
                    op.then_inc(gvt_mm, 1)
                    units(3, 11)
                    pe.wait_ge(gqk_ready, it + 1)
                    for a in range(2):
                        for c in range(CH):
                            op = mm(side[0][:, (2 * a + c) * P:(2 * a + c + 1) * P], head[:, 1, c * P:(c + 1) * P],
                                    head[:, 1 - a, c * P:(c + 1) * P], start=True, stop=True)
                    op.then_inc(gkq_mm, 1)
                    for c in range(CH):
                        op = nc.tensor.transpose(side[1][:, c * P:(c + 1) * P], head[:, 1, c * P:(c + 1) * P], ident)
                    op.then_inc(gkt_mm, 1)
                    units(11, 14)
                    pe.wait_ge(gR_ready, it * 2 + 2)
                    for c in range(CH):
                        op = nc.tensor.transpose(side[0][:, c * P:(c + 1) * P], TR[:, 1, c, :], ident)
                    op.then_inc(gT_mm, 1)
                    units(14, LEV0)
                    at = LEV0
                    for v in range(1, LEVELS):
                        if v == 1:
                            pe.wait_ge(gT_ready, it + 1)
                        else:
                            pe.wait_ge(gTR_ready, it * 6 + v - 1)
                        pe.wait_ge(gem_ready, it * 6 + v)
                        for c in range(CH):
                            op = mm(side[0][:, c * P:(c + 1) * P], Em[:, v % 2, c * P:(c + 1) * P], TR[:, 0, c, :], start=True, stop=True)
                        op.then_inc(gX_mm, 1)
                        if v in (2, 4):
                            if v == 2:
                                pe.wait_ge(state_loaded, (it + l * BT) * 16 + 16 * BT + 16)
                                pe.wait_ge(gqd_ready, it + 1)
                                pe.wait_ge(kdvt_ready, it + (l + 1) * BT + 1)
                            else:
                                pe.wait_ge(gstate_new, it * NS + 4)
                            for b in range(2 * v - 4, 2 * v):
                                dst = side[3][:, (b % 4) * P:(b % 4 + 1) * P]
                                mm(dst, head[:, 2, T + b:T + b + 1].to_broadcast([P, P]), ident, start=True, stop=False)
                                op = mm(dst, mk[:, b:b + 1].to_broadcast([P, P]), state[:, b, :], start=False, stop=True)
                            op.then_inc(gdl_mm, 1)
                        if v == 6:
                            pe.wait_ge(gstate_new, it * NS + NS)
                            for b in range(NS):
                                op = mm(side[3][:, b:b + 1], state[:, b, :], head[:, 0, T + b:T + b + 1], start=True, stop=True)
                            op.then_inc(gos_mm, 1)
                        units(at, at + 2)
                        pe.wait_ge(gX_ready, it * 6 + v)
                        if v < LEVELS - 1:
                            for c in range(CH):
                                mm(side[1][:, c * P:(c + 1) * P], TR[:, 1, c, :], Xs[:, c, :], start=True, stop=True)
                        for c in range(CH):
                            op = mm(side[1][:, T + c * P:T + (c + 1) * P], Xs[:, c, :], TR[:, 1, c, :], start=True, stop=True)
                        op.then_inc(gD_mm, 1)
                        units(at + 2, at + LEVU)
                        at += LEVU
                    pe.wait_ge(gTR_ready, it * 6 + 6)
                    mm(side[2][:, 0:P], TR[:, 1, 0, :], vt[:, 0, :], start=True, stop=True).then_inc(gsol_mm, 1)
                    units(at, 43)
                    pe.wait_ge(gvn_ready, it * 2 + 1)
                    pe.wait_ge(gkd_ready, it + 1)
                    pe.wait_ge(gos_copied, it + 1)
                    mm(side[3][:, 0:P], kd[:, 0, :], vn[:, 0, :], start=True, stop=True).then_inc(gst_mm, 1)
                    units(43, 46)
                    pe.wait_ge(gst_ready, it * 2 + 1)
                    mm(side[1][:, 0:P], head[:, 1, P:T], pstate[:, 1, :], start=True, stop=True).then_inc(gks_mm, 1)
                    pe.wait_ge(gattn_ready, it + 1)
                    mm(side[0][:, 0:P], vn[:, 0, :], attn[:, 0, :], start=True, stop=True)
                    units(46, 48)
                    pe.wait_ge(grhs_ready, it + 1)
                    mm(side[2][:, 0:P], TR[:, 1, 1, :], rhs1[:, :], start=True, stop=True).then_inc(gsol_mm, 1)
                    units(48, 51)
                    mm(side[0][:, P:T], pstate[:, 1, :], qd[:, :], start=True, stop=False)
                    pe.wait_ge(gvn_ready, it * 2 + 2)
                    mm(side[0][:, P:T], vn[:, 1, :], attn[:, 1, :], start=False, stop=True).then_inc(go_mm, 1)
                    mm(side[3][:, 0:P], kd[:, 1, :], vn[:, 1, :], start=True, stop=True).then_inc(gst_mm, 1)
                    units(51, 54)
                    pe.wait_ge(go_copied, it * 2 + 2)
                    mm(side[2][:, 0:N], ones, osq[:, :], start=True, stop=True).then_inc(gss_mm, 1)
                    units(54, 60)

                with pe.Fori(0, BT) as h:
                    unit = streamer(l, OFF_X, h, XTURN)
                    free = pe.snap(l * BANK_USES + BK_X + h * 2)
                    merge_units(unit, 0, 4, (GDN,), free)
                    pe.wait_ge(y_ready[GDN], l * BT + BT)
                    merge_units(unit, 4, XTURN, (GDN,), free)

                with pe.Fori(0, BT) as h:
                    unit = streamer(l, OFF_O, h, TURN)
                    blocks(unit, 0, TURN, pe.snap(l * BANK_USES + BK_O + h), y_hi, y_lo, ready=mlo_ready)
            norm_sum(DEPTH)


def shape_constants():
    f = np.float32
    con = np.zeros((P, C_END), f)
    i = np.arange(P)
    con[:, C_ID:C_ID + P] = np.eye(P)
    con[:, C_ONE:C_ONE + P] = 1.0
    upper = i[None, :] >= i[:, None]
    con[:, C_TRI:C_TRI + P] = upper
    con[:, C_NEG:C_NEG + P] = np.where(upper, 0.0, -1e30)
    con[:, C_STRICT:C_STRICT + P] = i[None, :] > i[:, None]
    for v in range(LEVELS):
        blk = i >> v
        con[:, C_LEV + v * P:C_LEV + (v + 1) * P] = (blk[:, None] % 2 == 0) & (blk[None, :] == blk[:, None] + 1)
    lg = np.log(1.0 - 2.0 ** (-5.0 - np.arange(BT)))
    t = np.arange(T)
    lag = t[None, :] - i[:, None]
    for h in range(BT):
        con[:, C_DM + h * T:C_DM + (h + 1) * T] = np.where(lag >= 0, np.exp(lg[h] * np.maximum(lag, 0)), 0.0)
        for c in range(CH):
            con[:, C_GDEC + h * CH + c] = np.exp(lg[h] * (T - 1 - (c * P + i)))
        con[:, C_GAM + h] = np.exp(lg[h])
    half = P // 2
    inv = (f(10000.0) ** (-np.arange(half, dtype=f) / f(half))).astype(f)
    pos = np.concatenate([np.arange(T), np.full(NS, PAST)]).astype(f)
    ang = (pos[None, :] * inv[:, None]).astype(f).astype(np.float64)
    cos, sin = np.cos(ang), np.sin(ang)
    con[:, C_COS:C_COS + N] = np.concatenate([cos, cos])
    con[:, C_SIN:C_SIN + N] = np.concatenate([sin, -sin])
    for g, w in enumerate(WINDOWS):
        con[:, C_CORR + 16 * g:C_CORR + 16 * (g + 1)] = w / np.minimum(np.arange(16) + 1, w)
    return con


def kernel(x_prompt, x_sample, state_ret, state_gdn, state_gdn_conv, state_sconv, state_pool,
           norm_g, w_in, gdn_conv_w, gdn_a_log, gdn_dt_bias, gdn_norm_g,
           sconv_w, pool_w, pool_scale, w_branch, w_out, final_norm_g):
    import concourse.bacc as bacc
    from concourse.bass_utils import run_bass_kernel_spmd

    A = np.asarray
    w_in, w_branch, w_out = A(w_in), A(w_branch), A(w_out)

    SPLIT = [BW] * 4 + [3 * BW, BW, BT, BT] + [BW] * 6 + [4 * D_MODEL]
    start = np.concatenate([[0], np.cumsum(SPLIT)])
    (RQ, RK, RV, RG, GQKV, GG, GA, GB, SB, SCC, SH, SG, PU, PG, ML) = start[:-1]

    def units(w, c0):
        k = w.shape[1] // P
        b = w[:, :, c0:c0 + P].reshape(DEPTH, k // UK, UK, P, P)
        return b.transpose(0, 1, 3, 2, 4).reshape(DEPTH, k // UK, P, UC)

    parts = []
    for h in range(BT):
        parts += [units(w_in, c + h * P) for c in (GQKV, GQKV + BW, GQKV + 2 * BW, GG)]
    for h in range(BT):
        parts += [units(w_in, c + h * P) for c in (RQ, RK, RV, RG)]
    for h in range(BT):
        parts += [units(w_in, c + h * P) for c in (SCC, SH, SB, SG)]
    for h in range(BT):
        parts += [units(w_in, c + h * P) for c in (PU, PG)]
    for m in range(KT):
        for n in (SCV, POOL, RET):
            parts += [units(w_in, ML + n * D_MODEL + m * P), units(w_branch[:, n], m * P)]
    for m in range(KT):
        parts += [units(w_in, ML + GDN * D_MODEL + m * P), units(w_branch[:, GDN], m * P)]
    for m in range(KT):
        parts += [units(w_out, m * P)]
    w_stream = np.concatenate(parts, axis=1).reshape(-1, P, UC)
    assert w_stream.shape[0] == DEPTH * UNITS
    w_stream = np.concatenate([w_stream, w_stream[:RING]])

    xt = np.concatenate([A(x_prompt)[0], A(x_sample)[:, 0]], axis=0)
    x_in = np.ascontiguousarray(xt.T.reshape(KT, P, N).transpose(1, 0, 2))

    def chan(a, tiles):
        a = A(a)
        a = a.reshape(a.shape[:-1] + (tiles, P))
        return np.moveaxis(a, -1, 0)

    def flat(a):
        return np.ascontiguousarray(a).reshape(P, -1)

    def rows(a):
        return flat(np.broadcast_to(A(a)[None, :, None, :], (P, DEPTH, 3, BT)))

    wab = w_in[:, :, GA:GA + 2 * BT].reshape(DEPTH, KT, P, 2 * BT).transpose(2, 0, 1, 3)
    gh = chan(state_gdn_conv, 3 * BT).reshape(P, DEPTH, NS, GW - 1, 3, BT).transpose(0, 1, 5, 4, 2, 3)
    sh = chan(state_sconv, BT).transpose(0, 1, 4, 2, 3)
    pool_in = np.ascontiguousarray(chan(state_pool, BT).transpose(1, 0, 4, 2, 3)).reshape(DEPTH, P, BT * NS * PH)
    params = np.concatenate([
        flat(chan(norm_g, KT)), flat(chan(final_norm_g, KT)),
        flat(chan(gdn_conv_w, 3 * BT).reshape(P, DEPTH, GW, 3, BT).transpose(0, 1, 4, 3, 2)),
        flat(chan(sconv_w, BT).transpose(0, 1, 3, 2)),
        flat(A(gdn_norm_g).T), flat(chan(pool_scale, BT)),
        rows(gdn_dt_bias), rows(gdn_a_log), flat(wab), flat(gh), flat(sh)], axis=1)
    assert params.shape[1] == Q_END
    w_pool = np.ascontiguousarray(A(pool_w).transpose(0, 2, 1, 3))

    arrays = {"w_stream": w_stream, "w_pool": w_pool, "pool_in": pool_in, "x_in": x_in, "params": params, "consts": shape_constants(),
              "ret_in": A(state_ret), "gdn_in": A(state_gdn)}
    st = (DEPTH, NS, BT, P, P)
    outs = {"y_out": (P, KT * N), "hist_out": (DEPTH, P, H_END), "p_ret": (DEPTH, 1, BT, P, P), "p_gdn": (DEPTH, 1, BT, P, P),
            "s_ret": st, "s_gdn": st}
    nc = bacc.Bacc("TRN2", target_bir_lowering=False, num_devices=1)
    args = [nc.dram_tensor(k, a.shape, F32, kind="ExternalInput").ap() for k, a in arrays.items()]
    args += [nc.dram_tensor(k, s, F32, kind="ExternalOutput").ap() for k, s in outs.items()]
    trunk(nc, *args)
    r = run_bass_kernel_spmd(nc, [arrays], core_ids=[0]).results[0]

    y = r["y_out"].reshape(P, KT, N).transpose(2, 1, 0).reshape(N, D_MODEL)
    y_prompt, y_sample = y[None, :T], y[T:, None]
    ho = r["hist_out"]

    def hists(lo, hi, shape, perm, k, ch):
        a = ho[:, :, lo:hi].reshape((DEPTH, P) + shape).transpose(perm)
        a = a.reshape(DEPTH, NS + 1, k, ch)
        return np.ascontiguousarray(a[:, :1]), np.ascontiguousarray(a[:, 1:])

    pgc, sgc = hists(H_G, H_S, (BT, 3, NS + 1, GW - 1), (0, 4, 5, 3, 2, 1), GW - 1, 3 * BW)
    psc, ssc = hists(H_S, H_P, (BT, NS + 1, SW - 1), (0, 3, 4, 2, 1), SW - 1, BW)
    ppl, spl = hists(H_P, H_END, (BT, NS + 1, PH), (0, 3, 4, 2, 1), PH, BW)
    return (np.ascontiguousarray(y_prompt), np.ascontiguousarray(y_sample), r["p_ret"], r["p_gdn"], pgc, psc, ppl,
            r["s_ret"], r["s_gdn"], sgc, ssc, spl)
```

```python
from contextlib import ExitStack

import numpy as np

import concourse.bass as bass
from concourse import mybir

F32 = mybir.dt.float32
F32R = mybir.dt.float32r
ALU = mybir.AluOpType
ACT = mybir.ActivationFunctionType

P = 128
DEPTH = 2
D_MODEL = 2048
KT = D_MODEL // P
BW = D_MODEL // 4
BT = BW // P
T = 256
NS = 8
N = T + NS
CH = T // P
PAST = 2048
EPS = 1e-6
WINDOWS = (2, 4, 8, 16)
RET, GDN, SCV, POOL = range(4)
YT = {SCV: 0, POOL: BT, RET: 2 * BT, GDN: 3 * BT}
GW, SW, PH = 4, 3, 15

GE = GW - 1 + T + NS * GW
SE = SW - 1 + T + NS * SW
PE_ = PH + T + NS * (PH + 1)
GC = GE - (GW - 1)
SC = SE - (SW - 1)

UK = 4
UC = UK * P
RING = 4
UB = KT // UK
TURN = 4 * UB
PTURN = 2 * UB
MB = UB + 1
MTURN = 12 * MB
KQ0, LEV0, LEVU = 6, 11, 5
XTURN = 4 * MB
OFF_G = 0
OFF_R = OFF_G + 4 * TURN
OFF_S = OFF_R + 4 * TURN
OFF_P = OFF_S + 4 * TURN
OFF_M = OFF_P + 4 * PTURN
OFF_X = OFF_M + 4 * MTURN
OFF_O = OFF_X + 4 * XTURN
UNITS = OFF_O + 4 * TURN

BK_G, BK_R, BK_S, BK_P, BK_M, BK_X, BK_O = 0, 4, 8, 12, 14, 38, 46
BANK_USES = 50
BF = 4

PWIN_AT = (0, 2, 5, 9)
PWIN = 14

C_ID, C_ONE, C_TRI, C_NEG, C_STRICT, C_LEV = 0, P, 2 * P, 3 * P, 4 * P, 5 * P
LEVELS = 7
C_DM = C_LEV + LEVELS * P
C_COS = C_DM + BT * T
C_SIN = C_COS + N
C_CORR = C_SIN + N
C_GDEC = C_CORR + BT * 16
C_GAM = C_GDEC + BT * CH
C_END = C_GAM + BT

Q_NG = 0
Q_GCW = Q_NG + (DEPTH + 1) * KT
Q_SCW = Q_GCW + DEPTH * BT * 3 * GW
Q_GNG = Q_SCW + DEPTH * BT * SW
Q_PSC = Q_GNG + DEPTH
Q_DT = Q_PSC + DEPTH * BT
Q_AL = Q_DT + DEPTH * 3 * BT
Q_WAB = Q_AL + DEPTH * 3 * BT
Q_GH = Q_WAB + DEPTH * KT * 2 * BT
Q_SH = Q_GH + DEPTH * BT * 3 * NS * (GW - 1)
Q_PH = Q_SH + DEPTH * BT * NS * (SW - 1)
Q_END = Q_PH

H_G = 0
H_S = H_G + BT * 3 * (NS + 1) * (GW - 1)
H_P = H_S + BT * (NS + 1) * (SW - 1)
H_END = H_P + BT * (NS + 1) * PH

SHARED = 6514


def trunk(nc, w_stream, w_pool, pool_in, x_in, params, consts, ret_in, gdn_in, y_out, hist_out,
          p_ret, p_gdn, s_ret, s_gdn):
    with ExitStack() as ctx:
        def sb(name, shape, dt=F32):
            return ctx.enter_context(nc.sbuf_tensor(name, [P] + shape, dt))

        def psum(name):
            return ctx.enter_context(nc.psum_tensor(name, [P, 512], F32))

        primes = []

        def sem(name, primed=0):
            s = ctx.enter_context(nc.semaphore(name))
            if primed:
                primes.append((s, primed))
            return s

        raw = sb("raw", [RING, UC])
        whi = sb("whi", [RING, UC], F32R)
        wlo = sb("wlo", [RING, UC], F32R)
        x = sb("x", [KT, N])
        act_hi = sb("act_hi", [KT, N], F32R)
        act_lo = sb("act_lo", [KT, N], F32R)
        y_hi = sb("y_hi", [KT, N], F32R)
        y_lo = sb("y_lo", [KT, N], F32R)
        wide = sb("wide", [KT, N])
        rqkv = wide[:, 0:3 * BT, :].rearrange("p a n -> p (a n)")
        gqkv = sb("gqkv", [BT * 3 * N])
        gates = sb("gates", [BT, N])
        con = sb("con", [C_END])
        par = sb("par", [Q_END])
        hist = sb("hist", [H_END])
        phist = sb("phist", [BT * NS * PH])
        pieces = {}

        def shared(kind, shape):
            size = int(np.prod(shape))
            at = pieces.get(kind, 0)
            pieces[kind] = at + size
            assert at + size <= SHARED, (kind, at + size)
            view = share[:, at:at + size]
            if len(shape) == 2:
                view = view.rearrange("p (a b) -> p a b", b=shape[1])
            if len(shape) == 3:
                view = view.rearrange("p (a b c) -> p a b c", b=shape[1], c=shape[2])
            return view

        def early(shape):
            return shared("early", shape)

        def late(shape):
            return shared("late", shape)

        share = sb("share", [SHARED])
        ident, ones = con[:, C_ID:C_ID + P], con[:, C_ONE:C_ONE + P]
        tri, neg = con[:, C_TRI:C_TRI + P], con[:, C_NEG:C_NEG + P]
        strict = con[:, C_STRICT:C_STRICT + P]
        squares = early([2, N])
        ms = early([N])
        rms = early([N])
        rstd = ms
        ab = sb("ab", [3 * 2 * BT])
        A3 = 3 * BT
        ab_x, ab_abs, ab_e, ab_den, ab_rec, ab_s, ab_s2, ab_q, ab_relu, ab_sp, ab_ea, g_col, beta = \
            [sb(n, [A3]) for n in ("ab_x", "ab_abs", "ab_e", "ab_den", "ab_rec", "ab_s", "ab_s2", "ab_q",
                                   "ab_relu", "ab_sp", "ab_ea", "g_col", "beta")]
        b_col = sb("b_col", [CH * BT])
        gext = early([3, GE])
        gconv = early([3, GC])
        rope_a = early([2, N])
        rope_b = early([2, N])
        sq2 = gext.rearrange("p a n -> p (a n)")[:, 0:2 * N].rearrange("p (a n) -> p a n", n=N)
        rn2 = gconv.rearrange("p a n -> p (a n)")[:, 0:2 * N].rearrange("p (a n) -> p a n", n=N)
        sc_c = early([N])
        sext = early([SE])
        sconv = early([SC])
        sgate = early([N])
        sprod = early([N])
        pext = early([PE_])
        psum_a = rope_a.rearrange("p a n -> p (a n)")[:, 0:PE_]
        psum_b = rope_b.rearrange("p a n -> p (a n)")[:, 0:PE_]
        pdiff = early([N])
        pgate = early([N])
        plw = sb("plw", [BT, P])
        y32 = sb("y32", [2, N])
        head = sb("head", [3, N])
        qd = late([P])
        state = sb("state", [NS, P])
        pstate = sb("pstate", [2, P])
        osb = sb("osb", [N])
        osq = sb("osq", [N])
        sq_sum = osq
        oms = sb("oms", [N])
        orc = sb("orc", [N])
        scores = early([T + P])
        kd = sb("kd", [CH, P])
        vt = sb("vt", [CH, P])
        g_bc = late([3, P])
        beta_bc = late([P])
        BR = N + NS
        b_row = late([BR])
        eb_row = late([BR])
        hcol = sb("hcol", [8])
        nebc = sb("nebc", [CH])
        bet2 = sb("bet2", [CH])
        dec = late([CH, P])
        decs = late([CH, P])
        E_ = late([CH, P])
        Em = late([2, CH * P])
        attn = late([CH, P])
        TR = late([2, CH, P])
        Xs = late([CH, P])
        vn = late([CH, P])
        rhs1 = late([P])
        mk, sdelta, qkb = sb("mk", [NS]), sb("sdelta", [NS]), sb("qkb", [NS])
        kb = sb("kb", [NS])
        msig = late([2, N])
        mprod = late([2, N])

        acc = [psum(f"acc{i}") for i in range(4)]
        side = [psum(f"side{i}") for i in range(4)]

        raw_loaded = [sem(f"raw_loaded{i}") for i in range(RING)]
        hi_ready = sem("hi_ready")
        lo_ready = sem("lo_ready", RING)
        unit_used = sem("unit_used", RING)
        bank_free = [sem(f"bank_free{i}", BF) for i in range(4)]
        x_loaded = [sem(f"x_loaded{q}") for q in range(4)]
        con_loaded, par_loaded = sem("con_loaded"), sem("par_loaded")
        plw_loaded, ph_loaded, state_loaded = sem("plw_loaded"), sem("ph_loaded"), sem("state_loaded")
        out_written, hist_written = sem("out_written"), sem("hist_written")
        state_written, pstate_written, pstate_free = sem("state_written"), sem("pstate_written"), sem("pstate_free", 1)
        zeros_set, passed = sem("zeros_set"), sem("passed")
        sum_cleared = sem("sum_cleared")
        sq_ready, norm_mm, ms_ready, rms_ready, rstd_ready = [sem(n) for n in
            ("sq_ready", "norm_mm", "ms_ready", "rms_ready", "rstd_ready")]
        sq_added, xhi_ready, xlo_ready = sem("sq_added", 2), sem("xhi_ready"), sem("xlo_ready")
        x_updated = sem("x_updated")
        h_ready, hhi_ready, hlo_ready = sem("h_ready"), sem("hhi_ready"), sem("hlo_ready")
        ahi_copied, alo_copied = sem("ahi_copied"), sem("alo_copied")
        ab_mm, ab_evac, ab_step, ab_act, bcol_mm, bcol_ready = [sem(n) for n in
            ("ab_mm", "ab_evac", "ab_step", "ab_act", "bcol_mm", "bcol_ready")]
        ghist_in, gconv_step, gqkv_ready, ghist_out = [sem(n, p) for n, p in
            (("ghist_in", 0), ("gconv_step", 3 * GW), ("gqkv_ready", 0), ("ghist_out", 3))]
        rope_step = sem("rope_step")
        head_copied, rsc_mm, rtr_mm, scores_ready, kdvt_ready, ro_mm, rst_mm, rst_ready, rvb_mm = [sem(n) for n in
            ("head_copied", "rsc_mm", "rtr_mm", "scores_ready", "kdvt_ready", "ro_mm", "rst_mm", "rst_ready", "rvb_mm")]
        rdecayed, rstate_new, ros_mm, ro_copied, rss_mm, ro_step, rors_ready = [sem(n) for n in
            ("rdecayed", "rstate_new", "ros_mm", "ro_copied", "rss_mm", "ro_step", "rors_ready")]
        sconv_step, shist_in, shist_out, sy_ready, syhi = [sem(n, p) for n, p in
            (("sconv_step", SW), ("shist_in", 0), ("shist_out", 1), ("sy_ready", 0), ("syhi", 0))]
        phist_in, psum_step, phist_out, pmix_mm, py_ready, pyhi, pwin = [sem(n, p) for n, p in
            (("phist_in", 0), ("psum_step", 1), ("phist_out", 1), ("pmix_mm", BT), ("py_ready", 1), ("pyhi", 0),
             ("pwin", 0))]
        y_ready = [sem(f"y_ready{n}") for n in range(4)]
        ryhi, gyhi = sem("ryhi"), sem("gyhi")
        gsq_ready, gbc_ready, gn_mm, grow_mm, gvt_mm, grow_ready, grn_step, grn_act, gqn_ready, gcol_step, gcol_act = \
            [sem(n) for n in ("gsq_ready", "gbc_ready", "gn_mm", "grow_mm", "gvt_mm", "grow_ready", "grn_step",
                              "grn_act", "gqn_ready", "gcol_step", "gcol_act")]
        gkq_mm, gkt_mm, gE_ready, gattn_ready, gkd_ready, gem_ready, gR_ready, gT_mm, gT_ready, gX_mm, gX_ready, \
            gD_mm, gTR_ready = [sem(n) for n in ("gkq_mm", "gkt_mm", "gE_ready", "gattn_ready", "gkd_ready",
            "gem_ready", "gR_ready", "gT_mm", "gT_ready", "gX_mm", "gX_ready", "gD_mm", "gTR_ready")]
        gsol_mm, gvn_ready, gst_mm, gst_ready, gks_mm, grhs_ready, gqd_ready, go_mm, go_copied, gss_mm, go_step, \
            gors_ready = [sem(n) for n in ("gsol_mm", "gvn_ready", "gst_mm", "gst_ready", "gks_mm", "grhs_ready",
            "gqd_ready", "go_mm", "go_copied", "gss_mm", "go_step", "gors_ready")]
        gmk_ready, gdl_mm, gdecayed, gstate_new, gos_mm, gos_copied = [sem(n) for n in
            ("gmk_ready", "gdl_mm", "gdecayed", "gstate_new", "gos_mm", "gos_copied")]
        merged_ready = sem("merged_ready")
        gdecs_ready, gv_ready = sem("gdecs_ready"), sem("gv_ready")
        first_square, first_square_late, first_sum = sem("first_square"), sem("first_square_late"), sem("first_sum")
        gsam_step, gdelta_ready = sem("gsam_step"), sem("gdelta_ready")
        mhi_ready, mlo_ready = sem("mhi_ready"), sem("mlo_ready")

        def col(table, at):
            return table[:, bass.ds(at, 1)]

        def tile_of(tiles, k):
            return tiles[:, k, :] if isinstance(k, int) else tiles[:, bass.ds(k, 1), :].rearrange("p a n -> p (a n)")

        def quarter(tiles, q, part=4):
            return tiles[:, 4 * q:4 * q + part, :].rearrange("p a n -> p (a n)")

        def samples(tile, lead, taps, shift=0, width=1):
            body = tile[:, lead:lead + NS * taps].rearrange("p (b k) -> p b k", k=taps)
            return body[:, :, shift] if width == 1 else body[:, :, shift:shift + width]

        def settled(eng):
            eng.sem_inc(passed, 1)

        block = ctx.enter_context(nc.Block())

        @block.sync
        def _(sp):
            for s, n in primes:
                sp.sem_inc(s, n)
            sp.dma_start(par[:, :], params).then_inc(par_loaded, 16)
            for q in range(4):
                sp.dma_start(x[:, 4 * q:4 * q + 4, :], x_in[:, 4 * q:4 * q + 4, :]).then_inc(x_loaded[q], 16)
                if q == 0:
                    for s in range(RING):
                        sp.dma_start(raw[:, s, :], w_stream[s]).then_inc(raw_loaded[s], 16)
            sp.dma_start(con[:, :], consts).then_inc(con_loaded, 16)
            with sp.Fori(0, DEPTH * UNITS // RING) as r:
                u = sp.snap(r * RING)
                for s in range(RING):
                    sp.wait_ge(lo_ready, u + s + 1 + RING)
                    sp.dma_start(raw[:, s, :], w_stream[u + RING + s]).then_inc(raw_loaded[s], 16)
            for s in range(RING):
                sp.wait_ge(raw_loaded[s], (DEPTH * UNITS // RING + 1) * 16)
            for q in range(4):
                sp.wait_ge(h_ready, DEPTH * 2 * BT + q + 1)
                sp.dma_start(y_out[:, q * 4 * N:(q + 1) * 4 * N],
                             wide[:, 4 * q:4 * q + 4, :].rearrange("p a n -> p (a n)")).then_inc(out_written, 16)
            sp.wait_ge(out_written, 4 * 16)

        @block.gpsimd
        def _(pool):
            gp = nc.gpsimd
            gp.memset(ab[:, :], 0.0).then_inc(zeros_set, 1)
            for q in range(2):
                pool.wait_ge(x_loaded[q], 16)
                gp.tensor_tensor(quarter(wide, q), quarter(x, q), quarter(x, q), ALU.mult).then_inc(first_square, 1)
            pool.wait_ge(first_square, 2)
            gp.tensor_tensor(quarter(wide, 0), quarter(wide, 0), quarter(wide, 1), ALU.add).then_inc(first_square, 1)
            pool.wait_ge(par_loaded, 16)
            pool.wait_ge(con_loaded, 16)
            with pool.Fori(0, DEPTH) as l:
                pool.wait_ge(xlo_ready, l * KT + KT)
                settled(pool)
                gp.memset(gext[:, :, 0:GW - 1], 0.0)
                gp.memset(sext[:, 0:SW - 1], 0.0)
                gp.memset(pext[:, 0:PH], 0.0).then_inc(zeros_set, 1)
                pool.wait_ge(pmix_mm, l * BT + BT)
                settled(pool)
                pool.dma_start(plw[:, :, :], w_pool[l]).then_inc(plw_loaded, 16)
                pool.dma_start(phist[:, :], pool_in[l]).then_inc(ph_loaded, 16)
                with pool.Fori(0, BT) as h:
                    it = pool.snap(l * BT + h)
                    pool.wait_ge(ghist_out, it * 3 + 3)
                    settled(pool)
                    for j in range(3):
                        pool.wait_ge(gconv_step, it * (3 * GW) + GW * (j + 1))
                        settled(pool)
                        src = par[:, bass.ds(Q_GH + (it * 3 + j) * NS * (GW - 1), NS * (GW - 1))]
                        gp.tensor_copy(samples(gext[:, j, :], GW - 1 + T, GW, 0, GW - 1),
                                       src.rearrange("p (b k) -> p b k", k=GW - 1)).then_inc(ghist_in, 1)
                    for j in range(3):
                        pool.wait_ge(bank_free[j], l * BANK_USES + BK_G + h + 1 + BF)
                        pool.wait_ge(ghist_in, it * 3 + j + 1)
                        settled(pool)
                        at = H_G + (h * 3 + j) * (NS + 1) * (GW - 1)
                        gp.tensor_copy(hist[:, bass.ds(at, GW - 1)], gext[:, j, T:T + GW - 1])
                        gp.tensor_copy(hist[:, bass.ds(at + GW - 1, NS * (GW - 1))].rearrange("p (b k) -> p b k", k=GW - 1),
                                       samples(gext[:, j, :], GW - 1 + T, GW, 1, GW - 1)).then_inc(ghist_out, 1)
                pool.wait_ge(gqkv_ready, l * 4 * BT + 3 * BT)
                pool.wait_ge(ghist_out, (l + 1) * 3 * BT + 3)
                pool.wait_ge(hlo_ready, l * 2 * BT + 2 * BT)
                settled(pool)
                with pool.Fori(0, BT) as h:
                    it = pool.snap(l * BT + h)
                    for a in range(2):
                        src = gqkv[:, bass.ds((h * 3 + a) * N, N)]
                        last = gp.tensor_tensor(sq2[:, a, :], src, src, ALU.mult)
                    last.then_inc(gsq_ready, 1)
                    pool.wait_ge(unit_used, l * UNITS + RING + OFF_R)
                    settled(pool)
                    gp.tensor_copy(act_lo[:, bass.ds(h * 4, 4), :], y_lo[:, bass.ds(h * 4, 4), :]).then_inc(alo_copied, 1)
                    pool.wait_ge(grn_act, it + 1)
                    settled(pool)
                    for a in range(2):
                        src = gqkv[:, bass.ds((h * 3 + a) * N, N)]
                        last = gp.tensor_tensor(src, src, rn2[:, a, :], ALU.mult)
                    last.then_inc(gqn_ready, 1)
                with pool.Fori(0, BT) as h:
                    it = pool.snap(l * BT + h)
                    pool.dma_start(state[:, :, :], ret_in[l, :, h].rearrange("b d e -> d b e")).then_inc(state_loaded, 16)
                    pool.wait_ge(sconv_step, it * SW + SW)
                    pool.wait_ge(shist_out, it + 1)
                    settled(pool)
                    src = par[:, bass.ds(Q_SH + it * NS * (SW - 1), NS * (SW - 1))]
                    gp.tensor_copy(samples(sext[:, :], SW - 1 + T, SW, 0, SW - 1),
                                   src.rearrange("p (b k) -> p b k", k=SW - 1)).then_inc(shist_in, 1)
                    pool.wait_ge(bank_free[1], l * BANK_USES + BK_S + h + 1 + BF)
                    pool.wait_ge(shist_in, it + 1)
                    settled(pool)
                    at = H_S + h * (NS + 1) * (SW - 1)
                    gp.tensor_copy(hist[:, bass.ds(at, SW - 1)], sext[:, T:T + SW - 1])
                    gp.tensor_copy(hist[:, bass.ds(at + SW - 1, NS * (SW - 1))].rearrange("p (b k) -> p b k", k=SW - 1),
                                   samples(sext[:, :], SW - 1 + T, SW, 1, SW - 1)).then_inc(shist_out, 1)
                    pool.wait_ge(rst_ready, it + 1)
                    settled(pool)
                    pool.dma_start(p_ret[l, 0, h], pstate[:, 0, :]).then_inc(pstate_written, 16)
                    pool.wait_ge(pstate_written, (it + l * BT) * 16 + 16)
                    pool.sem_inc(pstate_free, 1)
                    pool.wait_ge(rstate_new, it * NS + NS)
                    settled(pool)
                    pool.dma_start(s_ret[l, :, h].rearrange("b d e -> d b e"), state[:, :, :]).then_inc(state_written, 16)
                    pool.wait_ge(ros_mm, it + 1)
                    pool.wait_ge(state_written, (it + l * BT) * 16 + 16)
                    settled(pool)
                pool.wait_ge(ph_loaded, l * 16 + 16)
                settled(pool)
                for g in range(BT):
                    it = pool.snap(l * BT + g)
                    pool.wait_ge(psum_step, it + 1)
                    pool.wait_ge(phist_out, it + 1)
                    settled(pool)
                    src = phist[:, g * NS * PH:(g + 1) * NS * PH]
                    gp.tensor_copy(samples(pext[:, :], PH + T, PH + 1, 0, PH),
                                   src.rearrange("p (b k) -> p b k", k=PH)).then_inc(phist_in, 1)
                    pool.wait_ge(bank_free[2 * (g % 2)], l * BANK_USES + BK_P + g // 2 + 1 + BF)
                    pool.wait_ge(phist_in, it + 1)
                    settled(pool)
                    at = H_P + g * (NS + 1) * PH
                    gp.tensor_copy(hist[:, at:at + PH], pext[:, T:T + PH])
                    gp.tensor_copy(hist[:, at + PH:at + PH + NS * PH].rearrange("p (b k) -> p b k", k=PH),
                                   samples(pext[:, :], PH + T, PH + 1, 1, PH)).then_inc(phist_out, 1)
                pool.wait_ge(phist_out, l * BT + BT + 1)
                settled(pool)
                pool.dma_start(hist_out[l], hist[:, :]).then_inc(hist_written, 16)
                pool.wait_ge(hist_written, l * 16 + 16)
                settled(pool)
                with pool.Fori(0, BT) as h:
                    it = pool.snap(l * BT + h)
                    pool.dma_start(state[:, :, :], gdn_in[l, :, h].rearrange("b d e -> d b e")).then_inc(state_loaded, 16)
                    pool.wait_ge(gcol_act, it * 2 + 2)
                    settled(pool)
                    for c in range(CH):
                        last = gp.tensor_tensor(decs[:, c, :], dec[:, c, :], strict, ALU.mult)
                    last.then_inc(gdecs_ready, 1)
                    pool.wait_ge(gE_ready, it + 1)
                    settled(pool)
                    for v in range(1, LEVELS):
                        if v > 2:
                            pool.wait_ge(gX_mm, it * 6 + v - 2)
                            settled(pool)
                        for c in range(CH):
                            last = gp.tensor_tensor(Em[:, v % 2, c * P:(c + 1) * P], E_[:, c, :],
                                                    con[:, C_LEV + v * P:C_LEV + (v + 1) * P], ALU.mult)
                        last.then_inc(gem_ready, 1)
                    pool.wait_ge(gstate_new, it * NS + NS)
                    settled(pool)
                    pool.dma_start(s_gdn[l, :, h].rearrange("b d e -> d b e"), state[:, :, :]).then_inc(state_written, 16)
                    pool.wait_ge(state_written, (it + l * BT) * 16 + 16 * BT + 16)
                    pool.wait_ge(gst_ready, it * 2 + 2)
                    settled(pool)
                    pool.dma_start(p_gdn[l, 0, h], pstate[:, 1, :]).then_inc(pstate_written, 16)
                    pool.wait_ge(pstate_written, (it + l * BT) * 16 + 16 * BT + 16)
                    pool.sem_inc(pstate_free, 1)
        @block.scalar
        def _(act):
            sc = nc.scalar

            def splitter(l, off, i, per):
                ub = act.snap(l * UNITS + off + i * per)
                rb = act.snap((l * (UNITS // RING) + off // RING + i * (per // RING)) * 16)

                def split(a, b):
                    for j in range(a, b):
                        s = j % RING
                        act.wait_ge(raw_loaded[s], rb + 16 * (j // RING + 1))
                        act.wait_ge(unit_used, ub + j + 1)
                        sc.activation(whi[:, s, :], raw[:, s, :], ACT.Copy).then_inc(hi_ready, 1)
                return ub, split

            def x_hi(n, k):
                sc.activation(tile_of(act_hi, k), tile_of(x, k), ACT.Copy, scale=col(par, Q_NG + n * KT + k)).then_inc(xhi_ready, 1)

            def x_square(k, buf, done):
                act.wait_ge(sq_added, done + 1)
                sc.activation(squares[:, buf, :], tile_of(x, k), ACT.Square).then_inc(sq_ready, 1)

            def inverse_rms(n):
                act.wait_ge(rms_ready, n + 1)
                sc.activation(rstd[:, :], rms[:, :], ACT.Sqrt).then_inc(rstd_ready, 1)

            act.wait_ge(par_loaded, 16)
            ub, split = splitter(0, 0, 0, 0)
            for q in range(4):
                if q == 0:
                    split(0, 1)
                act.wait_ge(x_loaded[q], 16)
                for k in range(4 * q, 4 * q + 4):
                    x_hi(0, k)
                if q < 2:
                    split(q + 1, q + 2)
            for q in (2, 3):
                sc.activation(quarter(wide, q), quarter(x, q), ACT.Square).then_inc(first_square_late, 1)
            with act.Fori(0, DEPTH) as l:
                def gdn_turn(h, first):
                    it = act.snap(l * BT + h)
                    ub, split = splitter(l, OFF_G, h, TURN)

                    def silu_out(j, back=0):
                        act.wait_ge(gconv_step, it * (3 * GW) + 3 * GW * (back + 1) + GW * (j + 1))
                        at = (h * 3 + j + 3 * back) * N
                        sc.activation(gqkv[:, bass.ds(at, T)], gconv[:, j, 0:T], ACT.Silu)
                        sc.activation(gqkv[:, bass.ds(at + T, NS)], gconv[:, j, GW - 1 + T:GC:GW], ACT.Silu).then_inc(gqkv_ready, 1)

                    if first:
                        split(3, 7)
                        inverse_rms(l)
                        split(7, 8)
                    else:
                        split(3, 5)
                        silu_out(2, -1)
                        split(5, 8)
                    def normed_hi(a):
                        act.wait_ge(h_ready, it * 2 + a + 1)
                        sc.activation(y_hi[:, bass.ds(h * 4 + 2 * a, 2), :], wide[:, bass.ds(h * 4 + 2 * a, 2), :],
                                      ACT.Copy).then_inc(hhi_ready, 1)

                    split(8, 10)
                    silu_out(0)
                    split(10, 13)
                    normed_hi(0)
                    split(13, 15)
                    silu_out(1)
                    split(15, 17)
                    normed_hi(1)
                    split(17, 19)

                gdn_turn(0, True)
                with act.Fori(0, BT - 1) as r:
                    gdn_turn(act.snap(r + 1), False)
                act.wait_ge(gconv_step, (l + 1) * BT * 3 * GW + 3 * GW)
                sc.activation(gqkv[:, (3 * BT - 1) * N:(3 * BT - 1) * N + T], gconv[:, 2, 0:T], ACT.Silu)
                sc.activation(gqkv[:, (3 * BT - 1) * N + T:3 * BT * N], gconv[:, 2, GW - 1 + T:GC:GW], ACT.Silu).then_inc(gqkv_ready, 1)

                act.wait_ge(con_loaded, 16)
                with act.Fori(0, BT) as h:
                    it = act.snap(l * BT + h)
                    ub, split = splitter(l, OFF_R, h, TURN)
                    split(3, 7)
                    act.wait_ge(unit_used, ub + RING)
                    sc.activation(act_hi[:, bass.ds(h * 4, 4), :], y_hi[:, bass.ds(h * 4, 4), :].bitcast(F32), ACT.Copy).then_inc(ahi_copied, 1)
                    split(7, 11)
                    act.wait_ge(bank_free[3], l * BANK_USES + BK_G + BT + BF)
                    sc.activation(gates[:, bass.ds(h, 1), :], gates[:, bass.ds(h, 1), :], ACT.Silu).then_inc(gqkv_ready, 1)
                    split(11, 15)
                    act.wait_ge(unit_used, ub + RING + UB * 3)
                    sc.activation(rqkv[:, bass.ds((h * 3 + 2) * N, N)], acc[2][:, 0:N], ACT.Copy).then_inc(bank_free[2], 1)
                    split(15, 17)
                    act.wait_ge(grn_step, it * 3 + 3)
                    sc.activation(rn2[:, :, :], rn2[:, :, :], ACT.Sqrt).then_inc(grn_act, 1)
                    split(17, 19)
                    act.wait_ge(unit_used, ub + RING + UB * 4)
                    sc.activation(wide[:, bass.ds(h + 3 * BT, 1), :], acc[3][:, 0:N], ACT.Silu).then_inc(bank_free[3], 1)

                with act.Fori(0, BT) as h:
                    it = act.snap(l * BT + h)
                    ub, split = splitter(l, OFF_S, h, TURN)
                    act.wait_ge(rope_step, it * 6 + 6)
                    act.wait_ge(bank_free[2], l * BANK_USES + BK_R + BT + BF)
                    sc.activation(head[:, :, :].rearrange("p a n -> p (a n)"), rqkv[:, bass.ds(h * 3 * N, 3 * N)],
                                  ACT.Copy).then_inc(head_copied, 1)
                    split(3, 7)
                    act.wait_ge(rtr_mm, it + 1)
                    for c in range(CH):
                        sc.activation(kd[:, c, :], side[1][:, c * P:(c + 1) * P], ACT.Copy, scale=col(con, C_GDEC + h * CH + c))
                    sc.activation(vt[:, :, :].rearrange("p c d -> p (c d)"), side[1][:, T:2 * T], ACT.Copy).then_inc(kdvt_ready, 1)
                    act.wait_ge(unit_used, ub + RING + UB)
                    sc.activation(sc_c[:, :], acc[0][:, 0:N], ACT.Copy).then_inc(bank_free[0], 1)
                    split(7, 9)
                    act.wait_ge(state_loaded, (it + l * BT) * 16 + 16)
                    sc.activation(state[:, :, :].rearrange("p b e -> p (b e)"), state[:, :, :].rearrange("p b e -> p (b e)"),
                                  ACT.Copy, scale=col(con, C_GAM + h)).then_inc(rdecayed, 1)
                    split(9, 15)
                    act.wait_ge(ros_mm, it + 1)
                    sc.activation(osb[:, :], side[2][:, 0:N], ACT.Copy)
                    sc.activation(osq[:, :], side[2][:, 0:N], ACT.Square).then_inc(ro_copied, 1)
                    split(15, 18)
                    act.wait_ge(ro_step, it * 4 + 2)
                    sc.activation(oms[:, :], orc[:, :], ACT.Sqrt).then_inc(rors_ready, 1)
                    split(18, 19)
                    act.wait_ge(unit_used, ub + RING + UB * 4)
                    sc.activation(sgate[:, :], acc[3][:, 0:N], ACT.Silu).then_inc(bank_free[3], 1)
                    act.wait_ge(ro_step, it * 4 + 4)
                    sc.activation(y_hi[:, bass.ds(h + YT[RET], 1), :], y32[:, 0, :], ACT.Copy).then_inc(ryhi, 1)
                    act.wait_ge(sy_ready, it + 1)
                    sc.activation(y_hi[:, bass.ds(h + YT[SCV], 1), :], y32[:, 1, :], ACT.Copy).then_inc(syhi, 1)

                for g in range(BT):
                    it = l * BT + g
                    ub, split = splitter(l, OFF_P, g, PTURN)
                    b0 = 2 * (g % 2)
                    split(3, 7)
                    act.wait_ge(unit_used, ub + RING + UB)
                    act.wait_ge(phist_out, it + 1)
                    act.wait_ge(psum_step, it + 1)
                    sc.activation(pext[:, PH:PH + T], acc[b0][:, 0:T], ACT.Copy)
                    sc.activation(samples(pext[:, :], PH + T, PH + 1, PH), acc[b0][:, T:N], ACT.Copy).then_inc(bank_free[b0], 1)
                    if g == 0:
                        act.wait_ge(ab_step, l * 15 + 1)
                        sc.activation(ab_abs[:, :], ab_x[:, :], ACT.Abs).then_inc(ab_act, 1)
                        act.wait_ge(ab_act, l * 4 + 1)
                        sc.activation(ab_e[:, :], ab_abs[:, :], ACT.Exp, scale=-1.0).then_inc(ab_act, 1)
                        sc.activation(ab_ea[:, :], par[:, bass.ds(Q_AL + l * A3, A3)], ACT.Exp).then_inc(ab_act, 1)
                        sc.activation(beta[:, :].rearrange("p (c h) -> p c h", h=BT),
                                      ab[:, :].rearrange("p (c t h) -> p c t h", t=2, h=BT)[:, :, 1, :],
                                      ACT.Sigmoid).then_inc(ab_act, 1)
                    split(7, 11)
                    act.wait_ge(unit_used, ub + RING + UB * 2)
                    act.wait_ge(py_ready, it + 1)
                    sc.activation(pgate[:, :], acc[b0 + 1][:, 0:N], ACT.Silu).then_inc(bank_free[b0 + 1], 1)
                    act.wait_ge(py_ready, it + 2)
                    sc.activation(y_hi[:, YT[POOL] + g, :], y32[:, 1, :], ACT.Copy).then_inc(pyhi, 1)

                act.wait_ge(phist_out, l * BT + BT + 1)
                settled(act)
                with act.Fori(0, BT) as h:
                    it = act.snap(l * BT + h)
                    ub, split = splitter(l, OFF_M, h, MTURN)
                    mb = act.snap(l * 4 * KT + h * 12)
                    fb = act.snap(l * BANK_USES + BK_M + h * 6)

                    def units(a, b):
                        for j in range(a, b):
                            split(j + 3, j + 4)
                            if j % MB == MB - 1:
                                i = j // MB
                                p = i % 2
                                act.wait_ge(unit_used, ub + RING + MB * i + UB)
                                act.wait_ge(bank_free[2 * p + 1], fb + i // 2 + BF)
                                sc.activation(msig[:, p, :], acc[2 * p][:, 0:N], ACT.Sigmoid).then_inc(bank_free[2 * p], 1)

                    act.wait_ge(gqn_ready, l * BT + BT)
                    sc.activation(head[:, :, :].rearrange("p a n -> p (a n)"), gqkv[:, bass.ds(h * 3 * N, 3 * N)],
                                  ACT.Copy).then_inc(gv_ready, 1)
                    units(0, 3)
                    act.wait_ge(grow_mm, it + 1)
                    sc.activation(b_row[:, :], side[2][:, 0:BR], ACT.Copy).then_inc(grow_ready, 1)
                    sc.activation(eb_row[:, 0:N], side[2][:, 0:N], ACT.Exp).then_inc(grow_ready, 1)
                    act.wait_ge(gvt_mm, it + 1)
                    sc.activation(vt[:, :, :].rearrange("p c d -> p (c d)"), side[3][:, 0:T], ACT.Copy).then_inc(kdvt_ready, 1)
                    units(3, 4)
                    act.wait_ge(gcol_step, it * 2 + 2)
                    sc.activation(hcol[:, 2:4], hcol[:, 0:2], ACT.Exp)
                    sc.activation(hcol[:, 6:8], hcol[:, 4:6], ACT.Exp).then_inc(gcol_act, 1)
                    sc.activation(dec[:, :, :].rearrange("p c d -> p (c d)"), dec[:, :, :].rearrange("p c d -> p (c d)"),
                                  ACT.Exp).then_inc(gcol_act, 1)
                    units(4, KQ0)
                    act.wait_ge(gkt_mm, it + 1)
                    act.wait_ge(gcol_act, it * 2 + 1)
                    for c in range(CH):
                        last = sc.activation(kd[:, c, :], side[1][:, c * P:(c + 1) * P], ACT.Copy, scale=hcol[:, 6 + c:7 + c])
                    last.then_inc(gkd_ready, 1)
                    units(KQ0, KQ0 + 3)
                    act.wait_ge(gT_mm, it + 1)
                    sc.activation(TR[:, 0, :, :].rearrange("p c d -> p (c d)"), side[0][:, 0:T], ACT.Copy).then_inc(gT_ready, 1)
                    units(KQ0 + 3, LEV0)
                    at = LEV0
                    for v in range(1, LEVELS):
                        act.wait_ge(gX_mm, it * 6 + v)
                        sc.activation(Xs[:, :, :].rearrange("p c d -> p (c d)"), side[0][:, 0:T], ACT.Copy).then_inc(gX_ready, 1)
                        if v in (2, 4):
                            act.wait_ge(grow_ready, it * 2 + 2)
                            act.wait_ge(gdl_mm, it * 3 + 1)
                            for b in range(2 * v - 4, 2 * v):
                                last = sc.activation(state[:, b, :], state[:, b, :], ACT.Copy, scale=eb_row[:, T + b:T + b + 1])
                            last.then_inc(gdecayed, 1)
                        units(at, at + LEVU)
                        at += LEVU
                    act.wait_ge(gsol_mm, it * 2 + 1)
                    sc.activation(vn[:, 0, :], side[2][:, 0:P], ACT.Copy, scale=bet2[:, 0:1]).then_inc(gvn_ready, 1)
                    units(at, 49)
                    act.wait_ge(gsol_mm, it * 2 + 2)
                    sc.activation(vn[:, 1, :], side[2][:, 0:P], ACT.Copy, scale=bet2[:, 1:2]).then_inc(gvn_ready, 1)
                    units(49, 52)
                    act.wait_ge(go_mm, it + 1)
                    sc.activation(osb[:, 0:T], side[0][:, 0:T], ACT.Copy).then_inc(go_copied, 1)
                    act.wait_ge(go_copied, it * 2 + 1)
                    act.wait_ge(gos_copied, it + 1)
                    sc.activation(osq[:, :], osb[:, :], ACT.Square).then_inc(go_copied, 1)
                    units(52, 57)
                    act.wait_ge(go_step, it * 4 + 2)
                    sc.activation(oms[:, :], orc[:, :], ACT.Sqrt).then_inc(gors_ready, 1)
                    units(57, 59)
                    act.wait_ge(go_step, it * 4 + 4)
                    sc.activation(y_hi[:, bass.ds(h + YT[GDN], 1), :], y32[:, 0, :], ACT.Copy).then_inc(gyhi, 1)
                    units(59, 60)

                def merged_hi(k):
                    act.wait_ge(merged_ready, l * 3 * KT + 2 * KT + k + 1)
                    sc.activation(tile_of(y_hi, k), tile_of(wide, k), ACT.Copy).then_inc(mhi_ready, 1)

                def gdn_merge_turn(h, last):
                    ub, split = splitter(l, OFF_X, h, XTURN)
                    fb = act.snap(l * BANK_USES + BK_X + h * 2)
                    for i in range(4):
                        p = i % 2
                        split(MB * i + 3 + (i > 0), MB * i + 8)
                        act.wait_ge(unit_used, ub + RING + MB * i + UB)
                        act.wait_ge(bank_free[2 * p + 1], fb + i // 2 + BF)
                        sc.activation(msig[:, p, :], acc[2 * p][:, 0:N], ACT.Sigmoid).then_inc(bank_free[2 * p], 1)
                        if i < 3:
                            split(MB * i + 8, MB * i + 9)
                        if not last:
                            merged_hi(act.snap(h * 4 + i))

                with act.Fori(0, BT - 1) as h:
                    gdn_merge_turn(h, False)
                gdn_merge_turn(BT - 1, True)
                act.wait_ge(unit_used, l * UNITS + RING + OFF_O)
                for k in range(KT - 4, KT):
                    merged_hi(k)

                with act.Fori(0, BT) as h:
                    ub, split = splitter(l, OFF_O, h, TURN)
                    for i in range(4):
                        split(4 * i + 3, 4 * i + 7)
                        k = act.snap(h * 4 + i)
                        act.wait_ge(x_updated, l * KT + h * 4 + i + 1)
                        x_square(k, i % 2, l * KT + h * 4 + i)
                        x_hi(l + 1, k)
            inverse_rms(DEPTH)

        @block.vector
        def _(dve):
            ve = nc.vector

            def splitter(l, off, i, per):
                ub = dve.snap(l * UNITS + off + i * per)

                def split(a, b):
                    for j in range(a, b):
                        s = j % RING
                        dve.wait_ge(hi_ready, ub + j + 1)
                        ve.tensor_tensor(wlo[:, s, :], raw[:, s, :], whi[:, s, :].bitcast(F32), ALU.subtract).then_inc(lo_ready, 1)
                return ub, split

            def x_added(buf, done):
                dve.wait_ge(sq_ready, done + 1)
                dve.wait_ge(sq_added, done + 2)
                ve.tensor_tensor(sq_sum[:, :], sq_sum[:, :], squares[:, buf, :], ALU.add).then_inc(sq_added, 1)

            def x_lo(n, k, done):
                dve.wait_ge(xhi_ready, done + 1)
                ve.scalar_tensor_tensor(out=tile_of(act_lo, k), in0=tile_of(x, k), scalar=col(par, Q_NG + n * KT + k),
                                        in1=tile_of(act_hi, k).bitcast(F32), op0=ALU.mult, op1=ALU.subtract).then_inc(xlo_ready, 1)

            def mean_square(n):
                dve.wait_ge(norm_mm, n + 1)
                ve.tensor_scalar(ms[:, :], side[0][:, 0:N], 1.0 / D_MODEL, EPS, ALU.mult, ALU.add).then_inc(ms_ready, 1)
                dve.wait_ge(ms_ready, n + 1)
                ve.reciprocal(rms[:, :], ms[:, :]).then_inc(rms_ready, 1)

            def normed(n, k):
                return ve.scalar_tensor_tensor(out=tile_of(wide, k), in0=tile_of(x, k), scalar=col(par, Q_NG + n * KT + k),
                                               in1=rstd[:, :], op0=ALU.mult, op1=ALU.mult)

            dve.wait_ge(par_loaded, 16)
            ub, split = splitter(0, 0, 0, 0)
            for q in range(4):
                if q == 0:
                    split(0, 1)
                dve.wait_ge(x_loaded[q], 16)
                for k in range(4 * q, 4 * q + 4):
                    x_lo(0, k, k)
                if q < 2:
                    split(q + 1, q + 2)
            dve.wait_ge(first_square_late, 2)
            ve.tensor_tensor(quarter(wide, 2), quarter(wide, 2), quarter(wide, 3), ALU.add).then_inc(first_sum, 1)
            dve.wait_ge(first_square, 3)
            dve.wait_ge(first_sum, 1)
            ve.tensor_tensor(quarter(wide, 0), quarter(wide, 0), quarter(wide, 2), ALU.add).then_inc(first_sum, 1)
            dve.wait_ge(first_sum, 2)
            ve.tensor_tensor(quarter(wide, 0, 2), quarter(wide, 0, 2), wide[:, 2:4, :].rearrange("p a n -> p (a n)"), ALU.add).then_inc(first_sum, 1)
            dve.wait_ge(first_sum, 3)
            ve.tensor_tensor(sq_sum[:, :], wide[:, 0, :], wide[:, 1, :], ALU.add).then_inc(first_sum, 1)
            with dve.Fori(0, DEPTH) as l:
                def gdn_turn(h, first):
                    it = dve.snap(l * BT + h)
                    ub, split = splitter(l, OFF_G, h, TURN)
                    split(3, 7)
                    if first:
                        mean_square(l)
                    if first:
                        dve.wait_ge(zeros_set, l + 2)
                        dve.wait_ge(rstd_ready, l + 1)

                    def normed_lo(a):
                        dve.wait_ge(hhi_ready, it * 2 + a + 1)
                        ve.tensor_tensor(y_lo[:, bass.ds(h * 4 + 2 * a, 2), :], wide[:, bass.ds(h * 4 + 2 * a, 2), :],
                                         y_hi[:, bass.ds(h * 4 + 2 * a, 2), :].bitcast(F32), ALU.subtract).then_inc(hlo_ready, 1)

                    for j in range(3):
                        dve.wait_ge(unit_used, ub + RING + UB * (j + 1))
                        dve.wait_ge(ghist_out, it * 3 + j + 1)
                        ve.tensor_tensor(gext[:, j, GW - 1:GW - 1 + T], acc[j][:, 0:T], rstd[:, 0:T], ALU.mult)
                        ve.tensor_tensor(samples(gext[:, j, :], GW - 1 + T, GW, GW - 1), acc[j][:, T:N], rstd[:, T:N],
                                         ALU.mult).then_inc(bank_free[j], 1)
                        split(7 + 4 * j, 8 + 4 * j)
                        dve.wait_ge(bank_free[j], l * BANK_USES + BK_G + h + 1 + BF)
                        dve.wait_ge(ghist_in, it * 3 + j + 1)
                        tap = Q_GCW + (it * 3 + j) * GW
                        ve.tensor_scalar(gconv[:, j, :], gext[:, j, 0:GC], col(par, tap), None, ALU.mult).then_inc(gconv_step, 1)
                        for k in range(1, GW):
                            dve.wait_ge(gconv_step, it * (3 * GW) + 3 * GW + GW * j + k)
                            ve.scalar_tensor_tensor(out=gconv[:, j, :], in0=gext[:, j, k:k + GC], scalar=col(par, tap + k),
                                                    in1=gconv[:, j, :], op0=ALU.mult, op1=ALU.add).then_inc(gconv_step, 1)
                            split(7 + 4 * j + k, 8 + 4 * j + k)
                            if j == 2 and k == 1:
                                normed_lo(0)
                        if j < 2:
                            normed(l, dve.snap(h * 4 + 2 * j))
                            normed(l, dve.snap(h * 4 + 2 * j + 1)).then_inc(h_ready, 1)
                        else:
                            normed_lo(1)
                    dve.wait_ge(unit_used, ub + RING + UB * 4)
                    ve.tensor_tensor(tile_of(gates, h), acc[3][:, 0:N], rstd[:, :], ALU.mult).then_inc(bank_free[3], 1)

                gdn_turn(0, True)
                with dve.Fori(0, BT - 1) as r:
                    gdn_turn(dve.snap(r + 1), False)

                def rotate(out, a, table, scale):
                    return ve.scalar_tensor_tensor(out=out, in0=a, scalar=scale, in1=table, op0=ALU.mult, op1=ALU.mult)

                dve.wait_ge(con_loaded, 16)
                dve.wait_ge(ab_mm, l * 3 + 3)
                dve.wait_ge(zeros_set, 1)
                settled(dve)
                ve.tensor_copy(ab[:, 0:4 * BT], side[1][:, 0:4 * BT])
                ve.tensor_copy(ab[0:NS, 4 * BT:6 * BT], side[1][0:NS, 4 * BT:6 * BT]).then_inc(ab_evac, 1)

                with dve.Fori(0, BT) as h:
                    it = dve.snap(l * BT + h)
                    ub, split = splitter(l, OFF_R, h, TURN)
                    split(3, 7)
                    for j, scale in enumerate((1.0, float(P) ** -0.5)):
                        dve.wait_ge(unit_used, ub + RING + UB * (j + 1))
                        rotate(rope_a[:, j, :], acc[j][:, 0:N], con[:, C_COS:C_COS + N], scale).then_inc(rope_step, 1)
                        rotate(rope_b[0:64, j, :], acc[j][64:P, 0:N], con[64:P, C_SIN:C_SIN + N], scale).then_inc(rope_step, 1)
                        rotate(rope_b[64:P, j, :], acc[j][0:64, 0:N], con[0:64, C_SIN:C_SIN + N], scale).then_inc(bank_free[j], 1)
                        dve.wait_ge(bank_free[j], l * BANK_USES + BK_R + h + 1 + BF)
                        ve.tensor_tensor(rqkv[:, bass.ds((h * 3 + j) * N, N)], rope_a[:, j, :], rope_b[:, j, :], ALU.add).then_inc(rope_step, 1)
                        split(7 + 4 * j, 9 + 4 * j)
                        if j == 0:
                            dve.wait_ge(gn_mm, it + 1)
                            ve.tensor_scalar(rn2[:, 0, :], side[2][:, 0:N], EPS, float(P), ALU.add, ALU.mult)
                            ve.tensor_scalar(rn2[:, 1, :], side[3][:, 0:N], EPS, None, ALU.add).then_inc(grn_step, 1)
                            split(9, 10)
                            dve.wait_ge(grn_step, it * 3 + 1)
                        ve.reciprocal(rn2[:, j, :], rn2[:, j, :]).then_inc(grn_step, 1)
                        split(10 - j + 4 * j, 11 + 4 * j)
                    split(15, 19)

                with dve.Fori(0, BT) as h:
                    it = dve.snap(l * BT + h)
                    ub, split = splitter(l, OFF_S, h, TURN)
                    split(3, 6)
                    dve.wait_ge(rsc_mm, it + 1)
                    ve.tensor_tensor(scores[:, 0:T], side[0][:, 0:T], con[:, bass.ds(C_DM + h * T, T)], ALU.mult)
                    ve.tensor_tensor(scores[:, T:T + P], side[0][:, T:T + P], con[:, bass.ds(C_DM + h * T, P)], ALU.mult).then_inc(scores_ready, 1)
                    split(6, 9)
                    dve.wait_ge(rst_mm, it + 1)
                    dve.wait_ge(pstate_free, it + l * BT + 1)
                    ve.tensor_copy(pstate[:, 0, :], side[3][:, 0:P]).then_inc(rst_ready, 1)
                    split(9, 11)
                    dve.wait_ge(unit_used, ub + RING + UB * 2)
                    dve.wait_ge(bank_free[0], l * BANK_USES + BK_S + h + 1 + BF)
                    dve.wait_ge(shist_out, it + 1)
                    ve.tensor_tensor(sext[:, SW - 1:SW - 1 + T], acc[1][:, 0:T], sc_c[:, 0:T], ALU.mult)
                    ve.tensor_tensor(samples(sext[:, :], SW - 1 + T, SW, SW - 1), acc[1][:, T:N], sc_c[:, T:N], ALU.mult).then_inc(bank_free[1], 1)
                    dve.wait_ge(rvb_mm, it + 1)
                    dve.wait_ge(rdecayed, it + 1)
                    for b in range(NS):
                        ve.scalar_tensor_tensor(out=state[:, b, :], in0=side[b // 4][:, (b % 4) * P:(b % 4 + 1) * P],
                                                scalar=head[:, 1, T + b:T + b + 1], in1=state[:, b, :],
                                                op0=ALU.mult, op1=ALU.add).then_inc(rstate_new, 1)
                    split(11, 13)
                    dve.wait_ge(bank_free[1], l * BANK_USES + BK_S + h + 1 + BF)
                    dve.wait_ge(shist_in, it + 1)
                    tap = Q_SCW + it * SW
                    ve.tensor_scalar(sconv[:, :], sext[:, 0:SC], col(par, tap), None, ALU.mult).then_inc(sconv_step, 1)
                    for k in range(1, SW):
                        dve.wait_ge(sconv_step, it * SW + SW + k)
                        ve.scalar_tensor_tensor(out=sconv[:, :], in0=sext[:, k:k + SC], scalar=col(par, tap + k),
                                                in1=sconv[:, :], op0=ALU.mult, op1=ALU.add).then_inc(sconv_step, 1)
                    split(13, 17)
                    dve.wait_ge(rss_mm, it + 1)
                    ve.tensor_scalar(oms[:, :], side[3][:, 0:N], 1.0 / P, EPS, ALU.mult, ALU.add).then_inc(ro_step, 1)
                    dve.wait_ge(ro_step, it * 4 + 1)
                    ve.reciprocal(orc[:, :], oms[:, :]).then_inc(ro_step, 1)
                    dve.wait_ge(sconv_step, it * SW + 2 * SW)
                    dve.wait_ge(unit_used, ub + RING + UB * 3)
                    ve.tensor_tensor(sprod[:, 0:T], acc[2][:, 0:T], sconv[:, 0:T], ALU.mult)
                    ve.tensor_tensor(sprod[:, T:N], acc[2][:, T:N], sconv[:, SW - 1 + T:SC:SW], ALU.mult).then_inc(bank_free[2], 1)
                    split(17, 19)
                    dve.wait_ge(rors_ready, it + 1)
                    ve.tensor_tensor(orc[:, :], osb[:, :], oms[:, :], ALU.mult).then_inc(ro_step, 1)
                    dve.wait_ge(ro_step, it * 4 + 3)
                    ve.tensor_tensor(y32[:, 0, :], orc[:, :], wide[:, bass.ds(h + 3 * BT, 1), :].rearrange("p a n -> p (a n)"),
                                     ALU.mult).then_inc(ro_step, 1)
                    dve.wait_ge(bank_free[3], l * BANK_USES + BK_S + h + 1 + BF)
                    dve.wait_ge(bank_free[2], l * BANK_USES + BK_S + h + 1 + BF)
                    ve.tensor_tensor(y32[:, 1, :], sprod[:, :], sgate[:, :], ALU.mult).then_inc(sy_ready, 1)
                    dve.wait_ge(ryhi, it + 1)
                    ve.tensor_tensor(y_lo[:, bass.ds(h + YT[RET], 1), :], y32[:, 0, :],
                                     y_hi[:, bass.ds(h + YT[RET], 1), :].bitcast(F32), ALU.subtract).then_inc(y_ready[RET], 1)
                    dve.wait_ge(syhi, it + 1)
                    ve.tensor_tensor(y_lo[:, bass.ds(h + YT[SCV], 1), :], y32[:, 1, :],
                                     y_hi[:, bass.ds(h + YT[SCV], 1), :].bitcast(F32), ALU.subtract).then_inc(y_ready[SCV], 1)

                nth = [0]

                def link(op):
                    nth[0] += 1
                    op.then_inc(ab_step, 1)
                    dve.wait_ge(ab_step, l * 15 + nth[0])

                def ab_sum():
                    link(ve.tensor_tensor(ab_x[:, :].rearrange("p (c h) -> p c h", h=BT),
                                          ab[:, :].rearrange("p (c t h) -> p c t h", t=2, h=BT)[:, :, 0, :],
                                          par[:, bass.ds(Q_DT + l * A3, A3)].rearrange("p (c h) -> p c h", h=BT), ALU.add))
                    ve.tensor_scalar(ab_relu[:, :], ab_x[:, :], 0.0, None, ALU.max)

                def ab_atanh_argument():
                    dve.wait_ge(ab_act, l * 4 + 2)
                    link(ve.tensor_scalar(ab_den[:, :], ab_e[:, :], 2.0, None, ALU.add))
                    link(ve.reciprocal(ab_rec[:, :], ab_den[:, :]))
                    link(ve.tensor_tensor(ab_s[:, :], ab_e[:, :], ab_rec[:, :], ALU.mult))
                    link(ve.tensor_tensor(ab_s2[:, :], ab_s[:, :], ab_s[:, :], ALU.mult))
                    link(ve.tensor_scalar(ab_q[:, :], ab_s2[:, :], 1.0 / 15, None, ALU.mult))

                def ab_series():
                    for d in (13, 11, 9, 7, 5, 3):
                        link(ve.scalar_tensor_tensor(out=ab_q[:, :], in0=ab_q[:, :], scalar=1.0 / d, in1=ab_s2[:, :],
                                                     op0=ALU.add, op1=ALU.mult))

                def ab_gate():
                    link(ve.scalar_tensor_tensor(out=ab_q[:, :], in0=ab_q[:, :], scalar=1.0, in1=ab_s[:, :],
                                                 op0=ALU.add, op1=ALU.mult))
                    link(ve.scalar_tensor_tensor(out=ab_sp[:, :], in0=ab_q[:, :], scalar=2.0, in1=ab_relu[:, :],
                                                 op0=ALU.mult, op1=ALU.add))
                    dve.wait_ge(ab_act, l * 4 + 4)
                    link(ve.scalar_tensor_tensor(out=g_col[:, :], in0=ab_sp[:, :], scalar=-1.0, in1=ab_ea[:, :],
                                                 op0=ALU.mult, op1=ALU.mult))
                    assert nth[0] == 15

                for g in range(BT):
                    it = l * BT + g
                    ub, split = splitter(l, OFF_P, g, PTURN)
                    split(3, 7)
                    (ab_sum, ab_atanh_argument, ab_series, ab_gate)[g]()
                    dve.wait_ge(bank_free[2 * (g % 2)], l * BANK_USES + BK_P + g // 2 + 1 + BF)
                    dve.wait_ge(phist_in, it + 1)
                    src, w, steps = pext, 1, 0
                    for v in range(g + 1):
                        dst = (psum_a, psum_b)[v % 2]
                        lo = 2 * w - 1
                        ve.tensor_tensor(dst[:, lo:PE_], src[:, lo:PE_], src[:, lo - w:PE_ - w], ALU.add).then_inc(pwin, 1)
                        steps += 1
                        dve.wait_ge(pwin, l * PWIN + PWIN_AT[g] + steps)
                        src, w = dst, 2 * w
                    ve.tensor_tensor(src[:, PH:PH + 16], src[:, PH:PH + 16], con[:, C_CORR + 16 * g:C_CORR + 16 * g + 16],
                                     ALU.mult).then_inc(pwin, 1)
                    dve.wait_ge(pwin, l * PWIN + PWIN_AT[g] + steps + 1)
                    ve.scalar_tensor_tensor(out=pdiff[:, 0:T], in0=src[:, PH:PH + T], scalar=1.0 / w, in1=pext[:, PH:PH + T],
                                            op0=ALU.mult, op1=ALU.subtract)
                    ve.scalar_tensor_tensor(out=pdiff[:, T:N], in0=samples(src[:, :], PH + T, PH + 1, PH), scalar=1.0 / w,
                                            in1=samples(pext[:, :], PH + T, PH + 1, PH),
                                            op0=ALU.mult, op1=ALU.subtract).then_inc(psum_step, 1)
                    split(7, 11)
                    dve.wait_ge(pmix_mm, it + 1 + BT)
                    dve.wait_ge(bank_free[2 * (g % 2) + 1], l * BANK_USES + BK_P + g // 2 + 1 + BF)
                    ve.scalar_tensor_tensor(out=y32[:, 1, :], in0=side[0][:, 0:N], scalar=col(par, Q_PSC + it), in1=pgate[:, :],
                                            op0=ALU.mult, op1=ALU.mult).then_inc(py_ready, 1)
                    dve.wait_ge(pyhi, it + 1)
                    ve.tensor_tensor(y_lo[:, YT[POOL] + g, :], y32[:, 1, :], y_hi[:, YT[POOL] + g, :].bitcast(F32),
                                     ALU.subtract).then_inc(y_ready[POOL], 1)

                dve.wait_ge(bcol_mm, l + 1)
                ve.tensor_copy(b_col[:, :], side[1][:, 0:CH * BT]).then_inc(bcol_ready, 1)
                dve.wait_ge(bcol_ready, l + 1)

                def merge_block(ub, i, p, first, m):
                    dve.wait_ge(unit_used, ub + RING + MB * (i + 1))
                    dve.wait_ge(bank_free[2 * p], bank_now[0] + i // 2 + 1 + BF)
                    dst = wide[:, bass.ds(m, 1), :]
                    if first:
                        ve.tensor_tensor(dst, msig[:, p, :], acc[2 * p + 1][:, 0:N], ALU.mult).then_inc(bank_free[2 * p + 1], 1)
                    else:
                        ve.tensor_tensor(mprod[:, p, :], msig[:, p, :], acc[2 * p + 1][:, 0:N], ALU.mult).then_inc(bank_free[2 * p + 1], 1)
                        dve.wait_ge(bank_free[2 * p + 1], bank_now[0] + i // 2 + 1 + BF)
                        ve.tensor_tensor(dst, dst, mprod[:, p, :], ALU.add).then_inc(merged_ready, 1)

                bank_now = [None]

                dve.wait_ge(phist_out, l * BT + BT + 1)
                settled(dve)
                with dve.Fori(0, BT) as h:
                    it = dve.snap(l * BT + h)
                    ub, split = splitter(l, OFF_M, h, MTURN)
                    bank_now[0] = dve.snap(l * BANK_USES + BK_M + h * 6)

                    def units(a, b):
                        for j in range(a, b):
                            split(j + 3, j + 4)
                            if j % MB == MB - 1:
                                i = j // MB
                                merge_block(ub, i, i % 2, i % 3 == 0, h * 4 + i // 3)

                    for c in range(3):
                        ve.tensor_copy(g_bc[:, c, :], col(g_col, h + c * BT).to_broadcast([P, P]))
                    ve.tensor_copy(beta_bc[:, :], col(beta, h + 2 * BT).to_broadcast([P, P]))
                    for c in range(CH):
                        ve.tensor_copy(hcol[:, c:c + 1], col(b_col, h + c * BT))
                        last = ve.tensor_copy(bet2[:, c:c + 1], col(beta, h + c * BT))
                    last.then_inc(gbc_ready, 1)
                    units(0, 3)
                    dve.wait_ge(grow_ready, it * 2 + 1)
                    dve.wait_ge(gbc_ready, it + 1)
                    for c in range(CH):
                        ve.scalar_tensor_tensor(out=dec[:, c, :], in0=b_row[:, c * P:(c + 1) * P], scalar=hcol[:, c:c + 1], in1=neg,
                                                op0=ALU.subtract, op1=ALU.add)
                    for c in range(CH):
                        ve.tensor_tensor(hcol[:, 4 + c:5 + c], b_row[:, c * P + P - 1:c * P + P], hcol[:, c:c + 1],
                                         ALU.subtract).then_inc(gcol_step, 1)
                    units(3, 5)
                    dve.wait_ge(gcol_act, it * 2 + 1)
                    ve.tensor_scalar(nebc[:, :], hcol[:, 2:4], -1.0, None, ALU.mult)
                    dve.wait_ge(gv_ready, it + 1)
                    dve.wait_ge(grow_ready, it * 2 + 2)
                    ve.tensor_tensor(kb[:, :], b_row[:, N:BR], head[:, 1, T:N], ALU.mult)
                    ve.tensor_tensor(qd[:, :], head[:, 0, P:T], eb_row[:, P:T], ALU.mult).then_inc(gqd_ready, 1)
                    units(5, KQ0)
                    dve.wait_ge(gkq_mm, it + 1)
                    dve.wait_ge(gdecs_ready, it + 1)
                    for c in range(CH):
                        last = ve.scalar_tensor_tensor(out=E_[:, c, :], in0=side[0][:, c * P:(c + 1) * P], scalar=bet2[:, c:c + 1],
                                                       in1=decs[:, c, :], op0=ALU.mult, op1=ALU.mult)
                    last.then_inc(gE_ready, 1)
                    ve.tensor_tensor(attn[:, :, :].rearrange("p c d -> p (c d)"), side[0][:, T:2 * T],
                                     dec[:, :, :].rearrange("p c d -> p (c d)"), ALU.mult).then_inc(gattn_ready, 1)
                    dve.wait_ge(gE_ready, it + 1)
                    for c in range(CH):
                        last = ve.tensor_tensor(Xs[:, c, :], E_[:, c, :], con[:, C_LEV:C_LEV + P], ALU.mult)
                    last.then_inc(gR_ready, 1)
                    dve.wait_ge(gR_ready, it * 2 + 1)
                    for c in range(CH):
                        last = ve.tensor_tensor(TR[:, 1, c, :], ident, Xs[:, c, :], ALU.subtract)
                    last.then_inc(gR_ready, 1)
                    units(KQ0, LEV0)
                    at = LEV0
                    for v in range(1, LEVELS):
                        if v in (3, 5):
                            dve.wait_ge(gdecayed, it * 2 + v // 2)
                            dve.wait_ge(gdl_mm, it * 3 + 1 + v // 2)
                            for b in range(2 * v - 6, 2 * v - 2):
                                ve.scalar_tensor_tensor(out=state[:, b, :], in0=side[3][:, (b % 4) * P:(b % 4 + 1) * P],
                                                        scalar=kb[:, b:b + 1], in1=state[:, b, :],
                                                        op0=ALU.mult, op1=ALU.add).then_inc(gstate_new, 1)
                        if v == 3:
                            dve.wait_ge(gos_mm, it + 1)
                            dve.wait_ge(gdelta_ready, it + 1)
                            ve.tensor_tensor(mk[:, :], side[2][:, 0:NS], sdelta[:, :], ALU.mult).then_inc(gsam_step, 1)
                            dve.wait_ge(gsam_step, it * 3 + 3)
                            ve.tensor_tensor(osb[:, T:N], osb[:, T:N], mk[:, :], ALU.add).then_inc(gos_copied, 1)
                        units(at, at + 2)
                        if v == 1:
                            dve.wait_ge(gdl_mm, it * 3 + 1)
                            ve.tensor_tensor(mk[:, :], side[3][:, 1:2 * NS:2], eb_row[:, T:N], ALU.mult).then_inc(gsam_step, 1)
                            ve.tensor_tensor(osb[:, T:N], side[3][:, 0:2 * NS:2], eb_row[:, T:N], ALU.mult).then_inc(gsam_step, 1)
                            ve.tensor_tensor(qkb[:, :], head[:, 0, T:N], kb[:, :], ALU.mult)
                            dve.wait_ge(gsam_step, it * 3 + 1)
                            ve.tensor_tensor(sdelta[:, :], head[:, 2, T:N], mk[:, :], ALU.subtract).then_inc(gdelta_ready, 1)
                        dve.wait_ge(gD_mm, it * 6 + v)
                        flat = TR[:, :, :, :].rearrange("p t c d -> p (t c d)")
                        if v < LEVELS - 1:
                            ve.tensor_tensor(flat, flat, side[1][:, :], ALU.subtract).then_inc(gTR_ready, 1)
                        else:
                            ve.tensor_tensor(flat[:, T:2 * T], flat[:, T:2 * T], side[1][:, T:2 * T], ALU.subtract).then_inc(gTR_ready, 1)
                        units(at + 2, at + LEVU)
                        at += LEVU
                    units(at, 45)
                    dve.wait_ge(gst_mm, it * 2 + 1)
                    dve.wait_ge(pstate_free, it + l * BT + BT + 1)
                    ve.tensor_copy(pstate[:, 1, :], side[3][:, 0:P]).then_inc(gst_ready, 1)
                    units(45, 47)
                    dve.wait_ge(gks_mm, it + 1)
                    ve.scalar_tensor_tensor(out=rhs1[:, :], in0=side[1][:, 0:P], scalar=nebc[:, 1:2], in1=vt[:, 1, :],
                                            op0=ALU.mult, op1=ALU.add).then_inc(grhs_ready, 1)
                    units(47, 52)
                    dve.wait_ge(gst_mm, it * 2 + 2)
                    ve.scalar_tensor_tensor(out=pstate[:, 1, :], in0=pstate[:, 1, :], scalar=eb_row[:, T - 1:T], in1=side[3][:, 0:P],
                                            op0=ALU.mult, op1=ALU.add).then_inc(gst_ready, 1)
                    units(52, 55)
                    dve.wait_ge(gss_mm, it + 1)
                    ve.tensor_scalar(oms[:, :], side[2][:, 0:N], 1.0 / P, EPS, ALU.mult, ALU.add).then_inc(go_step, 1)
                    dve.wait_ge(go_step, it * 4 + 1)
                    ve.reciprocal(orc[:, :], oms[:, :]).then_inc(go_step, 1)
                    units(55, 58)
                    dve.wait_ge(gors_ready, it + 1)
                    ve.scalar_tensor_tensor(out=orc[:, :], in0=osb[:, :], scalar=col(par, Q_GNG + l), in1=oms[:, :],
                                            op0=ALU.mult, op1=ALU.mult).then_inc(go_step, 1)
                    dve.wait_ge(go_step, it * 4 + 3)
                    ve.tensor_tensor(y32[:, 0, :], orc[:, :], gates[:, bass.ds(h, 1), :].rearrange("p a n -> p (a n)"),
                                     ALU.mult).then_inc(go_step, 1)
                    units(58, 59)
                    dve.wait_ge(gyhi, it + 1)
                    ve.tensor_tensor(y_lo[:, bass.ds(h + YT[GDN], 1), :], y32[:, 0, :],
                                     y_hi[:, bass.ds(h + YT[GDN], 1), :].bitcast(F32), ALU.subtract).then_inc(y_ready[GDN], 1)
                    units(59, 60)

                def merged_lo(k):
                    dve.wait_ge(mhi_ready, l * KT + k + 1)
                    ve.tensor_tensor(tile_of(y_lo, k), tile_of(wide, k), tile_of(y_hi, k).bitcast(F32),
                                     ALU.subtract).then_inc(mlo_ready, 1)

                def gdn_merge_turn(h, last):
                    ub, split = splitter(l, OFF_X, h, XTURN)
                    bank_now[0] = dve.snap(l * BANK_USES + BK_X + h * 2)
                    for i in range(4):
                        split(MB * i + 3 + (i > 0), MB * i + 8)
                        merge_block(ub, i, i % 2, False, h * 4 + i)
                        if i < 3:
                            split(MB * i + 8, MB * i + 9)
                        if not last:
                            merged_lo(dve.snap(h * 4 + i))

                with dve.Fori(0, BT - 1) as h:
                    gdn_merge_turn(h, False)
                gdn_merge_turn(BT - 1, True)
                for k in range(KT - 4, KT):
                    merged_lo(k)

                ve.memset(sq_sum[:, :], 0.0).then_inc(sum_cleared, 1)
                dve.wait_ge(sum_cleared, l + 1)
                settled(dve)
                with dve.Fori(0, BT) as h:
                    ub, split = splitter(l, OFF_O, h, TURN)
                    for i in range(4):
                        split(4 * i + 3, 4 * i + 7)
                        k = dve.snap(h * 4 + i)
                        dve.wait_ge(unit_used, ub + RING + UB * (i + 1))
                        ve.tensor_tensor(tile_of(x, k), tile_of(x, k), acc[i][:, 0:N], ALU.add).then_inc(bank_free[i], 1)
                        dve.wait_ge(bank_free[i], l * BANK_USES + BK_O + h + 1 + BF)
                        dve.sem_inc(x_updated, 1)
                        x_added(i % 2, l * KT + h * 4 + i)
                        x_lo(l + 1, k, (l + 1) * KT + h * 4 + i)
            mean_square(DEPTH)
            dve.wait_ge(rstd_ready, DEPTH + 1)
            for k in range(KT):
                last = normed(DEPTH, k)
                if k % 4 == 3:
                    last.then_inc(h_ready, 1)

        @block.tensor
        def _(pe):
            mm = nc.tensor.matmul

            def product(bank, slot, hi, lo, k0, first, last):
                for k in range(UK):
                    w_h, w_l = whi[:, slot, k * P:(k + 1) * P], wlo[:, slot, k * P:(k + 1) * P]
                    mm(acc[bank][:, 0:N], w_h, hi[:, k0 + k, :], start=first and k == 0, stop=False)
                    mm(acc[bank][:, 0:N], w_h, lo[:, k0 + k, :], start=False, stop=False)
                    op = mm(acc[bank][:, 0:N], w_l, hi[:, k0 + k, :], start=False, stop=last and k == UK - 1)
                op.then_inc(unit_used, 1)

            def streamer(l, off, i, per):
                ub = pe.snap(l * UNITS + off + i * per)

                def unit(j, bank, hi, lo, k0, first, last):
                    pe.wait_ge(lo_ready, ub + j + 1 + RING)
                    product(bank, j % RING, hi, lo, k0, first, last)
                return unit

            def norm_sum(n):
                pe.wait_ge(con_loaded, 16)
                pe.wait_ge(first_sum, 4)
                pe.wait_ge(sq_added, n * KT + 2)
                mm(side[0][:, 0:N], ones, sq_sum[:, :], start=True, stop=True).then_inc(norm_mm, 1)

            with pe.Fori(0, DEPTH) as l:
                def blocks(unit, a, b, free, hi=act_hi, lo=act_lo, ready=None):
                    for j in range(a, b):
                        i = j // UB
                        if j % UB == 0:
                            pe.wait_ge(bank_free[i % 4], free + BF)
                        if ready and j < UB:
                            pe.wait_ge(ready, l * KT + UK * (j + 1))
                        unit(j, i % 4, hi, lo, UK * (j % UB), j % UB == 0, j % UB == UB - 1)

                unit = streamer(l, OFF_G, 0, TURN)
                free = pe.snap(l * BANK_USES + BK_G)
                blocks(unit, 0, UB, free, ready=xlo_ready)
                norm_sum(l)
                blocks(unit, UB, TURN, free)
                with pe.Fori(0, BT - 1) as r:
                    h = pe.snap(r + 1)
                    unit = streamer(l, OFF_G, h, TURN)
                    blocks(unit, 0, TURN, pe.snap(l * BANK_USES + BK_G + h))

                pe.wait_ge(par_loaded, 16)
                pe.wait_ge(h_ready, l * 2 * BT + 2 * BT)
                for c in range(3):
                    lo, n = c * P, (P, P, NS)[c]
                    for k in range(KT):
                        op = mm(side[1][0:n, 2 * BT * c:2 * BT * (c + 1)], wide[:, k, lo:lo + n],
                                par[:, bass.ds(Q_WAB + (l * KT + k) * 2 * BT, 2 * BT)], start=k == 0, stop=k == KT - 1)
                    op.then_inc(ab_mm, 1)

                pe.wait_ge(hlo_ready, l * 2 * BT + 2 * BT)
                settled(pe)
                with pe.Fori(0, BT) as h:
                    it = pe.snap(l * BT + h)
                    unit = streamer(l, OFF_R, h, TURN)
                    free = pe.snap(l * BANK_USES + BK_R + h)
                    blocks(unit, 0, UB, free, y_hi, y_lo)
                    pe.wait_ge(gsq_ready, it + 1)
                    for a in range(2):
                        op = mm(side[2 + a][:, 0:N], ones, sq2[:, a, :], start=True, stop=True)
                    op.then_inc(gn_mm, 1)
                    blocks(unit, UB, TURN, free, y_hi, y_lo)

                pe.wait_ge(ahi_copied, l * BT + BT)
                pe.wait_ge(alo_copied, l * BT + BT)
                settled(pe)
                with pe.Fori(0, BT) as h:
                    it = pe.snap(l * BT + h)
                    unit = streamer(l, OFF_S, h, TURN)
                    free = pe.snap(l * BANK_USES + BK_S + h)
                    blocks(unit, 0, 3, free)
                    pe.wait_ge(head_copied, it + 1)
                    pe.wait_ge(ab_evac, l + 1)
                    mm(side[0][:, 0:T], head[:, 1, 0:P], head[:, 0, 0:T], start=True, stop=True)
                    mm(side[0][:, T:T + P], head[:, 1, P:T], head[:, 0, P:T], start=True, stop=True).then_inc(rsc_mm, 1)
                    for a in range(2):
                        for c in range(CH):
                            op = nc.tensor.transpose(side[1][:, (2 * a + c) * P:(2 * a + c + 1) * P],
                                                     head[:, 1 + a, c * P:(c + 1) * P], ident)
                    op.then_inc(rtr_mm, 1)
                    blocks(unit, 3, 5, free)
                    pe.wait_ge(scores_ready, it + 1)
                    pe.wait_ge(kdvt_ready, it + l * BT + 1)
                    mm(side[2][:, 0:T], vt[:, 0, :], scores[:, 0:T], start=True, stop=False)
                    mm(side[2][:, P:T], vt[:, 1, :], scores[:, T:T + P], start=False, stop=True).then_inc(ro_mm, 1)
                    for c in range(CH):
                        op = mm(side[3][:, 0:P], kd[:, c, :], vt[:, c, :], start=c == 0, stop=c == CH - 1)
                    op.then_inc(rst_mm, 1)
                    blocks(unit, 5, 7, free)
                    for b in range(NS):
                        op = mm(side[b // 4][:, (b % 4) * P:(b % 4 + 1) * P], head[:, 2, T + b:T + b + 1].to_broadcast([P, P]),
                                ident, start=True, stop=True)
                    op.then_inc(rvb_mm, 1)
                    blocks(unit, 7, 11, free)
                    pe.wait_ge(rstate_new, it * NS + NS)
                    for b in range(NS):
                        op = mm(side[2][:, T + b:T + b + 1], state[:, b, :], head[:, 0, T + b:T + b + 1], start=True, stop=True)
                    op.then_inc(ros_mm, 1)
                    blocks(unit, 11, 14, free)
                    pe.wait_ge(ro_copied, it + 1)
                    mm(side[3][:, 0:N], ones, osq[:, :], start=True, stop=True).then_inc(rss_mm, 1)
                    blocks(unit, 14, TURN, free)

                def mix(g):
                    pe.wait_ge(psum_step, l * BT + g + 2)
                    mm(side[0][:, 0:N], plw[:, g, :], pdiff[:, :], start=True, stop=True).then_inc(pmix_mm, 1)

                pe.wait_ge(plw_loaded, l * 16 + 16)
                for g in range(BT):
                    unit = streamer(l, OFF_P, g, PTURN)
                    for j in range(PTURN):
                        bank = 2 * (g % 2) + j // UB
                        if j % UB == 0:
                            pe.wait_ge(bank_free[bank], l * BANK_USES + BK_P + g // 2 + BF)
                        unit(j, bank, act_hi, act_lo, UK * (j % UB), j % UB == 0, j % UB == UB - 1)
                        if j == 0 and g:
                            mix(g - 1)
                pe.wait_ge(ab_step, l * 15 + 15)
                mm(side[1][:, 0:CH * BT], tri, g_col[:, 0:CH * BT], start=True, stop=True).then_inc(bcol_mm, 1)
                mix(BT - 1)

                def merge_units(unit, a, b, branches, free):
                    for j in range(a, b):
                        i, u = j // MB, j % MB
                        p = i % 2
                        if u == 0:
                            pe.wait_ge(bank_free[2 * p], free + i // 2 + BF)
                        if u < UB:
                            unit(j, 2 * p, act_hi, act_lo, UK * u, u == 0, u == UB - 1)
                        else:
                            pe.wait_ge(bank_free[2 * p + 1], free + i // 2 + BF)
                            unit(j, 2 * p + 1, y_hi, y_lo, YT[branches[i % len(branches)]], True, True)

                with pe.Fori(0, BT) as h:
                    it = pe.snap(l * BT + h)
                    unit = streamer(l, OFF_M, h, MTURN)
                    free = pe.snap(l * BANK_USES + BK_M + h * 6)

                    def units(a, b):
                        merge_units(unit, a, b, (SCV, POOL, RET), free)

                    units(0, 3)
                    for n in (SCV, POOL, RET):
                        pe.wait_ge(y_ready[n], l * BT + BT)
                    pe.wait_ge(gbc_ready, it + 1)
                    pe.wait_ge(gv_ready, it + 1)
                    for c in range(CH):
                        mm(side[2][:, c * P:(c + 1) * P], g_bc[:, c, :], tri, start=True, stop=True)
                    mm(side[2][:, T:N], g_bc[0:NS, 2, :], con[0:NS, C_ID:C_ID + NS], start=True, stop=True)
                    mm(side[2][:, N:BR], beta_bc[0:NS, :], con[0:NS, C_ID:C_ID + NS], start=True, stop=True).then_inc(grow_mm, 1)
                    for c in range(CH):
                        op = nc.tensor.transpose(side[3][:, c * P:(c + 1) * P], head[:, 2, c * P:(c + 1) * P], ident)
                    op.then_inc(gvt_mm, 1)
                    units(3, KQ0)
                    for a in range(2):
                        for c in range(CH):
                            op = mm(side[0][:, (2 * a + c) * P:(2 * a + c + 1) * P], head[:, 1, c * P:(c + 1) * P],
                                    head[:, 1 - a, c * P:(c + 1) * P], start=True, stop=True)
                    op.then_inc(gkq_mm, 1)
                    for c in range(CH):
                        op = nc.tensor.transpose(side[1][:, c * P:(c + 1) * P], head[:, 1, c * P:(c + 1) * P], ident)
                    op.then_inc(gkt_mm, 1)
                    units(KQ0, KQ0 + 3)
                    pe.wait_ge(gR_ready, it * 2 + 2)
                    for c in range(CH):
                        op = nc.tensor.transpose(side[0][:, c * P:(c + 1) * P], TR[:, 1, c, :], ident)
                    op.then_inc(gT_mm, 1)
                    units(KQ0 + 3, LEV0)
                    at = LEV0
                    for v in range(1, LEVELS):
                        if v == 1:
                            pe.wait_ge(gT_ready, it + 1)
                        else:
                            pe.wait_ge(gTR_ready, it * 6 + v - 1)
                        pe.wait_ge(gem_ready, it * 6 + v)
                        for c in range(CH):
                            op = mm(side[0][:, c * P:(c + 1) * P], Em[:, v % 2, c * P:(c + 1) * P], TR[:, 0, c, :], start=True, stop=True)
                        op.then_inc(gX_mm, 1)
                        if v == 1:
                            pe.wait_ge(state_loaded, (it + l * BT) * 16 + 16 * BT + 16)
                            pe.wait_ge(gqd_ready, it + 1)
                            pe.wait_ge(kdvt_ready, it + (l + 1) * BT + 1)
                            for b in range(NS):
                                op = mm(side[3][:, 2 * b:2 * b + 2], state[:, b, :], head[:, 0:2, T + b], start=True, stop=True)
                            op.then_inc(gdl_mm, 1)
                        if v == 2:
                            pe.wait_ge(grow_ready, it * 2 + 2)
                            pe.wait_ge(gdelta_ready, it + 1)
                            mm(side[2][:, 0:NS], ones, qkb[:, :], start=True, stop=True).then_inc(gos_mm, 1)
                        if v in (2, 4):
                            if v == 4:
                                pe.wait_ge(gstate_new, it * NS + 4)
                            for b in range(2 * v - 4, 2 * v):
                                op = mm(side[3][:, (b % 4) * P:(b % 4 + 1) * P], sdelta[:, b:b + 1].to_broadcast([P, P]),
                                        ident, start=True, stop=True)
                            op.then_inc(gdl_mm, 1)
                        units(at, at + 2)
                        pe.wait_ge(gX_ready, it * 6 + v)
                        if v < LEVELS - 1:
                            for c in range(CH):
                                mm(side[1][:, c * P:(c + 1) * P], TR[:, 1, c, :], Xs[:, c, :], start=True, stop=True)
                        for c in range(CH):
                            op = mm(side[1][:, T + c * P:T + (c + 1) * P], Xs[:, c, :], TR[:, 1, c, :], start=True, stop=True)
                        op.then_inc(gD_mm, 1)
                        units(at + 2, at + LEVU)
                        at += LEVU
                    pe.wait_ge(gTR_ready, it * 6 + 6)
                    pe.wait_ge(gos_copied, it + 1)
                    mm(side[2][:, 0:P], TR[:, 1, 0, :], vt[:, 0, :], start=True, stop=True).then_inc(gsol_mm, 1)
                    units(at, 43)
                    pe.wait_ge(gvn_ready, it * 2 + 1)
                    pe.wait_ge(gkd_ready, it + 1)
                    pe.wait_ge(gstate_new, it * NS + NS)
                    mm(side[3][:, 0:P], kd[:, 0, :], vn[:, 0, :], start=True, stop=True).then_inc(gst_mm, 1)
                    units(43, 46)
                    pe.wait_ge(gst_ready, it * 2 + 1)
                    mm(side[1][:, 0:P], head[:, 1, P:T], pstate[:, 1, :], start=True, stop=True).then_inc(gks_mm, 1)
                    pe.wait_ge(gattn_ready, it + 1)
                    mm(side[0][:, 0:P], vn[:, 0, :], attn[:, 0, :], start=True, stop=True)
                    units(46, 48)
                    pe.wait_ge(grhs_ready, it + 1)
                    mm(side[2][:, 0:P], TR[:, 1, 1, :], rhs1[:, :], start=True, stop=True).then_inc(gsol_mm, 1)
                    units(48, 51)
                    mm(side[0][:, P:T], pstate[:, 1, :], qd[:, :], start=True, stop=False)
                    pe.wait_ge(gvn_ready, it * 2 + 2)
                    mm(side[0][:, P:T], vn[:, 1, :], attn[:, 1, :], start=False, stop=True).then_inc(go_mm, 1)
                    mm(side[3][:, 0:P], kd[:, 1, :], vn[:, 1, :], start=True, stop=True).then_inc(gst_mm, 1)
                    units(51, 54)
                    pe.wait_ge(go_copied, it * 2 + 2)
                    mm(side[2][:, 0:N], ones, osq[:, :], start=True, stop=True).then_inc(gss_mm, 1)
                    units(54, 60)

                with pe.Fori(0, BT) as h:
                    unit = streamer(l, OFF_X, h, XTURN)
                    free = pe.snap(l * BANK_USES + BK_X + h * 2)
                    merge_units(unit, 0, 4, (GDN,), free)
                    pe.wait_ge(y_ready[GDN], l * BT + BT)
                    merge_units(unit, 4, XTURN, (GDN,), free)

                with pe.Fori(0, BT) as h:
                    unit = streamer(l, OFF_O, h, TURN)
                    blocks(unit, 0, TURN, pe.snap(l * BANK_USES + BK_O + h), y_hi, y_lo, ready=mlo_ready)
            norm_sum(DEPTH)


def shape_constants():
    f = np.float32
    con = np.zeros((P, C_END), f)
    i = np.arange(P)
    con[:, C_ID:C_ID + P] = np.eye(P)
    con[:, C_ONE:C_ONE + P] = 1.0
    upper = i[None, :] >= i[:, None]
    con[:, C_TRI:C_TRI + P] = upper
    con[:, C_NEG:C_NEG + P] = np.where(upper, 0.0, -1e30)
    con[:, C_STRICT:C_STRICT + P] = i[None, :] > i[:, None]
    for v in range(LEVELS):
        blk = i >> v
        con[:, C_LEV + v * P:C_LEV + (v + 1) * P] = (blk[:, None] % 2 == 0) & (blk[None, :] == blk[:, None] + 1)
    lg = np.log(1.0 - 2.0 ** (-5.0 - np.arange(BT)))
    t = np.arange(T)
    lag = t[None, :] - i[:, None]
    for h in range(BT):
        con[:, C_DM + h * T:C_DM + (h + 1) * T] = np.where(lag >= 0, np.exp(lg[h] * np.maximum(lag, 0)), 0.0)
        for c in range(CH):
            con[:, C_GDEC + h * CH + c] = np.exp(lg[h] * (T - 1 - (c * P + i)))
        con[:, C_GAM + h] = np.exp(lg[h])
    half = P // 2
    inv = (f(10000.0) ** (-np.arange(half, dtype=f) / f(half))).astype(f)
    pos = np.concatenate([np.arange(T), np.full(NS, PAST)]).astype(f)
    ang = (pos[None, :] * inv[:, None]).astype(f).astype(np.float64)
    cos, sin = np.cos(ang), np.sin(ang)
    con[:, C_COS:C_COS + N] = np.concatenate([cos, cos])
    con[:, C_SIN:C_SIN + N] = np.concatenate([sin, -sin])
    for g, w in enumerate(WINDOWS):
        con[:, C_CORR + 16 * g:C_CORR + 16 * (g + 1)] = w / np.minimum(np.arange(16) + 1, w)
    return con


def kernel(x_prompt, x_sample, state_ret, state_gdn, state_gdn_conv, state_sconv, state_pool,
           norm_g, w_in, gdn_conv_w, gdn_a_log, gdn_dt_bias, gdn_norm_g,
           sconv_w, pool_w, pool_scale, w_branch, w_out, final_norm_g):
    import concourse.bacc as bacc
    from concourse.bass_utils import run_bass_kernel_spmd

    A = np.asarray
    w_in, w_branch, w_out = A(w_in), A(w_branch), A(w_out)

    SPLIT = [BW] * 4 + [3 * BW, BW, BT, BT] + [BW] * 6 + [4 * D_MODEL]
    start = np.concatenate([[0], np.cumsum(SPLIT)])
    (RQ, RK, RV, RG, GQKV, GG, GA, GB, SB, SCC, SH, SG, PU, PG, ML) = start[:-1]

    def units(w, c0):
        k = w.shape[1] // P
        b = w[:, :, c0:c0 + P].reshape(DEPTH, k // UK, UK, P, P)
        return b.transpose(0, 1, 3, 2, 4).reshape(DEPTH, k // UK, P, UC)

    parts = []
    for h in range(BT):
        parts += [units(w_in, c + h * P) for c in (GQKV, GQKV + BW, GQKV + 2 * BW, GG)]
    for h in range(BT):
        parts += [units(w_in, c + h * P) for c in (RQ, RK, RV, RG)]
    for h in range(BT):
        parts += [units(w_in, c + h * P) for c in (SCC, SH, SB, SG)]
    for h in range(BT):
        parts += [units(w_in, c + h * P) for c in (PU, PG)]
    for m in range(KT):
        for n in (SCV, POOL, RET):
            parts += [units(w_in, ML + n * D_MODEL + m * P), units(w_branch[:, n], m * P)]
    for m in range(KT):
        parts += [units(w_in, ML + GDN * D_MODEL + m * P), units(w_branch[:, GDN], m * P)]
    for m in range(KT):
        parts += [units(w_out, m * P)]
    w_stream = np.concatenate(parts, axis=1).reshape(-1, P, UC)
    assert w_stream.shape[0] == DEPTH * UNITS
    w_stream = np.concatenate([w_stream, w_stream[:RING]])

    xt = np.concatenate([A(x_prompt)[0], A(x_sample)[:, 0]], axis=0)
    x_in = np.ascontiguousarray(xt.T.reshape(KT, P, N).transpose(1, 0, 2))

    def chan(a, tiles):
        a = A(a)
        a = a.reshape(a.shape[:-1] + (tiles, P))
        return np.moveaxis(a, -1, 0)

    def flat(a):
        return np.ascontiguousarray(a).reshape(P, -1)

    def rows(a):
        return flat(np.broadcast_to(A(a)[None, :, None, :], (P, DEPTH, 3, BT)))

    wab = w_in[:, :, GA:GA + 2 * BT].reshape(DEPTH, KT, P, 2 * BT).transpose(2, 0, 1, 3)
    gh = chan(state_gdn_conv, 3 * BT).reshape(P, DEPTH, NS, GW - 1, 3, BT).transpose(0, 1, 5, 4, 2, 3)
    sh = chan(state_sconv, BT).transpose(0, 1, 4, 2, 3)
    pool_in = np.ascontiguousarray(chan(state_pool, BT).transpose(1, 0, 4, 2, 3)).reshape(DEPTH, P, BT * NS * PH)
    params = np.concatenate([
        flat(chan(norm_g, KT)), flat(chan(final_norm_g, KT)),
        flat(chan(gdn_conv_w, 3 * BT).reshape(P, DEPTH, GW, 3, BT).transpose(0, 1, 4, 3, 2)),
        flat(chan(sconv_w, BT).transpose(0, 1, 3, 2)),
        flat(A(gdn_norm_g).T), flat(chan(pool_scale, BT)),
        rows(gdn_dt_bias), rows(gdn_a_log), flat(wab), flat(gh), flat(sh)], axis=1)
    assert params.shape[1] == Q_END
    w_pool = np.ascontiguousarray(A(pool_w).transpose(0, 2, 1, 3))

    arrays = {"w_stream": w_stream, "w_pool": w_pool, "pool_in": pool_in, "x_in": x_in, "params": params, "consts": shape_constants(),
              "ret_in": A(state_ret), "gdn_in": A(state_gdn)}
    st = (DEPTH, NS, BT, P, P)
    outs = {"y_out": (P, KT * N), "hist_out": (DEPTH, P, H_END), "p_ret": (DEPTH, 1, BT, P, P), "p_gdn": (DEPTH, 1, BT, P, P),
            "s_ret": st, "s_gdn": st}
    nc = bacc.Bacc("TRN2", target_bir_lowering=False, num_devices=1)
    args = [nc.dram_tensor(k, a.shape, F32, kind="ExternalInput").ap() for k, a in arrays.items()]
    args += [nc.dram_tensor(k, s, F32, kind="ExternalOutput").ap() for k, s in outs.items()]
    trunk(nc, *args)
    r = run_bass_kernel_spmd(nc, [arrays], core_ids=[0]).results[0]

    y = r["y_out"].reshape(P, KT, N).transpose(2, 1, 0).reshape(N, D_MODEL)
    y_prompt, y_sample = y[None, :T], y[T:, None]
    ho = r["hist_out"]

    def hists(lo, hi, shape, perm, k, ch):
        a = ho[:, :, lo:hi].reshape((DEPTH, P) + shape).transpose(perm)
        a = a.reshape(DEPTH, NS + 1, k, ch)
        return np.ascontiguousarray(a[:, :1]), np.ascontiguousarray(a[:, 1:])

    pgc, sgc = hists(H_G, H_S, (BT, 3, NS + 1, GW - 1), (0, 4, 5, 3, 2, 1), GW - 1, 3 * BW)
    psc, ssc = hists(H_S, H_P, (BT, NS + 1, SW - 1), (0, 3, 4, 2, 1), SW - 1, BW)
    ppl, spl = hists(H_P, H_END, (BT, NS + 1, PH), (0, 3, 4, 2, 1), PH, BW)
    return (np.ascontiguousarray(y_prompt), np.ascontiguousarray(y_sample), r["p_ret"], r["p_gdn"], pgc, psc, ppl,
            r["s_ret"], r["s_gdn"], sgc, ssc, spl)
```
